# Optimizing a Trainium2 kernel written in Bass

```python
import math
import jax, jax.numpy as jnp
from jax import lax
import numpy as np

D_MODEL = 1024
BATCH = 1
SEQ = 512
DEPTH = 1

CHUNK = 64
MIX_WIDTH = D_MODEL
LRU_WIDTH = MIX_WIDTH // 2
ATT_WIDTH = MIX_WIDTH - LRU_WIDTH
LRU_BLOCKS = 8
LRU_BLOCK_W = LRU_WIDTH // LRU_BLOCKS
CONV_W = 4
LRU_C = 8.0
ATT_HEADS = 8
ATT_HEAD_DIM = ATT_WIDTH // ATT_HEADS
Q_BLOCK = 128
D_FF = -(-8 * D_MODEL // (3 * 256)) * 256
IN_COLS = 2 * LRU_WIDTH + 3 * ATT_WIDTH
EPS = 1e-6


def rms_norm(x, g):
    xf = x.astype(jnp.float32)
    xf = xf * lax.rsqrt(jnp.mean(xf * xf, axis=-1, keepdims=True) + EPS)
    return xf.astype(x.dtype) * g

def causal_depthwise_conv(x, w, b):
    s = x.shape[1]
    xp = jnp.pad(x, ((0, 0), (CONV_W - 1, 0), (0, 0)))
    y = b
    for i in range(CONV_W):
        y = y + xp[:, i:i + s, :] * w[i]
    return y

def block_diag_linear(x, w, b):
    bsz, s, _ = x.shape
    xb = x.reshape(bsz, s, LRU_BLOCKS, LRU_BLOCK_W)
    y = jnp.einsum('bsnc,ncd->bsnd', xb, w) + b
    return y.reshape(bsz, s, LRU_WIDTH)

def rg_lru(x, w_rg, b_rg, w_ig, b_ig, lam):
    r = jax.nn.sigmoid(block_diag_linear(x, w_rg, b_rg).astype(jnp.float32))
    i = jax.nn.sigmoid(block_diag_linear(x, w_ig, b_ig).astype(jnp.float32))
    log_a = -LRU_C * r * jax.nn.softplus(-lam.astype(jnp.float32))
    a = jnp.exp(log_a)
    mult = jnp.sqrt(-jnp.expm1(2.0 * log_a))
    bterm = mult * (i * x.astype(jnp.float32))

    def combine(e1, e2):
        a1, b1 = e1
        a2, b2 = e2
        return a1 * a2, a2 * b1 + b2

    _, h = lax.associative_scan(combine, (a, bterm), axis=1)
    return h.astype(x.dtype)

def stick_breaking_attention(q, k, v):
    bsz, s, h, dh = q.shape
    nb = s // Q_BLOCK
    scale = 1.0 / math.sqrt(dh)
    qb = q.reshape(bsz, nb, Q_BLOCK, h, dh).transpose(1, 0, 2, 3, 4)
    key_pos = jnp.arange(s)

    def one_block(args):
        q_blk, blk = args
        z = jnp.einsum('bqhd,bkhd->bhqk', q_blk, k).astype(jnp.float32) * scale
        t = blk * Q_BLOCK + jnp.arange(Q_BLOCK)
        mask = key_pos[None, :] < t[:, None]
        log_beta = jax.nn.log_sigmoid(z)
        log_1mb = jnp.where(mask, jax.nn.log_sigmoid(-z), 0.0)
        suffix = lax.cumsum(log_1mb, axis=3, reverse=True) - log_1mb
        att = jnp.where(mask, jnp.exp(log_beta + suffix), 0.0)
        return jnp.einsum('bhqk,bkhd->bqhd', att.astype(v.dtype), v)

    out = lax.map(one_block, (qb, jnp.arange(nb)))
    return out.transpose(1, 0, 2, 3, 4).reshape(bsz, s, h, dh)

def first_inputs(seed: int = 0) -> dict:
    key = jax.random.key(seed)
    ks = jax.random.split(key, 20)
    f32 = jnp.float32
    nrm = lambda k, shp, sc: jax.random.normal(k, shp, f32) * sc
    gain = lambda k, shp: 1.0 + 0.05 * jax.random.normal(k, shp, f32)
    x = jax.random.normal(ks[0], (BATCH, SEQ, D_MODEL), f32)
    u = jax.random.uniform(ks[9], (DEPTH, LRU_WIDTH), f32, 0.9, 0.999)
    a0 = u ** (1.0 / LRU_C)
    lru_lambda = jnp.log(a0) - jnp.log1p(-a0)
    return {
        "x": x,
        "norm_mix": gain(ks[1], (DEPTH, D_MODEL)),
        "w_in": nrm(ks[2], (DEPTH, D_MODEL, IN_COLS), D_MODEL ** -0.5),
        "conv_w": nrm(ks[3], (DEPTH, CONV_W, LRU_WIDTH), CONV_W ** -0.5),
        "conv_b": nrm(ks[4], (DEPTH, LRU_WIDTH), 0.01),
        "w_rg": nrm(ks[5], (DEPTH, LRU_BLOCKS, LRU_BLOCK_W, LRU_BLOCK_W), LRU_BLOCK_W ** -0.5),
        "b_rg": nrm(ks[6], (DEPTH, LRU_BLOCKS, LRU_BLOCK_W), 0.01),
        "w_ig": nrm(ks[7], (DEPTH, LRU_BLOCKS, LRU_BLOCK_W, LRU_BLOCK_W), LRU_BLOCK_W ** -0.5),
        "b_ig": nrm(ks[8], (DEPTH, LRU_BLOCKS, LRU_BLOCK_W), 0.01),
        "lru_lambda": lru_lambda,
        "norm_lru_out": gain(ks[10], (DEPTH, LRU_WIDTH)),
        "norm_att_out": gain(ks[11], (DEPTH, ATT_WIDTH)),
        "w_out": nrm(ks[12], (DEPTH, MIX_WIDTH, D_MODEL), MIX_WIDTH ** -0.5),
        "norm_ffn": gain(ks[13], (DEPTH, D_MODEL)),
        "w_ffn_in": nrm(ks[14], (DEPTH, D_MODEL, 2 * D_FF), D_MODEL ** -0.5),
        "w_ffn_out": nrm(ks[15], (DEPTH, D_FF, D_MODEL), D_FF ** -0.5),
        "norm_final": gain(ks[16], (D_MODEL,)),
    }

def first_block(x, norm_mix, w_in, conv_w, conv_b, w_rg, b_rg, w_ig, b_ig, lru_lambda,
              norm_lru_out, norm_att_out, w_out, norm_ffn, w_ffn_in, w_ffn_out, norm_final):
    bsz, s, _ = x.shape
    for l in range(DEPTH):
        h = rms_norm(x, norm_mix[l])
        u = jnp.einsum('bsd,de->bse', h, w_in[l])
        o = 0
        lru_x = u[..., o:o + LRU_WIDTH]; o += LRU_WIDTH
        lru_g = u[..., o:o + LRU_WIDTH]; o += LRU_WIDTH
        q = u[..., o:o + ATT_WIDTH].reshape(bsz, s, ATT_HEADS, ATT_HEAD_DIM); o += ATT_WIDTH
        k = u[..., o:o + ATT_WIDTH].reshape(bsz, s, ATT_HEADS, ATT_HEAD_DIM); o += ATT_WIDTH
        v = u[..., o:o + ATT_WIDTH].reshape(bsz, s, ATT_HEADS, ATT_HEAD_DIM)

        xc = causal_depthwise_conv(lru_x, conv_w[l], conv_b[l])
        hl = rg_lru(xc, w_rg[l], b_rg[l], w_ig[l], b_ig[l], lru_lambda[l])
        y_lru = jax.nn.gelu(lru_g) * hl

        y_att = stick_breaking_attention(q, k, v).reshape(bsz, s, ATT_WIDTH)

        y = jnp.concatenate([rms_norm(y_lru, norm_lru_out[l]),
                             rms_norm(y_att, norm_att_out[l])], axis=-1)
        x = x + jnp.einsum('bse,ed->bsd', y, w_out[l])

        h2 = rms_norm(x, norm_ffn[l])
        gu = jnp.einsum('bsd,df->bsf', h2, w_ffn_in[l])
        x = x + jnp.einsum('bsf,fd->bsd', jax.nn.silu(gu[..., :D_FF]) * gu[..., D_FF:], w_ffn_out[l])
    return rms_norm(x, norm_final)


CONV_WIDTH = D_MODEL // 2
CONV_GROUPS = 8
CONV_K = 3
ATTN_HEADS = 8
HEAD_DIM = 64
ATTN_WIDTH = ATTN_HEADS * HEAD_DIM
N_BRANCH = 2
FFN_HIDDEN = 2816
FFN_CONV_K = 3
IN_SPLITS = (CONV_WIDTH, CONV_WIDTH, CONV_WIDTH, ATTN_WIDTH, ATTN_WIDTH, ATTN_WIDTH, ATTN_HEADS, N_BRANCH * D_MODEL)
IN_WIDTH = sum(IN_SPLITS)


def rms_norm_2(x, g):
    x32 = x.astype(jnp.float32)
    y = x32 * lax.rsqrt(jnp.mean(x32 * x32, axis=-1, keepdims=True) + EPS)
    return y.astype(x.dtype) * g

def causal_dwconv(x, w):
    K = w.shape[0]
    S = x.shape[1]
    xp = jnp.pad(x, ((0, 0), (K - 1, 0), (0, 0)))
    y = xp[:, K - 1:K - 1 + S, :] * w[K - 1]
    for k in range(K - 1):
        y = y + xp[:, k:k + S, :] * w[k]
    return y

def forgetting_attention(q, k, v, log_f):
    B, S, H, hd = q.shape
    scale = 1.0 / np.sqrt(hd).astype(np.float32)
    F = jnp.cumsum(log_f, axis=1).transpose(0, 2, 1)
    qh = q.transpose(0, 2, 1, 3).astype(jnp.float32) * scale
    kh = k.transpose(0, 2, 1, 3).astype(jnp.float32)
    vh = v.transpose(0, 2, 1, 3).astype(jnp.float32)
    nb = S // Q_BLOCK
    q_blocks = qh.reshape(B, H, nb, Q_BLOCK, hd).transpose(2, 0, 1, 3, 4)
    fq_blocks = F.reshape(B, H, nb, Q_BLOCK).transpose(2, 0, 1, 3)
    k_pos = jnp.arange(S)

    def one_block(args):
        q_blk, fq_blk, i = args
        q_pos = i * Q_BLOCK + jnp.arange(Q_BLOCK)
        s = jnp.einsum('bhqd,bhkd->bhqk', q_blk, kh) + fq_blk[..., None] - F[:, :, None, :]
        s = jnp.where(k_pos[None, :] <= q_pos[:, None], s, -jnp.inf)
        p = jax.nn.softmax(s, axis=-1)
        return jnp.einsum('bhqk,bhkd->bhqd', p, vh)

    o = lax.map(one_block, (q_blocks, fq_blocks, jnp.arange(nb)))
    o = o.transpose(1, 0, 3, 2, 4).reshape(B, S, H * hd)
    return o.astype(q.dtype)

def second_inputs(seed: int = 0) -> dict:
    key = jax.random.key(seed)
    ks = jax.random.split(key, 16)
    f32 = jnp.float32
    L = DEPTH
    x = jax.random.normal(ks[0], (BATCH, SEQ, D_MODEL), f32)
    norm_mix_g = 1.0 + 0.02 * jax.random.normal(ks[1], (L, D_MODEL), f32)
    w_in = jax.random.normal(ks[2], (L, D_MODEL, IN_WIDTH), f32) * D_MODEL ** -0.5
    b_f = 2.0 + 0.5 * jax.random.normal(ks[3], (L, ATTN_HEADS), f32)
    b_gate = 0.02 * jax.random.normal(ks[4], (L, N_BRANCH * D_MODEL), f32)
    conv_mix_w = jax.random.normal(ks[5], (L, CONV_K, CONV_WIDTH), f32) * CONV_K ** -0.5
    w_out_conv = jax.random.normal(ks[6], (L, CONV_WIDTH, D_MODEL), f32) * CONV_WIDTH ** -0.5
    w_out_attn = jax.random.normal(ks[7], (L, ATTN_WIDTH, D_MODEL), f32) * ATTN_WIDTH ** -0.5
    w_o = jax.random.normal(ks[8], (L, D_MODEL, D_MODEL), f32) * D_MODEL ** -0.5
    norm_ffn_g = 1.0 + 0.02 * jax.random.normal(ks[9], (L, D_MODEL), f32)
    w_up = jax.random.normal(ks[10], (L, D_MODEL, 2 * FFN_HIDDEN), f32) * D_MODEL ** -0.5
    conv_ffn_w = jax.random.normal(ks[11], (L, FFN_CONV_K, 2 * FFN_HIDDEN), f32) * FFN_CONV_K ** -0.5
    w_down = jax.random.normal(ks[12], (L, FFN_HIDDEN, D_MODEL), f32) * FFN_HIDDEN ** -0.5
    norm_f_g = 1.0 + 0.02 * jax.random.normal(ks[13], (D_MODEL,), f32)
    return {"x": x, "norm_mix_g": norm_mix_g, "w_in": w_in, "b_f": b_f, "b_gate": b_gate,
            "conv_mix_w": conv_mix_w, "w_out_conv": w_out_conv, "w_out_attn": w_out_attn,
            "w_o": w_o, "norm_ffn_g": norm_ffn_g, "w_up": w_up, "conv_ffn_w": conv_ffn_w,
            "w_down": w_down, "norm_f_g": norm_f_g}

def second_block(x, norm_mix_g, w_in, b_f, b_gate, conv_mix_w, w_out_conv, w_out_attn,
              w_o, norm_ffn_g, w_up, conv_ffn_w, w_down, norm_f_g):
    B, S, _ = x.shape
    split_idx = list(np.cumsum(IN_SPLITS)[:-1])
    for l in range(DEPTH):
        h = rms_norm_2(x, norm_mix_g[l])
        proj = h @ w_in[l]
        cb, cc, cin, q, k, v, f_logit, g_logit = jnp.split(proj, split_idx, axis=-1)
        u = causal_dwconv(cc * cin, conv_mix_w[l])
        y_conv = (cb * u) @ w_out_conv[l]
        log_f = jax.nn.log_sigmoid((f_logit + b_f[l]).astype(jnp.float32))
        o = forgetting_attention(q.reshape(B, S, ATTN_HEADS, HEAD_DIM),
                                 k.reshape(B, S, ATTN_HEADS, HEAD_DIM),
                                 v.reshape(B, S, ATTN_HEADS, HEAD_DIM), log_f)
        y_attn = o @ w_out_attn[l]
        gates = jax.nn.sigmoid(g_logit + b_gate[l])
        g_conv, g_attn = jnp.split(gates, 2, axis=-1)
        x = x + (g_conv * y_conv + g_attn * y_attn) @ w_o[l]
        h = rms_norm_2(x, norm_ffn_g[l])
        up = causal_dwconv(h @ w_up[l], conv_ffn_w[l])
        a, b = jnp.split(up, 2, axis=-1)
        x = x + (jax.nn.silu(a) * b) @ w_down[l]
    return rms_norm_2(x, norm_f_g)


def setup_inputs(seed=0):
    out = dict(first_inputs(seed))
    for name, value in second_inputs(seed + 1).items():
        if name != "x":
            out[name + "_2"] = value
    return out


def reference(
    x, norm_mix, w_in, conv_w, conv_b, w_rg, b_rg, w_ig, b_ig, lru_lambda, norm_lru_out,
    norm_att_out, w_out, norm_ffn, w_ffn_in, w_ffn_out, norm_final, norm_mix_g_2, w_in_2, b_f_2,
    b_gate_2, conv_mix_w_2, w_out_conv_2, w_out_attn_2, w_o_2, norm_ffn_g_2, w_up_2,
    conv_ffn_w_2, w_down_2, norm_f_g_2,
):
    x = first_block(
        x, norm_mix, w_in, conv_w, conv_b, w_rg, b_rg, w_ig, b_ig, lru_lambda, norm_lru_out,
        norm_att_out, w_out, norm_ffn, w_ffn_in, w_ffn_out, norm_final,
    )
    return second_block(
        x, norm_mix_g_2, w_in_2, b_f_2, b_gate_2, conv_mix_w_2, w_out_conv_2, w_out_attn_2,
        w_o_2, norm_ffn_g_2, w_up_2, conv_ffn_w_2, w_down_2, norm_f_g_2,
    )


_drawn_inputs = setup_inputs


def setup_inputs(seed=0):
    import zlib

    import numpy as np

    out = dict(_drawn_inputs(seed))
    spreads = {}
    factors = {'b_rg': 8.0,
     'b_ig': 8.0,
     'norm_mix_g_2': 2.859,
     'b_gate_2': 8.0,
     'norm_ffn_g_2': 12.461,
     'norm_f_g_2': 7.704}
    for name, (base, spread) in spreads.items():
        noise = np.random.default_rng([zlib.crc32(name.encode()), seed]).standard_normal(out[name].shape)
        drawn = base * np.exp(spread * noise) if base else spread * noise
        out[name] = __import__('jax').numpy.asarray(drawn.astype(out[name].dtype))
    for name, factor in factors.items():
        out[name] = (out[name] * factor).astype(out[name].dtype)
    return out
```

```python
from contextlib import ExitStack

import concourse.bass as bass
from concourse import mybir

F32 = mybir.dt.float32
F32R = mybir.dt.float32r
BF16 = mybir.dt.bfloat16
ALU = mybir.AluOpType
ACT = mybir.ActivationFunctionType

P = 128
TOKENS = 512
D = 1024
DC = D // P
TB = TOKENS // P
WIDTH = 512
WC = WIDTH // P
HEADS = 8
HD = WIDTH // HEADS
FF = 2816
FC = FF // P
EPS = 1e-6
SCALE = HD ** -0.5
MASKED = -1e30
SLAB = 2048
COLS_A = SLAB // DC
ROWS_B = SLAB // WIDTH
FFN_STEPS = FF // COLS_A
CAUSAL = sum(TOKENS - P * b for b in range(TB))
KEY_AT = [0, 512, 1024, 896]
QUERY_AT = [896, 1024, 512, 0]

ROWS = [("norm_mix", 8), ("norm_ffn", 8), ("norm_final", 8), ("conv_w", 16), ("conv_b", 4), ("b_rg", 4),
        ("b_ig", 4), ("lru_lambda", 4), ("norm_lru_out", 4), ("norm_att_out", 4), ("norm_mix_g_2", 8),
        ("b_gate_2", 16), ("conv_mix_w_2", 12), ("norm_ffn_g_2", 8)]
AT = {}
_n = 0
for _name, _rows in ROWS:
    AT[_name] = _n
    _n += _rows
NROWS = _n
TAP_ROWS = 3 * 2 * FC // 2

SLABS = []


def _add(w, kind, k0, nk, c0, nc_):
    SLABS.append((w, kind, k0, nk, c0, nc_))
    return len(SLABS) - 1


def _cols_a(w, c0, n):
    first = len(SLABS)
    for j in range(n // COLS_A):
        _add(w, "A", 0, DC, c0 + j * COLS_A, COLS_A)
    return first


def _down(w):
    first = len(SLABS)
    for half in range(2):
        for k0 in range(0, FC, ROWS_B):
            _add(w, "B", k0, min(ROWS_B, FC - k0), half * WIDTH, WIDTH)
    return first


S_LX = _cols_a("w_in", 0, WIDTH)
S_LG = _cols_a("w_in", WIDTH, WIDTH)
S_Q = _cols_a("w_in", 2 * WIDTH, WIDTH)
S_K = _cols_a("w_in", 3 * WIDTH, WIDTH)
S_V = _add("w_in", "B", 0, ROWS_B, 4 * WIDTH, WIDTH)
_add("w_in", "B", ROWS_B, ROWS_B, 4 * WIDTH, WIDTH)
S_OUT_LRU = _add("w_out", "B", 0, WC, 0, WIDTH)
_add("w_out", "B", 0, WC, WIDTH, WIDTH)
S_OUT_ATT = _add("w_out", "B", WC, WC, 0, WIDTH)
_add("w_out", "B", WC, WC, WIDTH, WIDTH)
S_FFN = len(SLABS)
for _i in range(FFN_STEPS):
    _add("w_ffn_in", "A", 0, DC, _i * COLS_A, COLS_A)
    _add("w_ffn_in", "A", 0, DC, FF + _i * COLS_A, COLS_A)
S_DOWN = _down("w_ffn_out")
F_AT = 6 * WIDTH
S_F2 = _add("w_in_2", "A", 0, DC, F_AT, P)
S_K2 = _cols_a("w_in_2", 4 * WIDTH, WIDTH)
S_Q2 = _cols_a("w_in_2", 3 * WIDTH, WIDTH)
S_V2 = _add("w_in_2", "B", 0, ROWS_B, 5 * WIDTH, WIDTH)
_add("w_in_2", "B", ROWS_B, ROWS_B, 5 * WIDTH, WIDTH)
S_CC = _cols_a("w_in_2", WIDTH, WIDTH)
S_CIN = _cols_a("w_in_2", 2 * WIDTH, WIDTH)
S_CB = _cols_a("w_in_2", 0, WIDTH)
S_GC = _cols_a("w_in_2", F_AT + HEADS, D)
S_GA = _cols_a("w_in_2", F_AT + HEADS + D, D)
S_OC2 = _add("w_out_conv_2", "B", 0, WC, 0, WIDTH)
_add("w_out_conv_2", "B", 0, WC, WIDTH, WIDTH)
S_OA2 = _add("w_out_attn_2", "B", 0, WC, 0, WIDTH)
_add("w_out_attn_2", "B", 0, WC, WIDTH, WIDTH)
S_O2 = _cols_a("w_o_2", 0, D)
S_UP = len(SLABS)
for _i in range(FFN_STEPS):
    _add("w_up_2", "A", 0, DC, _i * COLS_A, COLS_A)
    _add("w_up_2", "A", 0, DC, FF + _i * COLS_A, COLS_A)
S_DOWN2 = _down("w_down_2")
N_SLABS = len(SLABS)
DOWN_SLABS = (N_SLABS - S_DOWN2) // 2

GROUP = []
_g = -1
for _s in range(N_SLABS):
    _inner = (_s in (S_V + 1, S_V2 + 1)
              or any(f <= _s < f + 2 * DOWN_SLABS and (_s - f) % DOWN_SLABS for f in (S_DOWN, S_DOWN2)))
    _g += not _inner
    GROUP.append(_g)


def src_count(q):
    return q + 1 - (WC if q >= C_M2 else 0)


def bank_of(g):
    return 4 * ((g + (g > GROUP[S_V])) % 2)


def _shares_count(g):
    s = GROUP.index(g)
    return s < S_LG or S_Q <= s < S_FFN or S_F2 <= s < S_GC or S_OC2 <= s < S_O2


EVICTED_BEFORE = [sum(_shares_count(k) for k in range(g)) for g in range(GROUP[-1] + 1)]


def freed(g):
    s = GROUP.index(g)
    if S_LG <= s < S_Q:
        return "lg_ready", 2 * (s - S_LG + 1)
    if S_FFN <= s < S_DOWN:
        return ("ffn_up" if (s - S_FFN) % 2 else "ffn_gate"), 2 * ((s - S_FFN) // 2 + 1)
    if S_DOWN <= s < S_F2:
        return "x_sum", WC * ((s - S_DOWN) // DOWN_SLABS + 1)
    if S_GC <= s < S_OC2:
        return "gate_pre", 2 * (s - S_GC + 1)
    if S_O2 <= s < S_UP:
        return "src_ready", src_count(C_UP2 + 2 * (s - S_O2) + 1)
    if S_UP <= s < S_DOWN2:
        return "up_scaled", 2 * (s - S_UP + 1)
    if S_DOWN2 <= s:
        return "xn_sum", TB * ((s - S_DOWN2) // DOWN_SLABS + 1)
    return "evicted", 1 + EVICTED_BEFORE[g]


C_MIX, C_LRU, C_ATT, C_FFN, C_MIX2, C_Z2, C_O2, C_M2, C_UP2 = 0, 8, 12, 16, 24, 32, 36, 40, 48
N_MIX, N_LRU, N_ATT, N_FFN, N_FINAL, N_MIX2, N_FFN2 = range(7)
SQ_FIRST = [0, 8, 12, 16, 24, 25, 40]
SQ_DONE = [8, 12, 16, 24, 39, 40, 48]
RSTD_AT = [0, 1, 2, 0, 1, 2, 0]


def two_blocks(nc, t, out):
    with ExitStack() as ctx:
        def sb(name, shape, dt=F32, where=None):
            return (where or ctx).enter_context(nc.sbuf_tensor(name, shape, dt))

        def sem(name):
            return ctx.enter_context(nc.semaphore(name))

        xT = sb("xT", [P, DC, TOKENS])
        raw = sb("raw", [P, 2, SLAB])
        w_hi = sb("w_hi", [P, 2, SLAB], F32R)
        w_lo = sb("w_lo", [P, 2, SLAB], F32R)
        tmp = sb("tmp", [P, 6, TOKENS])
        rstd = sb("rstd", [P, 3, TOKENS])
        acc = tmp[:, 2:4]
        sq = tmp[:, 4:6]
        par = sb("par", [P, NROWS + 2 * TAP_ROWS])
        ident = sb("ident", [P, P])
        ones = sb("ones", [P, P])
        neg_ones = sb("neg_ones", [P, P])
        neg_tri = sb("neg_tri", [P, P])
        ident_bf = sb("ident_bf", [P, P], BF16)
        mask_kq = sb("mask_kq", [P, P], BF16)
        mask_qk = sb("mask_qk", [P, P], BF16)
        small = sb("small", [P, 64])
        decay = sb("decay", [P, WC])
        f_bias = sb("f_bias", [HEADS, 1])
        eps = sb("eps", [P, 1])
        act_scope = ExitStack()
        act_hi = sb("act_hi", [P, DC, TOKENS], F32R, act_scope)
        act_lo = sb("act_lo", [P, DC, TOKENS], F32R, act_scope)
        scope = ExitStack()
        hid_hi = sb("hid_hi", [P, FC, TOKENS], F32R, scope)
        hid_lo = sb("hid_lo", [P, FC, TOKENS], F32R, scope)
        scope.close()
        lx = sb("lx", [P, WC, TOKENS], F32, scope)
        lg = sb("lg", [P, WC, TOKENS], F32, scope)
        xc = sb("xc", [P, WC, TOKENS], F32, scope)
        inner = ExitStack()
        xin = sb("xin", [P, TB, D], F32, inner)
        rows = sb("rows", [NROWS, P], F32, inner)
        tap_rows = sb("tap_rows", [TAP_ROWS, 2, P], F32, inner)
        inner.close()
        qT = sb("qT", [P, WC, TOKENS], F32, scope)
        kT = sb("kT", [P, WC, TOKENS], F32, scope)
        v = sb("v", [P, TB, WIDTH], F32, scope)
        yatt = sb("yatt", [P, WC, TOKENS], F32, scope)
        gate_bd = sb("gate_bd", [P, 2, WC, P], F32, inner)
        gate_t = sb("gate_t", [P, 2, TOKENS], F32, inner)
        gate_i = sb("gate_i", [P, 2, TOKENS], F32, inner)
        root_t = sb("root_t", [P, 2, TOKENS], F32, inner)
        lru_rc = sb("lru_rc", [P, TOKENS], F32, inner)
        lru_a = sb("lru_a", [P, TOKENS], F32, inner)
        inner.close()
        stick = sb("stick", [P, 2, CAUSAL], F32, inner)
        soft = sb("soft", [P, 2, CAUSAL], F32, inner)
        att = sb("att", [P, 2, CAUSAL], F32, inner)
        inner.close()
        scope.close()
        q2 = sb("q2", [P, WC, TOKENS], F32, scope)
        k2 = sb("k2", [P, WC, TOKENS], F32, scope)
        v2 = sb("v2", [P, TB, WIDTH], F32, scope)
        gc = sb("gc", [P, DC, TOKENS], F32, scope)
        fsum = sb("fsum", [HEADS, 2, TOKENS], F32, inner)
        inner.close()
        ga = sb("ga", [P, DC, TOKENS], F32, scope)
        neg_f = sb("neg_f", [P, HEADS, TOKENS], F32, scope)
        conv_p = sb("conv_p", [P, WC, TOKENS], F32, inner)
        conv_u = sb("conv_u", [P, WC, TOKENS], F32, inner)
        inner.close()
        probs = sb("probs", [P, 2, CAUSAL], F32, inner)
        probs_T = tmp[:, 0:5].rearrange("p a n -> p (a n)").rearrange("p (a n) -> p a n", a=2)
        inner.close()
        scope.close()
        act_scope.close()
        xnat = sb("xnat", [P, TB, D], F32, act_scope)
        gain_out = sb("gain_out", [P, D], F32, act_scope)
        junk = sb("junk", [P, WIDTH], F32, act_scope)
        act_scope.close()

        psum = ctx.enter_context(nc.psum_tensor("psum", [P, 8, TOKENS], F32))

        x_in, row_in = sem("x_in"), sem("row_in")
        bd_in, gain_in = sem("bd_in"), sem("gain_in")
        raw_in = [sem("raw_in0"), sem("raw_in1")]
        const_set = sem("const_set")
        bd_zeroed = sem("bd_zeroed")
        const_bf = sem("const_bf")
        par_done, par_ready = sem("par_done"), sem("par_ready")
        decay_ready = sem("decay_ready")
        lam_abs, lam_exp = sem("lam_abs"), sem("lam_exp")
        x_turned = sem("x_turned")
        w_hi_ready, w_lo_ready = sem("w_hi_ready"), sem("w_lo_ready")
        slab_done = sem("slab_done")
        evicted = sem("evicted")
        src_ready = sem("src_ready")
        act_hi_ready, act_lo_ready = sem("act_hi_ready"), sem("act_lo_ready")
        sq_ready, sq_summed = sem("sq_ready"), sem("sq_summed")
        ssq_done, root_done, rstd_ready = sem("ssq_done"), sem("root_done"), sem("rstd_ready")
        dve_step = sem("dve_step")
        act_step = sem("act_step")
        conv_done, gates_done, gate_read, tanh_done = sem("conv_done"), sem("gates_done"), sem("gate_read"), sem("tanh_done")
        root_t_done, gelu_done = sem("root_t_done"), sem("gelu_done")
        row_turned, both_ready = sem("row_turned"), sem("both_ready")
        lg_ready = sem("lg_ready")
        z_done, z_abs, z_log, soft_ready = sem("z_done"), sem("z_abs"), sem("z_log"), sem("soft_ready")
        suffix_done, att_ready, pv_done = sem("suffix_done"), sem("att_ready"), sem("pv_done")
        ffn_gate, ffn_silu = sem("ffn_gate"), sem("ffn_silu")
        ffn_up, ffn_hidden, x_sum = sem("ffn_up"), sem("ffn_hidden"), sem("x_sum")
        hid_hi_ready, hid_lo_ready = sem("hid_hi_ready"), sem("hid_lo_ready")
        xn_sq, xn_mean = sem("xn_sq"), sem("xn_mean")
        f_abs = sem("f_abs")
        ms2_ready, f_pre, f_exp, f_ln, f_sum = sem("ms2_ready"), sem("f_pre"), sem("f_exp"), sem("f_ln"), sem("f_sum")
        negf_done, negf_ready = sem("negf_done"), sem("negf_ready")
        gate_pre, gate_ready = sem("gate_pre"), sem("gate_ready")
        s_done, s_max, p_exp, p_ready2, pt_done, pt_ready = sem("s_done"), sem("s_max"), sem("p_exp"), sem("p_ready2"), sem("pt_done"), sem("pt_ready")
        pv2_done = sem("pv2_done")
        up_scaled, up_tap, up_conv, up_silu = sem("up_scaled"), sem("up_tap"), sem("up_conv"), sem("up_silu")
        up_mid = sem("up_mid")
        up_hidden, up_hi, up_lo = sem("up_hidden"), sem("up_hi"), sem("up_lo")
        xn_turned, xn_ready, xn_sum, xn_root, xn_out, stored = sem("xn_turned"), sem("xn_ready"), sem("xn_sum"), sem("xn_root"), sem("xn_out"), sem("stored")

        def col(name, j, n=P):
            return par[0:n, AT[name] + j:AT[name] + j + 1]

        def tap_col(tap, chunk):
            return par[:, bass.ds(chunk + (NROWS + tap * 2 * FC), 1)]

        block = ctx.enter_context(nc.Block())

        @block.sync
        def _(sp):
            def load_slab(s, i=None):
                w, kind, k0, nk, c0, nc_ = SLABS[s]
                step = 0 if i is None else i
                if s >= 2 or i is not None:
                    sp.wait_ge(w_lo_ready, s - 1 + 2 * step)
                src = t[w][0].rearrange("(k p) n -> p k n", p=P)[:, k0:k0 + nk]
                src = src[:, :, c0:c0 + nc_] if i is None else src[:, :, bass.ds(i * COLS_A + c0, COLS_A)]
                dst = raw[:, s % 2, 0:nk * nc_].rearrange("p (k n) -> p k n", k=nk)
                sp.dma_start(dst, src).then_inc(raw_in[s % 2], 16)

            r = 0
            for name, n in ROWS:
                src = t[name]
                flat = src[0] if len(src.shape) > 1 else src
                if len(flat.shape) == 2:
                    flat = flat.rearrange("a b -> (a b)")
                sp.dma_start(rows[r:r + n, :], flat.rearrange("(r c) -> r c", c=P)).then_inc(row_in, 16)
                r += n
            x_rows = t["x"][0].rearrange("(b p) d -> p b d", p=P)
            for b in range(TB):
                sp.dma_start(xin[:, b, :], x_rows[:, b, :]).then_inc(x_in, 16)
            taps = t["conv_ffn_w_2"][0].rearrange("k (c p) -> (k c) p", p=P)
            for j in range(2):
                sp.dma_start(tap_rows[:, j, :], taps[j * TAP_ROWS:(j + 1) * TAP_ROWS, :]).then_inc(row_in, 16)
            load_slab(0)
            load_slab(1)
            sp.dma_start(f_bias[:, :], t["b_f_2"].rearrange("a h -> h a")).then_inc(row_in, 16)
            sp.wait_ge(bd_zeroed, 1)
            for g, name in enumerate(("w_rg", "w_ig")):
                for e in range(2):
                    src = t[name][0].rearrange("(c e) i o -> e i c o", e=2)
                    sp.dma_start(gate_bd[64 * e:64 * e + 64, g, :, 64 * e:64 * e + 64], src[e]).then_inc(bd_in, 16)
            for s in range(2, S_FFN):
                load_slab(s)
            with sp.Fori(0, FFN_STEPS) as i:
                load_slab(S_FFN, i)
                load_slab(S_FFN + 1, i)
            for s in range(S_DOWN, S_UP):
                load_slab(s)
            with sp.Fori(0, FFN_STEPS) as i:
                load_slab(S_UP, i)
                load_slab(S_UP + 1, i)
            sp.wait_ge(slab_done, S_DOWN2)
            sp.dma_start(gain_out[:, :], t["norm_f_g_2"].rearrange("(a d) -> a d", a=1).broadcast_to([P, D])).then_inc(gain_in, 16)
            for s in range(S_DOWN2, N_SLABS):
                load_slab(s)
            out_rows = out[0].rearrange("(b p) d -> p b d", p=P)
            for b in range(TB):
                sp.wait_ge(xn_out, b + 1)
                sp.dma_start(out_rows[:, b, :], xnat[:, b, :]).then_inc(stored, 16)
            sp.wait_ge(stored, 16 * TB)

        @block.gpsimd
        def _(pool):
            g = nc.gpsimd
            g.memset(ident[:], 0.0).then_inc(const_set, 1)
            g.memset(neg_tri[:], -1.0).then_inc(const_set, 1)
            g.memset(tmp[:, 0, 0:2 * P], MASKED).then_inc(const_set, 1)
            pool.wait_ge(const_set, 3)
            g.affine_select(out=ident[:], in_=ident[:], compare_op=ALU.not_equal, fill=1.0, base=0,
                            pattern=[[-1, P]], channel_multiplier=1).then_inc(const_set, 1)
            g.memset(ones[:], 1.0).then_inc(const_set, 1)
            g.memset(neg_ones[:], -1.0).then_inc(const_set, 1)
            g.memset(eps[:], EPS).then_inc(const_set, 1)
            g.memset(gate_bd[:], 0.0).then_inc(bd_zeroed, 1)
            g.affine_select(out=neg_tri[:], in_=neg_tri[:], compare_op=ALU.is_ge, fill=0.0, base=0,
                            pattern=[[-1, P]], channel_multiplier=1).then_inc(const_set, 1)
            g.affine_select(out=tmp[:, 0, 0:P], in_=tmp[:, 0, 0:P], compare_op=ALU.is_ge, fill=0.0, base=0,
                            pattern=[[-1, P]], channel_multiplier=1).then_inc(const_set, 1)
            g.affine_select(out=tmp[:, 0, P:2 * P], in_=tmp[:, 0, P:2 * P], compare_op=ALU.is_gt, fill=0.0, base=0,
                            pattern=[[1, P]], channel_multiplier=-1).then_inc(const_set, 1)
            pool.wait_ge(const_set, 10)
            g.tensor_copy(mask_kq[:], tmp[:, 0, 0:P]).then_inc(const_bf, 1)
            g.tensor_copy(mask_qk[:], tmp[:, 0, P:2 * P]).then_inc(const_bf, 1)
            g.tensor_copy(ident_bf[:], ident[:]).then_inc(const_bf, 1)
            n = 0
            for rs in ((N_MIX,), (N_LRU,), (N_ATT,), (N_FFN,), (N_FINAL, N_MIX2), (N_FFN2,)):
                for c in range(4 if rs[0] in (N_LRU, N_ATT) else DC):
                    for r in rs:
                        pool.wait_ge(sq_ready, n + 1)
                        if c == 0:
                            if r >= 2:
                                pool.wait_ge(ssq_done, r - 1)
                            ins = g.tensor_copy(acc[:, r % 2], sq[:, n % 2])
                        else:
                            pool.wait_ge(sq_summed, n)
                            ins = g.tensor_tensor(acc[:, r % 2], acc[:, r % 2], sq[:, n % 2], ALU.add)
                        ins.then_inc(sq_summed, 1)
                        n += 1

        @block.scalar
        def _(act):
            A = nc.scalar.activation
            state = {"sq": 0}

            def split_w(s, i=None, last=False):
                if s >= N_SLABS:
                    return
                step = 0 if i is None else i
                n = SLABS[s][3] * SLABS[s][5] if i is None else SLAB
                act.wait_ge(raw_in[s % 2], 16 * (s // 2 + 1 + step))
                if s >= 2:
                    act.wait_ge(slab_done, s - 1 + step * 2)
                A(w_hi[:, s % 2, 0:n], raw[:, s % 2, 0:n], ACT.Copy).then_inc(w_hi_ready, 1)

            def square(src, wait=None):
                n = state["sq"]
                if n >= 2:
                    act.wait_ge(sq_summed, n - 1)
                A(sq[:, n % 2], src, ACT.Square).then_inc(sq_ready, 1)
                state["sq"] += 1

            def split_act(q, chunk, src, gain, free=None):
                act.wait_ge(src_ready, src_count(q))
                if free is not None:
                    act.wait_ge(slab_done, free)
                A(act_hi[:, chunk], src, ACT.Copy, scale=gain).then_inc(act_hi_ready, 1)

            def root(r, src):
                act.wait_ge(ssq_done if r != N_MIX2 else ms2_ready, r + 1 if r != N_MIX2 else 1)
                if r == N_MIX2:
                    A(rstd[:, RSTD_AT[r]], src, ACT.Sqrt, bias=eps[:, 0:1]).then_inc(root_done, 1)
                else:
                    A(rstd[:, RSTD_AT[r]], src, ACT.Sqrt, bias=eps[:, 0:1], scale=1.0 / (WIDTH if r in (N_LRU, N_ATT) else D)).then_inc(root_done, 1)

            act.wait_ge(par_done, 1)
            A(par[:, 0:NROWS + 2 * TAP_ROWS], psum[:, 7, 0:NROWS + 2 * TAP_ROWS], ACT.Copy).then_inc(par_ready, 1)
            act.wait_ge(par_ready, 1)
            split_w(0)
            for c in range(DC):
                split_act(C_MIX + c, c, xT[:, c], col("norm_mix", c))
                square(xT[:, c])
                if c == 1:
                    split_w(1)
            A(small[:, 0:4], par[:, AT["lru_lambda"]:AT["lru_lambda"] + WC], ACT.Abs).then_inc(lam_abs, 1)
            act.wait_ge(lam_abs, 1)
            A(small[:, 4:8], small[:, 0:4], ACT.Exp, scale=-1.0).then_inc(lam_exp, 1)
            root(N_MIX, psum[:, bank_of(0) + 3])
            for s in range(0, S_OUT_LRU):
                split_w(s + 2)
                if s in (S_LG, S_LG + 1):
                    for c in range(2 * (s - S_LG), 2 * (s - S_LG) + 2):
                        act.wait_ge(lg_ready, c + 1)
                        A(lg[:, c], lg[:, c], ACT.Gelu_apprx_tanh).then_inc(gelu_done, 1)
                if 2 <= s < 2 + WC:
                    c = s - 2
                    b = bank_of(GROUP[s])
                    act.wait_ge(gates_done, c + 1)
                    if c >= 2:
                        act.wait_ge(src_ready, C_LRU + c - 1)
                    A(gate_t[:, c % 2], psum[:, b + 2], ACT.Sigmoid, bias=col("b_rg", c)).then_inc(act_step, 1)
                    A(gate_i[:, c % 2], psum[:, b + 3], ACT.Sigmoid, bias=col("b_ig", c)).then_inc(gate_read, 1)
                    act.wait_ge(act_step, c + 1)
                    if c == 0:
                        act.wait_ge(decay_ready, 1)
                    A(gate_t[:, c % 2], gate_t[:, c % 2], ACT.Tanh, scale=decay[:, c:c + 1]).then_inc(tanh_done, 1)
                    act.wait_ge(tanh_done, c + 1)
                    A(root_t[:, c % 2], gate_t[:, c % 2], ACT.Sqrt).then_inc(root_t_done, 1)
                if 4 <= s < 4 + WC:
                    act.wait_ge(src_ready, C_LRU + s - 3)
                    square(lx[:, s - 4])
            root(N_LRU, psum[:, 7])
            nc.scalar.preload_act_table_set("natural_log_exp_and_others")

            def log_part(h):
                z = stick[:, h % 2]
                act.wait_ge(z_done, h + 1)
                b = 3 * (h % 2)
                A(z, psum[:, b:b + 3].rearrange("p b n -> p (b n)")[:, 0:CAUSAL], ACT.Abs).then_inc(z_abs, 1)
                act.wait_ge(z_abs, h + 1)
                A(z, z, ACT.Exp, scale=-1.0).then_inc(act_step, 1)
                act.wait_ge(act_step, WC + h + 1)
                A(z, z, ACT.Ln, bias=1.0).then_inc(z_log, 1)

            def att_operand(c):
                act.wait_ge(src_ready, C_ATT + c + 1)
                square(yatt[:, c])
                split_act(C_ATT + c, WC + c, yatt[:, c], col("norm_att_out", c), S_V + 2)

            log_part(0)
            for h in range(HEADS):
                if h + 1 < HEADS:
                    log_part(h + 1)
                act.wait_ge(suffix_done, h + 1)
                if h >= 2:
                    act.wait_ge(pv_done, h - 1)
                b = 3 * (h % 2)
                A(att[:, h % 2], psum[:, b:b + 3].rearrange("p b n -> p (b n)")[:, 0:CAUSAL], ACT.Exp).then_inc(att_ready, 1)
                if h < WC:
                    split_act(C_LRU + h, h, lx[:, h], col("norm_lru_out", h), S_V + 2)
                if h >= 3 and h % 2:
                    att_operand((h - 3) // 2)
            att_operand(WC - 1)

            for s in range(S_OUT_LRU, S_FFN):
                split_w(s + 2)
                if s == S_OUT_LRU:
                    root(N_ATT, psum[:, 4])
                if s >= S_OUT_ATT:
                    for c in range(4 * (s - S_OUT_ATT), 4 * (s - S_OUT_ATT) + 4):
                        split_act(C_FFN + c, c, xT[:, c], col("norm_ffn", c), S_OUT_ATT if c < WC else S_FFN)
                        square(xT[:, c])
            root(N_FFN, psum[:, bank_of(GROUP[S_FFN]) + 3])
            nc.scalar.preload_act_table(ACT.Silu)
            with act.Fori(0, FFN_STEPS) as i:
                split_w(S_FFN + 2, i)
                for j in range(2):
                    act.wait_ge(ffn_gate, 2 * i + (j + 1))
                    A(tmp[:, 2 + j], tmp[:, j], ACT.Silu).then_inc(ffn_silu, 1)
                split_w(S_FFN + 3, i)
                for j in range(2):
                    act.wait_ge(ffn_hidden, 2 * i + (j + 1))
                    A(hid_hi[:, bass.ds(2 * i + j, 1)].rearrange("p a n -> p (a n)"), tmp[:, 4 + j], ACT.Copy).then_inc(hid_hi_ready, 1)
            for s in range(S_DOWN, S_F2):
                split_w(s + 2)
                half = (s - S_DOWN) // DOWN_SLABS
                if (s - S_DOWN) % DOWN_SLABS == DOWN_SLABS - 1:
                    for c in range(4 * half, 4 * half + 4):
                        act.wait_ge(x_sum, c + 1)
                        square(tmp[:, c % 2])
                        split_act(C_MIX2 + c, c, xT[:, c], col("norm_mix_g_2", c), S_DOWN)
                        square(xT[:, c])
            b = bank_of(GROUP[S_F2])
            root(N_FINAL, psum[:, b + 2])
            root(N_MIX2, rstd[:, RSTD_AT[N_MIX2]])
            n_gate = 0
            for s in range(S_F2, S_OA2):
                split_w(s + 2)
                if s == S_F2:
                    act.wait_ge(f_pre, 1)
                    nc.scalar.preload_act_table_set("natural_log_exp_and_others")
                    A(fsum[:, 1], fsum[:, 0], ACT.Abs).then_inc(f_abs, 1)
                    act.wait_ge(f_abs, 1)
                    A(fsum[:, 1], fsum[:, 1], ACT.Exp, scale=-1.0).then_inc(f_exp, 1)
                    act.wait_ge(f_exp, 1)
                    A(fsum[:, 1], fsum[:, 1], ACT.Ln, bias=1.0).then_inc(f_ln, 1)
                if S_CC <= s < S_CC + HEADS:
                    h = s - S_CC
                    act.wait_ge(negf_done, h + 1)
                    A(neg_f[:, h], psum[:, bank_of(GROUP[s]) + 3], ACT.Copy).then_inc(negf_ready, 1)
                if S_GC <= s < S_OC2:
                    for j in range(2):
                        m = n_gate % DC
                        dst = gc[:, m] if n_gate < DC else ga[:, m]
                        act.wait_ge(gate_pre, n_gate + 1)
                        A(dst, tmp[:, n_gate % 4], ACT.Sigmoid, bias=col("b_gate_2", n_gate)).then_inc(gate_ready, 1)
                        n_gate += 1
                if s == S_OC2 - 1:
                    for c in range(WC):
                        split_act(C_Z2 + c, c, conv_u[:, c], 1.0, S_OC2)

            def exps(h):
                for i in range(TB):
                    act.wait_ge(s_max, h + 1)
                    part = probs[:, h % 2, QUERY_AT[i]:QUERY_AT[i] + P * (i + 1)]
                    k = 4 * (h % 2) + i
                    A(part, part, ACT.Exp, bias=small[:, 24 + k:25 + k], accum_out=small[:, 32 + k:33 + k]).then_inc(p_exp, 1)

            exps(0)
            for h in range(HEADS):
                act.wait_ge(pt_done, h + 1)
                if h >= 2:
                    act.wait_ge(pv2_done, h - 1)
                b = 3 * (h % 2)
                A(probs_T[:, h % 2], psum[:, b:b + 3].rearrange("p b n -> p (b n)")[:, 0:CAUSAL], ACT.Copy).then_inc(pt_ready, 1)
                if h + 1 < HEADS:
                    exps(h + 1)
                if h >= 3 and h % 2:
                    c = (h - 3) // 2
                    act.wait_ge(pv2_done, 2 * c + 2)
                    A(act_hi[:, WC + c], psum[:, 6 + c % 2], ACT.Copy).then_inc(act_hi_ready, 1)
            act.wait_ge(pv2_done, HEADS)
            A(act_hi[:, DC - 1], psum[:, 7], ACT.Copy).then_inc(act_hi_ready, 1)
            for s in range(S_OA2, S_UP):
                split_w(s + 2)
                if s < S_O2:
                    for m in range(4 * (s - S_OA2), 4 * (s - S_OA2) + 4):
                        split_act(C_M2 + m, m, gc[:, m], 1.0, S_OA2 if m < WC else S_O2)
                else:
                    for c in range(2 * (s - S_O2), 2 * (s - S_O2) + 2):
                        act.wait_ge(src_ready, src_count(C_UP2 + c))
                        square(xT[:, c])
            for c in range(DC):
                split_act(C_UP2 + c, c, xT[:, c], col("norm_ffn_g_2", c), S_UP)
            root(N_FFN2, psum[:, bank_of(GROUP[S_UP]) + 3])
            nc.scalar.preload_act_table(ACT.Silu)
            with act.Fori(0, FFN_STEPS) as i:
                split_w(S_UP + 2, i)
                for j in range(2):
                    act.wait_ge(up_scaled, 4 * i + (j + 1))
                    A(tmp[:, 2 + j], tmp[:, j], ACT.Copy, scale=tap_col(2, 2 * i + j)).then_inc(up_tap, 1)
                for j in range(2):
                    act.wait_ge(up_conv, 4 * i + (j + 1))
                    A(tmp[:, 2 + j], tmp[:, 2 + j], ACT.Silu).then_inc(up_silu, 1)
                split_w(S_UP + 3, i)
                for j in range(2):
                    act.wait_ge(up_scaled, 4 * i + (j + 3))
                    A(tmp[:, j], tmp[:, 4 + j], ACT.Copy, scale=tap_col(2, 2 * i + (FC + j))).then_inc(up_tap, 1)
                for j in range(2):
                    act.wait_ge(up_hidden, 2 * i + (j + 1))
                    A(hid_hi[:, bass.ds(2 * i + j, 1)].rearrange("p a n -> p (a n)"), tmp[:, j], ACT.Copy).then_inc(hid_hi_ready, 1)
            for s in range(S_DOWN2, N_SLABS):
                split_w(s + 2)
                half = (s - S_DOWN2) // DOWN_SLABS
                if (s - S_DOWN2) % DOWN_SLABS == DOWN_SLABS - 1:
                    for b in range(TB):
                        n = TB * half + b
                        act.wait_ge(xn_sum, n + 1)
                        if n:
                            act.wait_ge(xn_sq, n)
                        A(junk[:, :], xnat[:, b, half * WIDTH:(half + 1) * WIDTH], ACT.Square,
                          accum_out=small[:, 8 + n:9 + n]).then_inc(xn_sq, 1)
            act.wait_ge(xn_mean, 1)
            A(small[:, 48:52], small[:, 48:52], ACT.Sqrt, bias=eps[:, 0:1], scale=1.0 / D).then_inc(xn_root, 1)

        @block.vector
        def _(dve):
            V = nc.vector
            steps = {"n": 0, "evicted": 0}

            def mark(ins):
                steps["n"] += 1
                ins.then_inc(dve_step, 1)

            def settle():
                if steps["n"]:
                    dve.wait_ge(dve_step, steps["n"])
                if steps["evicted"]:
                    dve.wait_ge(evicted, steps["evicted"])

            def free(ins):
                steps["evicted"] += 1
                ins.then_inc(evicted, 1)

            def split_w(s, i=None):
                if s >= N_SLABS:
                    return
                step = 0 if i is None else i
                n = SLABS[s][3] * SLABS[s][5] if i is None else SLAB
                dve.wait_ge(w_hi_ready, s + 1 + 2 * step)
                V.tensor_tensor(w_lo[:, s % 2, 0:n], raw[:, s % 2, 0:n], w_hi[:, s % 2, 0:n].bitcast(F32),
                                ALU.subtract).then_inc(w_lo_ready, 1)

            def split_act(q, chunk, src, gain=None):
                dve.wait_ge(act_hi_ready, q + 1)
                hi = act_hi[:, chunk].bitcast(F32)
                if gain is None:
                    ins = V.tensor_tensor(act_lo[:, chunk], src, hi, ALU.subtract)
                else:
                    ins = V.scalar_tensor_tensor(act_lo[:, chunk], src, gain, hi, ALU.mult, ALU.subtract)
                ins.then_inc(act_lo_ready, 1)

            def finished(s, i=None):
                dve.wait_ge(slab_done, s + 1 + (0 if i is None else 2 * i))

            def bank(s, m):
                return psum[:, bank_of(GROUP[s]) + m]

            def inverse(r):
                dve.wait_ge(root_done, r + 1)
                f = rstd[:, RSTD_AT[r]]
                V.reciprocal(f, f).then_inc(rstd_ready, 1)
                dve.wait_ge(rstd_ready, r + 1)

            def R(r):
                return rstd[:, RSTD_AT[r]]

            for c in range(DC):
                dve.wait_ge(x_turned, c + 1)
                V.tensor_copy(xT[:, c], psum[:, c]).then_inc(src_ready, 1)
                if c == 0:
                    split_w(0)
                    dve.wait_ge(par_ready, 1)
                else:
                    split_act(C_MIX + c - 1, c - 1, xT[:, c - 1], col("norm_mix", c - 1))
                if c == 3:
                    split_w(1)
            split_act(C_MIX + DC - 1, DC - 1, xT[:, DC - 1], col("norm_mix", DC - 1))
            lam = par[:, AT["lru_lambda"]:AT["lru_lambda"] + WC]
            dve.wait_ge(lam_exp, 1)
            mark(V.tensor_scalar(small[:, 8:12], small[:, 4:8], 2.0, None, ALU.add))
            settle()
            mark(V.reciprocal(small[:, 8:12], small[:, 8:12]))
            settle()
            mark(V.tensor_tensor(small[:, 12:16], small[:, 8:12], small[:, 4:8], ALU.mult))
            settle()
            mark(V.tensor_tensor(small[:, 16:20], small[:, 12:16], small[:, 12:16], ALU.mult))
            settle()
            mark(V.tensor_scalar(small[:, 20:24], small[:, 16:20], 1.0 / 19, None, ALU.mult))
            for k in range(17, 1, -2):
                settle()
                mark(V.scalar_tensor_tensor(small[:, 20:24], small[:, 20:24], 1.0 / k, small[:, 16:20], ALU.add, ALU.mult))
            settle()
            mark(V.scalar_tensor_tensor(small[:, 20:24], small[:, 20:24], 1.0, small[:, 12:16], ALU.add, ALU.mult))
            mark(V.tensor_scalar(small[:, 24:28], lam, 0.0, -4.0, ALU.min, ALU.mult))
            settle()
            V.scalar_tensor_tensor(decay[:, :], small[:, 20:24], 8.0, small[:, 24:28], ALU.mult, ALU.add).then_inc(decay_ready, 1)

            def conv(c):
                mark(V.tensor_scalar(xc[:, c], lx[:, c], col("conv_w", 3 * WC + c), col("conv_b", c), ALU.mult, ALU.add))
                for d in range(1, 4):
                    settle()
                    ins = V.scalar_tensor_tensor(xc[:, c, d:], lx[:, c, 0:TOKENS - d], col("conv_w", (3 - d) * WC + c),
                                                 xc[:, c, d:], ALU.mult, ALU.add)
                    if d < 3:
                        mark(ins)
                    else:
                        ins.then_inc(conv_done, 1)

            def lru(c):
                k = c % 2
                dve.wait_ge(tanh_done, c + 1)
                mark(V.tensor_scalar(lru_rc[:, :], gate_t[:, k], 1.0, None, ALU.add))
                mark(V.tensor_tensor(gate_i[:, k], gate_i[:, k], xc[:, c], ALU.mult))
                settle()
                mark(V.reciprocal(lru_rc[:, :], lru_rc[:, :]))
                settle()
                mark(V.tensor_scalar(lru_a[:, :], lru_rc[:, :], 2.0, -1.0, ALU.mult, ALU.add))
                dve.wait_ge(root_t_done, c + 1)
                mark(V.scalar_tensor_tensor(root_t[:, k], root_t[:, k], 2.0, lru_rc[:, :], ALU.mult, ALU.mult))
                settle()
                mark(V.tensor_tensor(root_t[:, k], root_t[:, k], gate_i[:, k], ALU.mult))
                settle()
                mark(V.tensor_tensor_scan(lru_rc[:, :], lru_a[:, :], root_t[:, k], 0.0, ALU.mult, ALU.add))
                settle()
                dve.wait_ge(gelu_done, c + 1)
                V.tensor_tensor(lx[:, c], lru_rc[:, :], lg[:, c], ALU.mult).then_inc(src_ready, 1)
                dve.wait_ge(src_ready, C_LRU + c + 1)


            inverse(N_MIX)
            for s in range(S_LX, S_V):
                finished(s)
                for j in range(2):
                    c = 2 * (s % 2) + j
                    if s < S_LG:
                        ins = V.tensor_tensor(lx[:, c], bank(s, j), R(N_MIX), ALU.mult)
                    elif s < S_Q:
                        ins = V.tensor_tensor(lg[:, c], bank(s, j), R(N_MIX), ALU.mult)
                        ins.then_inc(lg_ready, 1)
                    elif s < S_K:
                        ins = V.scalar_tensor_tensor(qT[:, c], bank(s, j), SCALE, R(N_MIX), ALU.mult, ALU.mult)
                    else:
                        ins = V.tensor_tensor(kT[:, c], bank(s, j), R(N_MIX), ALU.mult)
                if not S_LG <= s < S_Q:
                    free(ins)
                split_w(s + 2)
                if s < S_LG:
                    settle()
                    conv(2 * s)
                    conv(2 * s + 1)
                if 3 <= s < 3 + WC:
                    lru(s - 3)
            dve.wait_ge(row_turned, 1)
            mark(V.tensor_copy(small[:, 32:32 + TB], psum[:, 7, 0:TB]))
            settle()
            for s in (S_V, S_V + 1):
                finished(s)
                if s > S_V:
                    for b in range(TB):
                        ins = V.tensor_scalar(v[:, b], bank(s, b), small[:, 32 + b:33 + b], None, ALU.mult)
                    free(ins)
                split_w(s + 2)

            def head_columns(h):
                b = 3 * (h % 2)
                return psum[:, b:b + 3].rearrange("p b n -> p (b n)")[:, 0:CAUSAL]

            def log_part(h):
                dve.wait_ge(z_log, h + 1)
                if h >= 2:
                    dve.wait_ge(suffix_done, h - 1)
                V.scalar_tensor_tensor(soft[:, h % 2], head_columns(h), 0.0, stick[:, h % 2],
                                       ALU.max, ALU.add).then_inc(soft_ready, 1)

            def att_out(c):
                dve.wait_ge(pv_done, 2 * c + 2)
                V.tensor_copy(yatt[:, c], psum[:, 6 + c % 2]).then_inc(src_ready, 1)

            log_part(0)
            for h in range(HEADS):
                if h + 1 < HEADS:
                    log_part(h + 1)
                if h == 0:
                    inverse(N_LRU)
                if h >= 2 and h % 2 == 0:
                    att_out((h - 2) // 2)
                if h < WC:
                    split_act(C_LRU + h, h, lx[:, h], col("norm_lru_out", h))
                if h >= 3 and h % 2:
                    c = (h - 3) // 2
                    split_act(C_ATT + c, WC + c, yatt[:, c], col("norm_att_out", c))
            att_out(WC - 1)
            split_act(C_ATT + WC - 1, DC - 1, yatt[:, WC - 1], col("norm_att_out", WC - 1))
            for s in range(S_OUT_LRU, S_FFN):
                finished(s)
                if s == S_OUT_ATT:
                    inverse(N_ATT)
                r = N_LRU if s < S_OUT_ATT else N_ATT
                order = (1, 2, 3, 0) if s == S_OUT_LRU + 1 else (0, 1, 2, 3)
                for m in order:
                    c = 4 * (s % 2) + m
                    ins = V.tensor_tensor(tmp[:, m % 2], bank(s, m), R(r), ALU.mult)
                    free(ins) if m == order[-1] else mark(ins)
                    settle()
                    ins = V.tensor_tensor(xT[:, c], xT[:, c], tmp[:, m % 2], ALU.add)
                    if s >= S_OUT_ATT:
                        ins.then_inc(src_ready, 1)
                    else:
                        mark(ins)
                settle()
                split_w(s + 2)
                if s >= S_OUT_ATT:
                    for m in range(4):
                        c = 4 * (s % 2) + m
                        split_act(C_FFN + c, c, xT[:, c], col("norm_ffn", c))
            inverse(N_FFN)
            with dve.Fori(0, FFN_STEPS) as i:
                finished(S_FFN, i)
                for j in range(2):
                    V.tensor_tensor(tmp[:, j], bank(S_FFN, j), R(N_FFN), ALU.mult).then_inc(ffn_gate, 1)
                split_w(S_FFN + 2, i)
                finished(S_FFN + 1, i)
                for j in range(2):
                    V.tensor_tensor(tmp[:, 4 + j], bank(S_FFN + 1, j), R(N_FFN), ALU.mult).then_inc(ffn_up, 1)
                for j in range(2):
                    dve.wait_ge(ffn_up, 2 * i + (j + 1))
                    dve.wait_ge(ffn_silu, 2 * i + (j + 1))
                    V.tensor_tensor(tmp[:, 4 + j], tmp[:, 4 + j], tmp[:, 2 + j], ALU.mult).then_inc(ffn_hidden, 1)
                split_w(S_FFN + 3, i)
                for j in range(2):
                    dve.wait_ge(ffn_hidden, 2 * i + (j + 1))
                    dve.wait_ge(hid_hi_ready, 2 * i + (j + 1))
                    at = bass.ds(2 * i + j, 1)
                    V.tensor_tensor(hid_lo[:, at].rearrange("p a n -> p (a n)"), tmp[:, 4 + j],
                                    hid_hi[:, at].rearrange("p a n -> p (a n)").bitcast(F32),
                                    ALU.subtract).then_inc(hid_lo_ready, 1)
                dve.wait_ge(hid_lo_ready, 2 * i + 2)
            for s in range(S_DOWN, S_F2):
                finished(s)
                half = (s - S_DOWN) // DOWN_SLABS
                last = (s - S_DOWN) % DOWN_SLABS == DOWN_SLABS - 1
                if not last:
                    split_w(s + 2)
                    continue
                for m in range(4):
                    c = 4 * half + m
                    if c >= 2:
                        dve.wait_ge(sq_ready, SQ_FIRST[N_FINAL] + 2 * (c - 2) + 1)
                    V.tensor_tensor(tmp[:, c % 2], bank(s, m), xT[:, c], ALU.add).then_inc(x_sum, 1)
                    dve.wait_ge(x_sum, c + 1)
                    V.tensor_scalar(xT[:, c], tmp[:, c % 2], col("norm_final", c), None, ALU.mult).then_inc(src_ready, 1)
                    dve.wait_ge(src_ready, src_count(C_MIX2 + c))
                    if m == 1:
                        split_w(s + 2)
                    if m:
                        split_act(C_MIX2 + c - 1, c - 1, xT[:, c - 1], col("norm_mix_g_2", c - 1))
                split_act(C_MIX2 + c, c, xT[:, c], col("norm_mix_g_2", c))
            inverse(N_FINAL)
            dve.wait_ge(ssq_done, N_MIX2 + 1)
            v2_ = R(N_MIX2)
            mark(V.scalar_tensor_tensor(v2_, bank(S_F2, 3), 1.0 / D, R(N_FINAL), ALU.mult, ALU.mult))
            settle()
            V.tensor_tensor(v2_, v2_, R(N_FINAL), ALU.mult).then_inc(ms2_ready, 1)
            inverse(N_MIX2)
            both = rstd[:, 0]
            V.tensor_tensor(both, R(N_FINAL), R(N_MIX2), ALU.mult).then_inc(both_ready, 1)
            dve.wait_ge(both_ready, 1)
            n_gate = 0
            for s in range(S_F2, S_OA2):
                finished(s)
                c0 = (s - S_K2) % 2 * 2 if s < S_V2 else (s - S_CC) % 2 * 2
                if s == S_F2:
                    free(V.tensor_tensor(fsum[:, 0], psum[0:HEADS, bank_of(GROUP[s])], rstd[0:HEADS, 0], ALU.mult))
                    settle()
                    V.tensor_scalar(fsum[:, 0], fsum[:, 0], f_bias[:, 0:1], None, ALU.add).then_inc(f_pre, 1)
                elif s < S_V2:
                    for j in range(2):
                        if s < S_Q2:
                            ins = V.tensor_tensor(k2[:, c0 + j], bank(s, j), both, ALU.mult)
                        else:
                            ins = V.scalar_tensor_tensor(q2[:, c0 + j], bank(s, j), SCALE, both, ALU.mult, ALU.mult)
                    free(ins)
                elif s < S_CC:
                    if s > S_V2:
                        dve.wait_ge(row_turned, 2)
                        mark(V.tensor_copy(small[:, 52:52 + TB], psum[:, bank_of(GROUP[S_K2 + 1]) + 3, 0:TB]))
                        settle()
                        for b in range(TB):
                            ins = V.tensor_scalar(v2[:, b], bank(s, b), small[:, 52 + b:53 + b], None, ALU.mult)
                        free(ins)
                elif s < S_CIN:
                    for j in range(2):
                        ins = V.tensor_tensor(conv_p[:, c0 + j], bank(s, j), both, ALU.mult)
                    free(ins)
                elif s < S_GC:
                    for j in range(2):
                        ins = V.tensor_tensor(tmp[:, 4 + j], bank(s, j), both, ALU.mult)
                    free(ins)
                elif s < S_OC2:
                    for j in range(2):
                        if n_gate >= 4:
                            dve.wait_ge(gate_ready, n_gate - 3)
                        V.tensor_tensor(tmp[:, n_gate % 4], bank(s, j), both, ALU.mult).then_inc(gate_pre, 1)
                        n_gate += 1
                else:
                    dve.wait_ge(gate_ready, DC)
                    for m in range(4):
                        c = 4 * (s - S_OC2) + m
                        ins = V.tensor_tensor(gc[:, c], bank(s, m), gc[:, c], ALU.mult)
                    free(ins)
                split_w(s + 2)
                if s == S_F2:
                    dve.wait_ge(f_ln, 1)
                    mark(V.scalar_tensor_tensor(fsum[:, 1], fsum[:, 0], 0.0, fsum[:, 1], ALU.min, ALU.subtract))
                    mark(V.memset(tmp[0:HEADS, 5], 1.0))
                    settle()
                    V.tensor_tensor_scan(fsum[:, 0], tmp[0:HEADS, 5], fsum[:, 1], 0.0, ALU.mult, ALU.subtract).then_inc(f_sum, 1)
                if S_K2 <= s < S_K2 + 4:
                    for c in (2 * (s - S_K2), 2 * (s - S_K2) + 1):
                        dve.wait_ge(sq_ready, SQ_DONE[N_MIX2])
                        mark(V.tensor_tensor(xT[:, c], xT[:, c], R(N_FINAL), ALU.mult))
                if S_CIN <= s < S_CB:
                    settle()
                    for j in range(2):
                        c = c0 + j
                        mark(V.tensor_tensor(conv_p[:, c], conv_p[:, c], tmp[:, 4 + j], ALU.mult))
                    settle()
                    for j in range(2):
                        c = c0 + j
                        mark(V.tensor_scalar(conv_u[:, c], conv_p[:, c], col("conv_mix_w_2", 2 * WC + c), None, ALU.mult))
                    for d in range(1, 3):
                        settle()
                        for j in range(2):
                            c = c0 + j
                            mark(V.scalar_tensor_tensor(conv_u[:, c, d:], conv_p[:, c, 0:TOKENS - d],
                                                        col("conv_mix_w_2", (2 - d) * WC + c), conv_u[:, c, d:],
                                                        ALU.mult, ALU.add))
                if S_CB <= s < S_GC:
                    settle()
                    for j in range(2):
                        c = c0 + j
                        V.tensor_tensor(conv_u[:, c], conv_u[:, c], tmp[:, 4 + j], ALU.mult).then_inc(src_ready, 1)
                    dve.wait_ge(src_ready, src_count(C_Z2 + c0 + 1))
                if s == S_OC2 - 1:
                    for c in range(WC):
                        split_act(C_Z2 + c, c, conv_u[:, c])

            def largest(h):
                dve.wait_ge(s_done, h + 1)
                dve.wait_ge(negf_ready, h + 1)
                if h >= 2:
                    dve.wait_ge(pt_done, h - 1)
                at = 16 + 4 * (h % 2)
                for i in range(TB):
                    w = P * (i + 1)
                    mark(V.tensor_tensor_reduce(out=probs[:, h % 2, QUERY_AT[i]:QUERY_AT[i] + w],
                                                in0=head_columns(h)[:, QUERY_AT[i]:QUERY_AT[i] + w], in1=neg_f[:, h, 0:w],
                                                scale=1.0, scalar=-3.0e38, op0=ALU.add, op1=ALU.max,
                                                accum_out=small[:, at + i:at + i + 1]))
                settle()
                V.tensor_scalar(small[:, at + 8:at + 12], small[:, at:at + 4], -1.0, None, ALU.mult).then_inc(s_max, 1)

            def normalise(h):
                dve.wait_ge(p_exp, 4 * h + 4)
                at = 32 + 4 * (h % 2)
                mark(V.reciprocal(small[:, at + 8:at + 12], small[:, at:at + 4]))
                settle()
                for i in range(TB):
                    part = probs[:, h % 2, QUERY_AT[i]:QUERY_AT[i] + P * (i + 1)]
                    ins = V.tensor_scalar(part, part, small[:, at + 8 + i:at + 9 + i], None, ALU.mult)
                ins.then_inc(p_ready2, 1)

            largest(0)
            normalise(0)
            for h in range(HEADS):
                if h + 1 < HEADS:
                    largest(h + 1)
                    normalise(h + 1)
                if h >= 3 and h % 2:
                    c = (h - 3) // 2
                    split_act(C_O2 + c, WC + c, psum[:, 6 + c % 2])
            split_act(C_O2 + WC - 1, DC - 1, psum[:, 7])
            for s in range(S_OA2, S_O2):
                finished(s)
                for m in range(4):
                    ins = V.tensor_tensor(tmp[:, m], bank(s, m), ga[:, 4 * (s - S_OA2) + m], ALU.mult)
                free(ins)
                settle()
                for m in range(4):
                    c = 4 * (s - S_OA2) + m
                    V.tensor_tensor(gc[:, c], gc[:, c], tmp[:, m], ALU.add).then_inc(src_ready, 1)
                split_w(s + 2)
                for m in range(4):
                    c = 4 * (s - S_OA2) + m
                    dve.wait_ge(src_ready, src_count(C_M2 + c))
                    split_act(C_M2 + c, c, gc[:, c])
            for s in range(S_O2, S_UP):
                finished(s)
                for j in range(2):
                    c = 2 * (s - S_O2) + j
                    V.tensor_tensor(xT[:, c], bank(s, j), xT[:, c], ALU.add).then_inc(src_ready, 1)
                split_w(s + 2)
            dve.wait_ge(src_ready, src_count(C_UP2 + DC - 1))
            for c in range(DC):
                split_act(C_UP2 + c, c, xT[:, c], col("norm_ffn_g_2", c))
            inverse(N_FFN2)
            with dve.Fori(0, FFN_STEPS) as i:
                for side in range(2):
                    own, to = (0, 2) if side == 0 else (4, 0)
                    finished(S_UP + side, i)
                    for j in range(2):
                        V.tensor_tensor(tmp[:, own + j], bank(S_UP + side, j), R(N_FFN2), ALU.mult).then_inc(up_scaled, 1)
                    if side == 0:
                        split_w(S_UP + 2, i)
                    for j in range(2):
                        dve.wait_ge(up_scaled, 4 * i + (2 * side + j + 1))
                        dve.wait_ge(up_tap, 4 * i + (2 * side + j + 1))
                        V.scalar_tensor_tensor(tmp[:, to + j, 1:], tmp[:, own + j, 0:TOKENS - 1],
                                               tap_col(1, 2 * i + (side * FC + j)), tmp[:, to + j, 1:],
                                               ALU.mult, ALU.add).then_inc(up_mid, 1)
                    for j in range(2):
                        dve.wait_ge(up_mid, 4 * i + (2 * side + j + 1))
                        V.scalar_tensor_tensor(tmp[:, to + j, 2:], tmp[:, own + j, 0:TOKENS - 2],
                                               tap_col(0, 2 * i + (side * FC + j)), tmp[:, to + j, 2:],
                                               ALU.mult, ALU.add).then_inc(up_conv, 1)
                for j in range(2):
                    dve.wait_ge(up_conv, 4 * i + (j + 3))
                    dve.wait_ge(up_silu, 2 * i + (j + 1))
                    V.tensor_tensor(tmp[:, j], tmp[:, j], tmp[:, 2 + j], ALU.mult).then_inc(up_hidden, 1)
                split_w(S_UP + 3, i)
                for j in range(2):
                    dve.wait_ge(up_hidden, 2 * i + (j + 1))
                    dve.wait_ge(hid_hi_ready, 2 * i + (FC + j + 1))
                    at = bass.ds(2 * i + j, 1)
                    V.tensor_tensor(hid_lo[:, at].rearrange("p a n -> p (a n)"), tmp[:, j],
                                    hid_hi[:, at].rearrange("p a n -> p (a n)").bitcast(F32),
                                    ALU.subtract).then_inc(hid_lo_ready, 1)
                dve.wait_ge(hid_lo_ready, 2 * i + (FC + 2))
            for s in range(S_DOWN2, N_SLABS):
                finished(s)
                half = (s - S_DOWN2) // DOWN_SLABS
                if (s - S_DOWN2) % DOWN_SLABS == DOWN_SLABS - 1:
                    for b in range(TB):
                        part = xnat[:, b, half * WIDTH:(half + 1) * WIDTH]
                        V.tensor_tensor(part, bank(s, b), part, ALU.add).then_inc(xn_sum, 1)
                split_w(s + 2)
                if s in (S_DOWN2 + 1, S_DOWN2 + 3):
                    k = (s - S_DOWN2 - 1) // 2
                    dve.wait_ge(xn_turned, k + 1)
                    V.tensor_copy(xnat[:, 2 * k:2 * k + 2].rearrange("p b d -> p (b d)"),
                                  psum[:, 4:8].rearrange("p b n -> p (b n)")).then_inc(xn_ready, 1)
                    dve.wait_ge(xn_ready, k + 1)
            dve.wait_ge(xn_sq, 2 * TB)
            V.tensor_tensor(small[:, 48:52], small[:, 8:8 + TB], small[:, 8 + TB:8 + 2 * TB], ALU.add).then_inc(xn_mean, 1)
            dve.wait_ge(xn_root, 1)
            mark(V.reciprocal(small[:, 52:56], small[:, 48:52]))
            settle()
            dve.wait_ge(gain_in, 16)
            dve.wait_ge(xn_sum, 2 * TB)
            for b in range(TB):
                V.scalar_tensor_tensor(xnat[:, b], xnat[:, b], small[:, 52 + b:53 + b], gain_out[:, :],
                                       ALU.mult, ALU.mult).then_inc(xn_out, 1)

        @block.tensor
        def _(pe):
            mm = nc.tensor.matmul
            sems = {"evicted": evicted, "lg_ready": lg_ready, "ffn_gate": ffn_gate, "ffn_up": ffn_up, "x_sum": x_sum,
                    "gate_pre": gate_pre, "src_ready": src_ready, "up_scaled": up_scaled, "xn_sum": xn_sum}

            def wait_freed(g, more=0):
                name, count = freed(g)
                pe.wait_ge(sems[name], count + more)

            def wait_banks(g):
                for k in (g - 1, g - 2):
                    if k >= 0 and bank_of(k) == bank_of(g):
                        wait_freed(k)
                        break

            def wait_w(s, i=None):
                pe.wait_ge(w_lo_ready, s + 1 + (0 if i is None else 2 * i))

            def product(dst, stationary, moving, first, last):
                mm(dst, stationary[0], moving[0], start=first, stop=False)
                mm(dst, stationary[0], moving[1], start=False, stop=False)
                return mm(dst, stationary[1], moving[0], start=False, stop=last)

            def w_part(s, k, c0, n):
                at = k * SLABS[s][5] + c0
                return w_hi[:, s % 2, at:at + n], w_lo[:, s % 2, at:at + n]

            def act_part(chunk, t0=0, n=TOKENS):
                return act_hi[:, chunk, t0:t0 + n], act_lo[:, chunk, t0:t0 + n]

            def slab_a(s, q=None, i=None):
                wait_w(s, i)
                b = bank_of(GROUP[s])
                for k in range(DC):
                    if q is not None:
                        pe.wait_ge(act_lo_ready, q + k + 1)
                    for j in range(SLABS[s][5] // P):
                        ins = product(psum[:, b + j], w_part(s, k, j * P, P), act_part(k), k == 0, k == DC - 1)
                ins.then_inc(slab_done, 1)

            def slab_b(s, place, q=None, order=(0, 1, 2, 3), before_last=None):
                wait_w(s)
                wait_banks(GROUP[s])
                b = bank_of(GROUP[s])
                if q is not None:
                    pe.wait_ge(act_lo_ready, q + WC)
                for m in order:
                    if m == order[-1] and before_last is not None:
                        before_last()
                    for k in range(WC):
                        ins = product(psum[:, b + m], w_part(s, k, m * P, P), act_part(place + k), k == 0, k == WC - 1)
                ins.then_inc(slab_done, 1)

            def slab_v(s, part):
                wait_w(s)
                if part == 0:
                    wait_banks(GROUP[s])
                b = bank_of(GROUP[s])
                for k in range(ROWS_B):
                    for tb in range(TB):
                        ins = product(psum[:, b + tb], act_part(ROWS_B * part + k, tb * P, P), w_part(s, k, 0, WIDTH),
                                      part == 0 and k == 0, part == 1 and k == ROWS_B - 1)
                ins.then_inc(slab_done, 1)

            def sum_squares(r, bank):
                pe.wait_ge(sq_summed, SQ_DONE[r])
                mm(psum[:, bank], ones[:], acc[:, r % 2], start=True, stop=True).then_inc(ssq_done, 1)

            def turn_row(row, bank):
                for tb in range(TB):
                    ins = mm(psum[:, bank, tb:tb + 1], row[:, tb * P:(tb + 1) * P], ident[:, 0:1],
                             start=tb == 0, stop=True, skip_group_check=True)
                ins.then_inc(row_turned, 1)

            pe.wait_ge(const_bf, 3)
            pe.wait_ge(row_in, 16 * (len(ROWS) + 3))
            nc.tensor.transpose(psum[:, 7, 0:NROWS], rows[:, :], ident[0:NROWS, 0:NROWS])
            for j in range(2):
                ins = nc.tensor.transpose(psum[:, 7, NROWS + j * TAP_ROWS:NROWS + (j + 1) * TAP_ROWS], tap_rows[:, j],
                                          ident[0:TAP_ROWS, 0:TAP_ROWS])
            ins.then_inc(par_done, 1)
            pe.wait_ge(x_in, 16 * TB)
            for c in range(DC):
                if c == DC - 1:
                    pe.wait_ge(par_ready, 1)
                for tb in range(TB):
                    ins = nc.tensor.transpose(psum[:, c, tb * P:(tb + 1) * P], xin[:, tb, c * P:(c + 1) * P], ident[:])
                ins.then_inc(x_turned, 1)
            for s in range(S_V):
                if s == 0:
                    pe.wait_ge(src_ready, DC)
                if s == S_Q:
                    pe.wait_ge(evicted, 2)
                wait_banks(GROUP[s])
                slab_a(s, q=C_MIX if s == 0 else None)
                if s == 0:
                    sum_squares(N_MIX, bank_of(0) + 3)
                if 2 <= s < 2 + WC:
                    c = s - 2
                    if c == 0:
                        pe.wait_ge(bd_in, 64)
                    if c >= 2:
                        pe.wait_ge(gate_read, c - 1)
                    pe.wait_ge(conv_done, c + 1)
                    b = bank_of(GROUP[s])
                    mm(psum[:, b + 2], gate_bd[:, 0, c], xc[:, c], start=True, stop=True)
                    mm(psum[:, b + 3], gate_bd[:, 1, c], xc[:, c], start=True, stop=True).then_inc(gates_done, 1)
            pe.wait_ge(gate_read, WC)
            turn_row(rstd[:, 0], 7)
            slab_v(S_V, 0)
            slab_v(S_V + 1, 1)

            def columns(h, at, n):
                return psum[:, 3 * (h % 2) + at // TOKENS, at % TOKENS:at % TOKENS + n]

            def head_rows(x, h, t0, n):
                p = HD * (h % 2)
                return x[p:p + HD, h // 2, t0:t0 + n]

            def values(h, weights, v_rows):
                p = HD * (h % 2)
                for kb in range(TB):
                    n = TOKENS - kb * P
                    ins = mm(psum[p:p + HD, 6 + (h // 2) % 2, kb * P:TOKENS], v_rows[:, kb, h * HD:(h + 1) * HD],
                             weights[:, h % 2, KEY_AT[kb]:KEY_AT[kb] + n], start=kb == 0, stop=kb == TB - 1,
                             skip_group_check=True)
                return ins

            def scores_kq(h):
                if h >= 2:
                    pe.wait_ge(att_ready, h - 1)
                for kb in (0, 1, 3, 2):
                    n = TOKENS - kb * P
                    dst = columns(h, KEY_AT[kb], n)
                    mm(dst, head_rows(kT, h, kb * P, P), head_rows(qT, h, kb * P, n), start=kb != 3, stop=False,
                       skip_group_check=True)
                    ins = mm(dst[:, 0:P], ident_bf[:], mask_kq[:], start=False, stop=True, skip_group_check=True)
                ins.then_inc(z_done, 1)

            def suffix(h):
                pe.wait_ge(soft_ready, h + 1)
                for kb in (0, 1, 3, 2):
                    for jb in range(kb, TB):
                        n = TOKENS - jb * P
                        ins = mm(columns(h, KEY_AT[kb] + (jb - kb) * P, n), neg_tri[:] if jb == kb else neg_ones[:],
                                 soft[:, h % 2, KEY_AT[jb]:KEY_AT[jb] + n], start=False, stop=True, skip_group_check=True)
                ins.then_inc(suffix_done, 1)

            def values_kq(h):
                pe.wait_ge(att_ready, h + 1)
                if h == 2:
                    pe.wait_ge(root_done, N_LRU + 1)
                if h >= 4 and h % 2 == 0:
                    pe.wait_ge(src_ready, C_ATT + h // 2 - 1)
                values(h, att, v).then_inc(pv_done, 1)

            pe.wait_ge(evicted, freed(GROUP[S_V])[1])
            sum_squares(N_LRU, 7)
            scores_kq(0)
            for h in range(HEADS):
                if h + 1 < HEADS:
                    scores_kq(h + 1)
                suffix(h)
                if h:
                    values_kq(h - 1)
            pe.wait_ge(att_ready, HEADS)
            values_kq(HEADS - 1)
            slab_b(S_OUT_LRU, 0, q=C_LRU)
            pe.wait_ge(src_ready, C_ATT + WC)
            sum_squares(N_ATT, 4)
            slab_b(S_OUT_LRU + 1, 0, order=(1, 2, 3, 0), before_last=lambda: pe.wait_ge(root_done, N_ATT + 1))
            slab_b(S_OUT_ATT, WC, q=C_ATT)
            slab_b(S_OUT_ATT + 1, WC)


            def up_and_down(s0, s_down, q, r, transposed, hid0, between):
                wait_banks(GROUP[s0])
                slab_a(s0, q=q)
                sum_squares(r, bank_of(GROUP[s0]) + 3)
                wait_banks(GROUP[s0 + 1])
                slab_a(s0 + 1)
                with pe.Fori(1, FFN_STEPS) as i:
                    for j in range(2):
                        name, _ = freed(GROUP[s0 + j])
                        per = freed(GROUP[s0 + 2 + j])[1] - freed(GROUP[s0 + j])[1]
                        pe.wait_ge(sems[name], i * per + (freed(GROUP[s0 + j])[1] - per))
                        slab_a(s0 + j, i=i)
                for s in range(s_down, s_down + 2 * DOWN_SLABS):
                    half, part = (s - s_down) // DOWN_SLABS, (s - s_down) % DOWN_SLABS
                    wait_w(s)
                    if part == 0:
                        wait_banks(GROUP[s])
                    b = bank_of(GROUP[s])
                    for k in range(SLABS[s][3]):
                        n = SLABS[s][2] + k
                        if half == 0:
                            pe.wait_ge(hid_lo_ready, hid0 + n + 1)
                        for m in range(4):
                            if transposed:
                                ins = product(psum[:, b + m], w_part(s, k, m * P, P), (hid_hi[:, n], hid_lo[:, n]),
                                              n == 0, n == FC - 1)
                            else:
                                ins = product(psum[:, b + m], (hid_hi[:, n, m * P:(m + 1) * P], hid_lo[:, n, m * P:(m + 1) * P]),
                                              w_part(s, k, 0, WIDTH), n == 0, n == FC - 1)
                    ins.then_inc(slab_done, 1)
                    between(s)

            up_and_down(S_FFN, S_DOWN, C_FFN, N_FFN, True, 0, lambda s: None)
            wait_banks(GROUP[S_F2])
            slab_a(S_F2, q=C_MIX2)
            sum_squares(N_FINAL, bank_of(GROUP[S_F2]) + 2)
            sum_squares(N_MIX2, bank_of(GROUP[S_F2]) + 3)
            for s in list(range(S_K2, S_V2)) + list(range(S_CC, S_OC2)):
                wait_banks(GROUP[s])
                slab_a(s)
                if s == S_K2 + 1:
                    pe.wait_ge(both_ready, 1)
                    turn_row(rstd[:, 0], bank_of(GROUP[s]) + 3)
                if s == S_V2 - 1:
                    pe.wait_ge(row_turned, 2)
                    slab_v(S_V2, 0)
                    slab_v(S_V2 + 1, 1)
                if S_CC <= s < S_CC + HEADS:
                    h = s - S_CC
                    pe.wait_ge(f_sum, 1)
                    if h == 0:
                        wait_freed(GROUP[S_V2])
                    if h >= 2:
                        pe.wait_ge(negf_ready, h - 1)
                    mm(psum[:, bank_of(GROUP[s]) + 3], ident[0:HEADS, h:h + 1].broadcast_to([HEADS, P]), fsum[:, 0], start=True, stop=True).then_inc(negf_done, 1)
            slab_b(S_OC2, 0, q=C_Z2)
            slab_b(S_OC2 + 1, 0)

            def scores_qk(h):
                if h >= 2:
                    pe.wait_ge(pt_ready, h - 1)
                for i in (3, 2, 0, 1):
                    n = P * (i + 1)
                    dst = columns(h, QUERY_AT[i], n)
                    mm(dst, head_rows(q2, h, i * P, P), head_rows(k2, h, 0, n), start=i != 0, stop=False,
                       skip_group_check=True)
                    ins = mm(dst[:, i * P:n], ident_bf[:], mask_qk[:], start=False, stop=True, skip_group_check=True)
                ins.then_inc(s_done, 1)

            def turn_probs(h):
                pe.wait_ge(p_ready2, h + 1)
                for kb in range(TB):
                    for i in range(kb, TB):
                        ins = nc.tensor.transpose(columns(h, KEY_AT[kb] + (i - kb) * P, P),
                                                  probs[:, h % 2, QUERY_AT[i] + kb * P:QUERY_AT[i] + (kb + 1) * P], ident[:])
                ins.then_inc(pt_done, 1)

            def values_qk(h):
                pe.wait_ge(pt_ready, h + 1)
                if h >= 4 and h % 2 == 0:
                    pe.wait_ge(act_lo_ready, C_O2 + h // 2 - 1)
                values(h, probs_T, v2).then_inc(pv2_done, 1)

            wait_freed(GROUP[S_OC2])
            wait_freed(GROUP[S_OC2 + 1])
            scores_qk(0)
            for h in range(HEADS):
                if h + 1 < HEADS:
                    scores_qk(h + 1)
                turn_probs(h)
                if h:
                    values_qk(h - 1)
            values_qk(HEADS - 1)
            pe.wait_ge(act_lo_ready, C_O2 + WC)
            slab_b(S_OA2, WC, q=C_O2)
            slab_b(S_OA2 + 1, WC)
            for s in range(S_O2, S_UP):
                wait_banks(GROUP[s])
                slab_a(s, q=C_M2 if s == S_O2 else None)

            def turn_x(s):
                if s not in (S_DOWN2 + 1, S_DOWN2 + 3):
                    return
                k = (s - S_DOWN2 - 1) // 2
                if k == 0:
                    wait_freed(GROUP[S_DOWN2 - 1])
                else:
                    pe.wait_ge(xn_ready, 1)
                for tb in range(2):
                    for c in range(DC):
                        ins = nc.tensor.transpose(psum[:, 4 + 2 * tb + c // 4, (c % 4) * P:(c % 4 + 1) * P],
                                                  xT[:, c, (2 * k + tb) * P:(2 * k + tb + 1) * P], ident[:])
                ins.then_inc(xn_turned, 1)

            assert bank_of(GROUP[S_DOWN2]) == 0
            up_and_down(S_UP, S_DOWN2, C_UP2, N_FFN2, False, FC, turn_x)


NAMES = ["x", "norm_mix", "w_in", "conv_w", "conv_b", "w_rg", "b_rg", "w_ig", "b_ig", "lru_lambda", "norm_lru_out",
         "norm_att_out", "w_out", "norm_ffn", "w_ffn_in", "w_ffn_out", "norm_final", "norm_mix_g_2", "w_in_2", "b_f_2",
         "b_gate_2", "conv_mix_w_2", "w_out_conv_2", "w_out_attn_2", "w_o_2", "norm_ffn_g_2", "w_up_2",
         "conv_ffn_w_2", "w_down_2", "norm_f_g_2"]


def kernel(**inputs):
    import numpy as np
    import concourse.bacc as bacc
    from concourse.bass_utils import run_bass_kernel_spmd

    nc = bacc.Bacc("TRN2", target_bir_lowering=False, num_devices=1)
    arrays, tensors = {}, {}
    for name in NAMES:
        a = np.ascontiguousarray(inputs[name])
        arrays[f"in_{name}"] = a
        tensors[name] = nc.dram_tensor(f"in_{name}", a.shape, mybir.dt.from_np(a.dtype), kind="ExternalInput").ap()
    out = nc.dram_tensor("out", (1, TOKENS, D), F32, kind="ExternalOutput").ap()
    two_blocks(nc, tensors, out)
    r = run_bass_kernel_spmd(nc, [arrays], core_ids=[0])
    return r.results[0]["out"]
```

```python
from contextlib import ExitStack

import concourse.bass as bass
from concourse import mybir

F32 = mybir.dt.float32
F32R = mybir.dt.float32r
BF16 = mybir.dt.bfloat16
ALU = mybir.AluOpType
ACT = mybir.ActivationFunctionType

P = 128
TOKENS = 512
D = 1024
DC = D // P
TB = TOKENS // P
WIDTH = 512
WC = WIDTH // P
HEADS = 8
HD = WIDTH // HEADS
FF = 2816
FC = FF // P
EPS = 1e-6
SCALE = HD ** -0.5
MASKED = -1e30
SLAB = 2048
COLS_A = SLAB // DC
ROWS_B = SLAB // WIDTH
FFN_STEPS = FF // COLS_A
CAUSAL = sum(TOKENS - P * b for b in range(TB))
KEY_AT = [0, 512, 1024, 896]
QUERY_AT = [896, 1024, 512, 0]

ROWS = [("norm_mix", 8), ("norm_ffn", 8), ("norm_final", 8), ("conv_w", 16), ("conv_b", 4), ("b_rg", 4),
        ("b_ig", 4), ("lru_lambda", 4), ("norm_lru_out", 4), ("norm_att_out", 4), ("norm_mix_g_2", 8),
        ("b_gate_2", 16), ("conv_mix_w_2", 12), ("norm_ffn_g_2", 8)]
AT = {}
_n = 0
for _name, _rows in ROWS:
    AT[_name] = _n
    _n += _rows
NROWS = _n
TAP_ROWS = 3 * 2 * FC // 2

SLABS = []


def _add(w, kind, k0, nk, c0, nc_):
    SLABS.append((w, kind, k0, nk, c0, nc_))
    return len(SLABS) - 1


def _cols_a(w, c0, n):
    first = len(SLABS)
    for j in range(n // COLS_A):
        _add(w, "A", 0, DC, c0 + j * COLS_A, COLS_A)
    return first


def _down(w):
    first = len(SLABS)
    for half in range(2):
        for k0 in range(0, FC, ROWS_B):
            _add(w, "B", k0, min(ROWS_B, FC - k0), half * WIDTH, WIDTH)
    return first


S_LX = _cols_a("w_in", 0, WIDTH)
S_LG = _cols_a("w_in", WIDTH, WIDTH)
S_Q = _cols_a("w_in", 2 * WIDTH, WIDTH)
S_K = _cols_a("w_in", 3 * WIDTH, WIDTH)
S_V = _add("w_in", "B", 0, ROWS_B, 4 * WIDTH, WIDTH)
_add("w_in", "B", ROWS_B, ROWS_B, 4 * WIDTH, WIDTH)
S_OUT_LRU = _add("w_out", "B", 0, WC, 0, WIDTH)
_add("w_out", "B", 0, WC, WIDTH, WIDTH)
S_OUT_ATT = _add("w_out", "B", WC, WC, 0, WIDTH)
_add("w_out", "B", WC, WC, WIDTH, WIDTH)
S_FFN = len(SLABS)
for _i in range(FFN_STEPS):
    _add("w_ffn_in", "A", 0, DC, _i * COLS_A, COLS_A)
    _add("w_ffn_in", "A", 0, DC, FF + _i * COLS_A, COLS_A)
S_DOWN = _down("w_ffn_out")
F_AT = 6 * WIDTH
S_F2 = _add("w_in_2", "A", 0, DC, F_AT, P)
S_K2 = _cols_a("w_in_2", 4 * WIDTH, WIDTH)
S_Q2 = _cols_a("w_in_2", 3 * WIDTH, WIDTH)
S_V2 = _add("w_in_2", "B", 0, ROWS_B, 5 * WIDTH, WIDTH)
_add("w_in_2", "B", ROWS_B, ROWS_B, 5 * WIDTH, WIDTH)
S_CC = _cols_a("w_in_2", WIDTH, WIDTH)
S_CIN = _cols_a("w_in_2", 2 * WIDTH, WIDTH)
S_CB = _cols_a("w_in_2", 0, WIDTH)
S_GC = _cols_a("w_in_2", F_AT + HEADS, D)
S_OC2 = _add("w_out_conv_2", "B", 0, WC, 0, WIDTH)
_add("w_out_conv_2", "B", 0, WC, WIDTH, WIDTH)
S_GA = _cols_a("w_in_2", F_AT + HEADS + D, D)
S_OA2 = _add("w_out_attn_2", "B", 0, WC, 0, WIDTH)
_add("w_out_attn_2", "B", 0, WC, WIDTH, WIDTH)
S_O2 = _cols_a("w_o_2", 0, D)
S_UP = len(SLABS)
for _i in range(FFN_STEPS):
    _add("w_up_2", "A", 0, DC, _i * COLS_A, COLS_A)
    _add("w_up_2", "A", 0, DC, FF + _i * COLS_A, COLS_A)
S_DOWN2 = _down("w_down_2")
N_SLABS = len(SLABS)
DOWN_SLABS = (N_SLABS - S_DOWN2) // 2

GROUP = []
_g = -1
for _s in range(N_SLABS):
    _inner = (_s in (S_V + 1, S_V2 + 1)
              or any(f <= _s < f + 2 * DOWN_SLABS and (_s - f) % DOWN_SLABS for f in (S_DOWN, S_DOWN2)))
    _g += not _inner
    GROUP.append(_g)


def src_count(q):
    return q + 1 - (WC if q >= C_M2 else 0)


def bank_of(g):
    return 4 * (g % 2)


def head_bank(h):
    return 5 - 3 * (h % 2)


def pair_bank(c):
    return c % 2


def _shares_count(g):
    s = GROUP.index(g)
    return s < S_LG or S_Q <= s < S_FFN or S_F2 <= s < S_GC or S_OC2 <= s < S_GA or S_OA2 <= s < S_O2


EVICTED_BEFORE = [sum(_shares_count(k) for k in range(g)) for g in range(GROUP[-1] + 1)]


def freed(g):
    s = GROUP.index(g)
    if S_LG <= s < S_Q:
        return "lg_ready", 2 * (s - S_LG + 1)
    if S_FFN <= s < S_DOWN:
        return ("ffn_up" if (s - S_FFN) % 2 else "ffn_gate"), 2 * ((s - S_FFN) // 2 + 1)
    if S_DOWN <= s < S_F2:
        return "src_ready", src_count(C_MIX2 + WC * ((s - S_DOWN) // DOWN_SLABS + 1) - 1)
    if S_GC <= s < S_OC2:
        return "gate_pre", 2 * (s - S_GC + 1)
    if S_GA <= s < S_OA2:
        return "gate_pre", DC + 2 * (s - S_GA + 1)
    if S_O2 <= s < S_UP:
        return "src_ready", src_count(C_UP2 + 2 * (s - S_O2) + 1)
    if S_UP <= s < S_DOWN2:
        return "up_scaled", 2 * (s - S_UP + 1)
    if S_DOWN2 <= s:
        return "xn_sum", TB * ((s - S_DOWN2) // DOWN_SLABS + 1)
    return "evicted", 1 + EVICTED_BEFORE[g]


C_MIX, C_LRU, C_ATT, C_FFN, C_MIX2, C_Z2, C_O2, C_M2, C_UP2 = 0, 8, 12, 16, 24, 32, 36, 40, 48
N_MIX, N_LRU, N_ATT, N_FFN, N_FINAL, N_MIX2, N_FFN2 = range(7)
SQ_FIRST = [0, 8, 12, 16, 24, 25, 40]
SQ_DONE = [8, 12, 16, 24, 39, 40, 48]
RSTD_AT = [0, 1, 2, 0, 1, 2, 0]
TURN = [0, 1, 2, 3, 5, 4, 6]


def two_blocks(nc, t, out):
    with ExitStack() as ctx:
        def sb(name, shape, dt=F32, where=None):
            return (where or ctx).enter_context(nc.sbuf_tensor(name, shape, dt))

        def sem(name):
            return ctx.enter_context(nc.semaphore(name))

        xT = sb("xT", [P, DC, TOKENS])
        raw = sb("raw", [P, 2, SLAB])
        w_hi = sb("w_hi", [P, 2, SLAB], F32R)
        w_lo = sb("w_lo", [P, 2, SLAB], F32R)
        tmp = sb("tmp", [P, 6, TOKENS])
        rstd = sb("rstd", [P, 3, TOKENS])
        acc = tmp[:, 2:4]
        sq = tmp[:, 4:6]
        par = sb("par", [P, NROWS + 2 * TAP_ROWS])
        ident = sb("ident", [P, P])
        ones = sb("ones", [P, P])
        neg_ones = sb("neg_ones", [P, P])
        neg_tri = sb("neg_tri", [P, P])
        ident_bf = sb("ident_bf", [P, P], BF16)
        mask_kq = sb("mask_kq", [P, P], BF16)
        mask_qk = sb("mask_qk", [P, P], BF16)
        small = sb("small", [P, 64])
        decay = sb("decay", [P, WC])
        f_bias = sb("f_bias", [HEADS, 1])
        eps = sb("eps", [P, 2])
        gain_both = sb("gain_both", [P, DC])
        act_scope = ExitStack()
        act_hi = sb("act_hi", [P, DC, TOKENS], F32R, act_scope)
        act_lo = sb("act_lo", [P, DC, TOKENS], F32R, act_scope)
        scope = ExitStack()
        hid_hi = sb("hid_hi", [P, FC, TOKENS], F32R, scope)
        hid_lo = sb("hid_lo", [P, FC, TOKENS], F32R, scope)
        scope.close()
        lx = sb("lx", [P, WC, TOKENS], F32, scope)
        lg = sb("lg", [P, WC, TOKENS], F32, scope)
        xc = sb("xc", [P, WC, TOKENS], F32, scope)
        inner = ExitStack()
        xin = sb("xin", [P, TB, D], F32, inner)
        rows = sb("rows", [NROWS, P], F32, inner)
        tap_rows = sb("tap_rows", [TAP_ROWS, 2, P], F32, inner)
        inner.close()
        qT = sb("qT", [P, WC, TOKENS], F32, scope)
        kT = sb("kT", [P, WC, TOKENS], F32, scope)
        v = sb("v", [P, TB, WIDTH], F32, scope)
        yatt = sb("yatt", [P, WC, TOKENS], F32, scope)
        gate_bd = sb("gate_bd", [P, 2, WC, P], F32, inner)
        gate_t = sb("gate_t", [P, 2, TOKENS], F32, inner)
        gate_i = sb("gate_i", [P, 2, TOKENS], F32, inner)
        root_t = sb("root_t", [P, 2, TOKENS], F32, inner)
        lru_rc = sb("lru_rc", [P, TOKENS], F32, inner)
        lru_a = sb("lru_a", [P, TOKENS], F32, inner)
        inner.close()
        stick = sb("stick", [P, 2, CAUSAL], F32, inner)
        soft = sb("soft", [P, 2, CAUSAL], F32, inner)
        att = sb("att", [P, 2, CAUSAL], F32, inner)
        inner.close()
        scope.close()
        m_hi = sb("m_hi", [P, DC, TOKENS], F32R, inner)
        inner.close()
        q2 = sb("q2", [P, WC, TOKENS], F32, scope)
        k2 = sb("k2", [P, WC, TOKENS], F32, scope)
        v2 = sb("v2", [P, TB, WIDTH], F32, scope)
        gc = sb("gc", [P, DC, TOKENS], F32, scope)
        fsum = sb("fsum", [HEADS, 2, TOKENS], F32, inner)
        inner.close()
        ga = sb("ga", [P, DC, TOKENS], F32, scope)
        m_lo = sb("m_lo", [P, DC, TOKENS], F32R, inner)
        inner.close()
        neg_f = sb("neg_f", [P, HEADS, TOKENS], F32, scope)
        conv_p = sb("conv_p", [P, WC, TOKENS], F32, inner)
        conv_u = sb("conv_u", [P, WC, TOKENS], F32, inner)
        inner.close()
        z_hi = sb("z_hi", [P, WC, TOKENS], F32R, inner)
        z_lo = sb("z_lo", [P, WC, TOKENS], F32R, inner)
        inner.close()
        probs = sb("probs", [P, 2, CAUSAL], F32, inner)
        probs_T = tmp[:, 0:5].rearrange("p a n -> p (a n)").rearrange("p (a n) -> p a n", a=2)
        inner.close()
        scope.close()
        act_scope.close()
        xnat = sb("xnat", [P, TB, D], F32, act_scope)
        gain_out = sb("gain_out", [P, D], F32, act_scope)
        junk = sb("junk", [P, WIDTH], F32, act_scope)
        act_scope.close()

        psum = ctx.enter_context(nc.psum_tensor("psum", [P, 8, TOKENS], F32))

        x_in = [sem(f"x_in{b}") for b in range(TB)]
        row_in = sem("row_in")
        bd_in, gain_in = sem("bd_in"), sem("gain_in")
        raw_in = [sem("raw_in0"), sem("raw_in1")]
        ident_zeroed, ident_set, const_set = sem("ident_zeroed"), sem("ident_set"), sem("const_set")
        bd_zeroed = sem("bd_zeroed")
        const_bf = sem("const_bf")
        row_read = sem("row_read")
        par_done, par_ready = sem("par_done"), sem("par_ready")
        decay_ready = sem("decay_ready")
        lam_abs, lam_exp = sem("lam_abs"), sem("lam_exp")
        x_turned = sem("x_turned")
        w_hi_ready, w_lo_ready = sem("w_hi_ready"), sem("w_lo_ready")
        slab_done = sem("slab_done")
        evicted = sem("evicted")
        src_ready = sem("src_ready")
        act_hi_ready, act_lo_ready = sem("act_hi_ready"), sem("act_lo_ready")
        sq_ready, sq_summed = sem("sq_ready"), sem("sq_summed")
        ssq_done, root_done, rstd_ready = sem("ssq_done"), sem("root_done"), sem("rstd_ready")
        dve_step = sem("dve_step")
        act_step = sem("act_step")
        conv_done, gates_done, gate_read, tanh_done = sem("conv_done"), sem("gates_done"), sem("gate_read"), sem("tanh_done")
        root_t_done, gelu_done = sem("root_t_done"), sem("gelu_done")
        row_turned = sem("row_turned")
        lg_ready = sem("lg_ready")
        z_done, z_abs, z_log, soft_ready = sem("z_done"), sem("z_abs"), sem("z_log"), sem("soft_ready")
        suffix_done, att_ready, pv_done = sem("suffix_done"), sem("att_ready"), sem("pv_done")
        ffn_gate, ffn_silu = sem("ffn_gate"), sem("ffn_silu")
        ffn_up, ffn_hidden = sem("ffn_up"), sem("ffn_hidden")
        hid_hi_ready, hid_lo_ready = sem("hid_hi_ready"), sem("hid_lo_ready")
        xn_sq, xn_mean = sem("xn_sq"), sem("xn_mean")
        f_abs = sem("f_abs")
        ms2_ready, f_pre, f_exp, f_ln, f_sum = sem("ms2_ready"), sem("f_pre"), sem("f_exp"), sem("f_ln"), sem("f_sum")
        negf_done, negf_ready = sem("negf_done"), sem("negf_ready")
        gate_pre, gate_ready = sem("gate_pre"), sem("gate_ready")
        s_done, s_max, p_exp, p_ready2, pt_done, pt_ready = sem("s_done"), sem("s_max"), sem("p_exp"), sem("p_ready2"), sem("pt_done"), sem("pt_ready")
        pv2_done = sem("pv2_done")
        up_scaled, up_tap, up_conv, up_silu = sem("up_scaled"), sem("up_tap"), sem("up_conv"), sem("up_silu")
        up_mid = sem("up_mid")
        up_hidden, up_hi, up_lo = sem("up_hidden"), sem("up_hi"), sem("up_lo")
        xn_turned, xn_ready, xn_sum, xn_root, xn_out, stored = sem("xn_turned"), sem("xn_ready"), sem("xn_sum"), sem("xn_root"), sem("xn_out"), sem("stored")

        def col(name, j, n=P):
            return par[0:n, AT[name] + j:AT[name] + j + 1]

        def tap_col(tap, chunk):
            return par[:, bass.ds(chunk + (NROWS + tap * 2 * FC), 1)]

        block = ctx.enter_context(nc.Block())

        @block.sync
        def _(sp):
            def load_slab(s, i=None):
                w, kind, k0, nk, c0, nc_ = SLABS[s]
                step = 0 if i is None else i
                if s >= 2 or i is not None:
                    sp.wait_ge(w_lo_ready, s - 1 + 2 * step)
                src = t[w][0].rearrange("(k p) n -> p k n", p=P)[:, k0:k0 + nk]
                src = src[:, :, c0:c0 + nc_] if i is None else src[:, :, bass.ds(i * COLS_A + c0, COLS_A)]
                dst = raw[:, s % 2, 0:nk * nc_].rearrange("p (k n) -> p k n", k=nk)
                sp.dma_start(dst, src).then_inc(raw_in[s % 2], 16)

            load_slab(0)
            x_rows = t["x"][0].rearrange("(b p) d -> p b d", p=P)
            for b in range(TB):
                sp.dma_start(xin[:, b, :], x_rows[:, b, :]).then_inc(x_in[b], 16)
            load_slab(1)
            sp.wait_ge(bd_zeroed, 1)
            for g, name in enumerate(("w_rg", "w_ig")):
                for e in range(2):
                    src = t[name][0].rearrange("(c e) i o -> e i c o", e=2)
                    sp.dma_start(gate_bd[64 * e:64 * e + 64, g, :, 64 * e:64 * e + 64], src[e]).then_inc(bd_in, 16)
            for s in range(2, S_FFN):
                load_slab(s)
            with sp.Fori(0, FFN_STEPS) as i:
                load_slab(S_FFN, i)
                load_slab(S_FFN + 1, i)
            for s in range(S_DOWN, S_UP):
                load_slab(s)
            with sp.Fori(0, FFN_STEPS) as i:
                load_slab(S_UP, i)
                load_slab(S_UP + 1, i)
            for s in range(S_DOWN2, N_SLABS):
                load_slab(s)
                if s == S_DOWN2 + 2:
                    sp.wait_ge(slab_done, S_DOWN2)
                    sp.dma_start(gain_out[:, :], t["norm_f_g_2"].rearrange("(a d) -> a d", a=1).broadcast_to([P, D])).then_inc(gain_in, 16)
            out_rows = out[0].rearrange("(b p) d -> p b d", p=P)
            for b in range(TB):
                sp.wait_ge(xn_out, b + 1)
                sp.dma_start(out_rows[:, b, :], xnat[:, b, :]).then_inc(stored, 16)
            sp.wait_ge(stored, 16 * TB)

        @block.gpsimd
        def _(pool):
            g = nc.gpsimd
            g.memset(ident[:], 0.0).then_inc(ident_zeroed, 1)
            pool.wait_ge(ident_zeroed, 1)
            g.affine_select(out=ident[:], in_=ident[:], compare_op=ALU.not_equal, fill=1.0, base=0,
                            pattern=[[-1, P]], channel_multiplier=1).then_inc(ident_set, 1)
            g.memset(ones[:], 1.0).then_inc(const_set, 1)
            g.memset(eps[:, 0:1], EPS).then_inc(const_set, 1)
            g.memset(eps[:, 1:2], EPS * EPS).then_inc(const_set, 1)
            g.memset(neg_tri[:], -1.0).then_inc(const_set, 1)
            g.memset(tmp[:, 0, 0:2 * P], MASKED).then_inc(const_set, 1)
            g.memset(neg_ones[:], -1.0).then_inc(const_set, 1)
            pool.wait_ge(const_set, 6)
            g.affine_select(out=neg_tri[:], in_=neg_tri[:], compare_op=ALU.is_ge, fill=0.0, base=0,
                            pattern=[[-1, P]], channel_multiplier=1).then_inc(const_set, 1)
            g.affine_select(out=tmp[:, 0, 0:P], in_=tmp[:, 0, 0:P], compare_op=ALU.is_ge, fill=0.0, base=0,
                            pattern=[[-1, P]], channel_multiplier=1).then_inc(const_set, 1)
            g.affine_select(out=tmp[:, 0, P:2 * P], in_=tmp[:, 0, P:2 * P], compare_op=ALU.is_gt, fill=0.0, base=0,
                            pattern=[[1, P]], channel_multiplier=-1).then_inc(const_set, 1)
            pool.wait_ge(const_set, 9)
            pool.wait_ge(ident_set, 1)
            g.tensor_copy(mask_kq[:], tmp[:, 0, 0:P]).then_inc(const_bf, 1)
            g.tensor_copy(mask_qk[:], tmp[:, 0, P:2 * P]).then_inc(const_bf, 1)
            g.tensor_copy(ident_bf[:], ident[:]).then_inc(const_bf, 1)
            pool.wait_ge(x_turned, DC)
            pool.wait_ge(par_done, 1)
            g.memset(gate_bd[:], 0.0).then_inc(bd_zeroed, 1)
            n = 0
            for rs in ((N_MIX,), (N_LRU,), (N_ATT,), (N_FFN,), (N_FINAL, N_MIX2), (N_FFN2,)):
                for c in range(4 if rs[0] in (N_LRU, N_ATT) else DC):
                    for r in rs:
                        pool.wait_ge(sq_ready, n + 1)
                        if c == 0:
                            if r >= 2:
                                pool.wait_ge(ssq_done, r - 1)
                            ins = g.tensor_copy(acc[:, r % 2], sq[:, n % 2])
                        else:
                            pool.wait_ge(sq_summed, n)
                            ins = g.tensor_tensor(acc[:, r % 2], acc[:, r % 2], sq[:, n % 2], ALU.add)
                        ins.then_inc(sq_summed, 1)
                        n += 1

        @block.scalar
        def _(act):
            A = nc.scalar.activation
            state = {"sq": 0}

            def split_w(s, i=None, last=False):
                if s >= N_SLABS:
                    return
                step = 0 if i is None else i
                n = SLABS[s][3] * SLABS[s][5] if i is None else SLAB
                act.wait_ge(raw_in[s % 2], 16 * (s // 2 + 1 + step))
                if s >= 2:
                    act.wait_ge(slab_done, s - 1 + step * 2)
                A(w_hi[:, s % 2, 0:n], raw[:, s % 2, 0:n], ACT.Copy).then_inc(w_hi_ready, 1)

            def square(src, scale=1.0):
                n = state["sq"]
                if n >= 2:
                    act.wait_ge(sq_summed, n - 1)
                A(sq[:, n % 2], src, ACT.Square, scale=scale).then_inc(sq_ready, 1)
                state["sq"] += 1

            def split_act(q, hi, src, gain, free=None):
                act.wait_ge(src_ready, src_count(q))
                if free is not None:
                    act.wait_ge(slab_done, free)
                A(hi, src, ACT.Copy, scale=gain).then_inc(act_hi_ready, 1)

            def root(r, src):
                act.wait_ge(ssq_done, r + 1)
                A(rstd[:, RSTD_AT[r]], src, ACT.Sqrt, bias=eps[:, 0:1],
                  scale=1.0 / (WIDTH if r in (N_LRU, N_ATT) else D)).then_inc(root_done, 1)

            r = 0
            for name, n in ROWS:
                src = t[name]
                flat = src[0] if len(src.shape) > 1 else src
                if len(flat.shape) == 2:
                    flat = flat.rearrange("a b -> (a b)")
                act.dma_start(rows[r:r + n, :], flat.rearrange("(r c) -> r c", c=P)).then_inc(row_in, 16)
                r += n
            taps = t["conv_ffn_w_2"][0].rearrange("k (c p) -> (k c) p", p=P)
            for j in range(2):
                act.dma_start(tap_rows[:, j, :], taps[j * TAP_ROWS:(j + 1) * TAP_ROWS, :]).then_inc(row_in, 16)
            act.dma_start(f_bias[:, :], t["b_f_2"].rearrange("a h -> h a")).then_inc(row_in, 16)
            split_w(0)
            act.wait_ge(par_done, 1)
            A(par[:, 0:NROWS + 2 * TAP_ROWS], psum[:, 7, 0:NROWS + 2 * TAP_ROWS], ACT.Copy).then_inc(par_ready, 1)
            act.wait_ge(par_ready, 1)
            for c in range(DC):
                split_act(C_MIX + c, act_hi[:, c], xT[:, c], col("norm_mix", c))
                square(xT[:, c])
                if c == 3:
                    split_w(1)
            A(small[:, 0:4], par[:, AT["lru_lambda"]:AT["lru_lambda"] + WC], ACT.Abs).then_inc(lam_abs, 1)
            act.wait_ge(lam_abs, 1)
            A(small[:, 4:8], small[:, 0:4], ACT.Exp, scale=-1.0).then_inc(lam_exp, 1)
            root(N_MIX, psum[:, bank_of(0) + 3])
            for s in range(0, S_V + 1):
                split_w(s + 2)
                if s in (S_LG, S_LG + 1):
                    for c in range(2 * (s - S_LG), 2 * (s - S_LG) + 2):
                        act.wait_ge(lg_ready, c + 1)
                        A(lg[:, c], lg[:, c], ACT.Gelu_apprx_tanh).then_inc(gelu_done, 1)
                if 2 <= s < 2 + WC:
                    c = s - 2
                    b = bank_of(GROUP[s])
                    act.wait_ge(gates_done, c + 1)
                    if c >= 2:
                        act.wait_ge(src_ready, C_LRU + c - 1)
                    A(gate_t[:, c % 2], psum[:, b + 2], ACT.Sigmoid, bias=col("b_rg", c)).then_inc(act_step, 1)
                    A(gate_i[:, c % 2], psum[:, b + 3], ACT.Sigmoid, bias=col("b_ig", c)).then_inc(gate_read, 1)
                    act.wait_ge(act_step, c + 1)
                    if c == 0:
                        act.wait_ge(decay_ready, 1)
                    A(gate_t[:, c % 2], gate_t[:, c % 2], ACT.Tanh, scale=decay[:, c:c + 1]).then_inc(tanh_done, 1)
                    act.wait_ge(tanh_done, c + 1)
                    A(root_t[:, c % 2], gate_t[:, c % 2], ACT.Sqrt).then_inc(root_t_done, 1)
                if 4 <= s < 4 + WC:
                    act.wait_ge(src_ready, C_LRU + s - 3)
                    square(lx[:, s - 4])
            root(N_LRU, psum[:, 4])
            nc.scalar.preload_act_table_set("natural_log_exp_and_others")

            def log_part(h):
                z = stick[:, h % 2]
                act.wait_ge(z_done, h + 1)
                b = head_bank(h)
                A(z, psum[:, b:b + 3].rearrange("p b n -> p (b n)")[:, 0:CAUSAL], ACT.Abs).then_inc(z_abs, 1)
                act.wait_ge(z_abs, h + 1)
                A(z, z, ACT.Exp, scale=-1.0).then_inc(act_step, 1)
                act.wait_ge(act_step, WC + h + 1)
                A(z, z, ACT.Ln, bias=1.0).then_inc(z_log, 1)

            def att_operand(c):
                act.wait_ge(src_ready, C_ATT + c + 1)
                square(yatt[:, c])
                split_act(C_ATT + c, act_hi[:, WC + c], yatt[:, c], col("norm_att_out", c), S_V + 2)

            log_part(0)
            split_w(S_V + 3)
            for h in range(HEADS):
                if h + 1 < HEADS:
                    log_part(h + 1)
                act.wait_ge(suffix_done, h + 1)
                if h >= 2:
                    act.wait_ge(pv_done, h - 1)
                b = head_bank(h)
                A(att[:, h % 2], psum[:, b:b + 3].rearrange("p b n -> p (b n)")[:, 0:CAUSAL], ACT.Exp).then_inc(att_ready, 1)
                if h < WC:
                    split_act(C_LRU + h, act_hi[:, h], lx[:, h], col("norm_lru_out", h), S_V + 2)
                if h >= 3 and h % 2:
                    att_operand((h - 3) // 2)
            att_operand(WC - 1)

            for s in range(S_OUT_LRU, S_FFN):
                split_w(s + 2)
                if s == S_OUT_LRU:
                    root(N_ATT, psum[:, 0])
                if s >= S_OUT_ATT:
                    for c in range(4 * (s - S_OUT_ATT), 4 * (s - S_OUT_ATT) + 4):
                        split_act(C_FFN + c, act_hi[:, c], xT[:, c], col("norm_ffn", c), S_OUT_ATT if c < WC else S_FFN)
                        square(xT[:, c])
            root(N_FFN, psum[:, bank_of(GROUP[S_FFN]) + 3])
            nc.scalar.preload_act_table(ACT.Silu)
            with act.Fori(0, FFN_STEPS) as i:
                split_w(S_FFN + 2, i)
                for j in range(2):
                    act.wait_ge(ffn_gate, 2 * i + (j + 1))
                    A(tmp[:, 2 + j], tmp[:, j], ACT.Silu).then_inc(ffn_silu, 1)
                split_w(S_FFN + 3, i)
                for j in range(2):
                    act.wait_ge(ffn_hidden, 2 * i + (j + 1))
                    A(hid_hi[:, bass.ds(2 * i + j, 1)].rearrange("p a n -> p (a n)"), tmp[:, 4 + j], ACT.Copy).then_inc(hid_hi_ready, 1)
            for s in range(S_DOWN, S_F2):
                split_w(s + 2)
                half = (s - S_DOWN) // DOWN_SLABS
                if (s - S_DOWN) % DOWN_SLABS == DOWN_SLABS - 1:
                    for c in range(4 * half, 4 * half + 4):
                        split_act(C_MIX2 + c, act_hi[:, c], xT[:, c], gain_both[:, c:c + 1], S_DOWN)
                        square(xT[:, c])
                        square(xT[:, c], col("norm_final", c))
            b = bank_of(GROUP[S_F2])
            act.wait_ge(ms2_ready, 1)
            A(rstd[:, RSTD_AT[N_MIX2]], rstd[:, RSTD_AT[N_MIX2]], ACT.Sqrt, bias=eps[:, 1:2], scale=1.0 / D).then_inc(root_done, 1)
            root(N_FINAL, psum[:, b + 2])
            n_gate = 0
            for s in range(S_F2, S_OA2 - 1):
                split_w(s + 2)
                if s == S_F2:
                    act.wait_ge(f_pre, 1)
                    nc.scalar.preload_act_table_set("natural_log_exp_and_others")
                    A(fsum[:, 1], fsum[:, 0], ACT.Abs).then_inc(f_abs, 1)
                    act.wait_ge(f_abs, 1)
                    A(fsum[:, 1], fsum[:, 1], ACT.Exp, scale=-1.0).then_inc(f_exp, 1)
                    act.wait_ge(f_exp, 1)
                    A(fsum[:, 1], fsum[:, 1], ACT.Ln, bias=1.0).then_inc(f_ln, 1)
                if S_CC <= s < S_CC + HEADS:
                    h = s - S_CC
                    act.wait_ge(negf_done, h + 1)
                    A(neg_f[:, h], psum[:, bank_of(GROUP[s]) + 3], ACT.Copy).then_inc(negf_ready, 1)
                if S_GC <= s < S_OC2 or S_GA <= s < S_OA2 - 1:
                    for j in range(2):
                        m = n_gate % DC
                        dst = gc[:, m] if n_gate < DC else ga[:, m]
                        act.wait_ge(gate_pre, n_gate + 1)
                        A(dst, tmp[:, n_gate % 4], ACT.Sigmoid, bias=col("b_gate_2", n_gate)).then_inc(gate_ready, 1)
                        n_gate += 1
                if s in (S_CB, S_CB + 1):
                    for c in range(2 * (s - S_CB), 2 * (s - S_CB) + 2):
                        split_act(C_Z2 + c, z_hi[:, c], conv_u[:, c], 1.0)

            def exps(h):
                for i in range(TB):
                    act.wait_ge(s_max, h + 1)
                    part = probs[:, h % 2, QUERY_AT[i]:QUERY_AT[i] + P * (i + 1)]
                    k = 4 * (h % 2) + i
                    A(part, part, ACT.Exp, bias=small[:, 24 + k:25 + k], accum_out=small[:, 32 + k:33 + k]).then_inc(p_exp, 1)

            exps(0)
            split_w(S_OA2 + 1)
            for h in range(HEADS):
                act.wait_ge(pt_done, h + 1)
                if h >= 2:
                    act.wait_ge(pv2_done, h - 1)
                b = head_bank(h)
                A(probs_T[:, h % 2], psum[:, b:b + 3].rearrange("p b n -> p (b n)")[:, 0:CAUSAL], ACT.Copy).then_inc(pt_ready, 1)
                if h + 1 < HEADS:
                    exps(h + 1)
                if h >= 2 and h % 2 == 0:
                    c = (h - 2) // 2
                    act.wait_ge(pv2_done, 2 * c + 2)
                    A(act_hi[:, WC + c], psum[:, pair_bank(c)], ACT.Copy).then_inc(act_hi_ready, 1)
            act.wait_ge(pv2_done, HEADS)
            A(act_hi[:, DC - 1], psum[:, pair_bank(WC - 1)], ACT.Copy).then_inc(act_hi_ready, 1)
            act.wait_ge(gate_pre, 2 * DC)
            for m in (DC - 2, DC - 1):
                A(ga[:, m], ga[:, m], ACT.Sigmoid, bias=col("b_gate_2", DC + m)).then_inc(gate_ready, 1)
            for s in range(S_OA2, S_UP):
                split_w(s + 2)
                if s < S_O2:
                    for m in range(4 * (s - S_OA2), 4 * (s - S_OA2) + 4):
                        split_act(C_M2 + m, m_hi[:, m], gc[:, m], 1.0)
                else:
                    for c in range(2 * (s - S_O2), 2 * (s - S_O2) + 2):
                        split_act(C_UP2 + c, act_hi[:, c], xT[:, c], col("norm_ffn_g_2", c))
                        square(xT[:, c])
            root(N_FFN2, psum[:, bank_of(GROUP[S_UP]) + 3])
            nc.scalar.preload_act_table(ACT.Silu)
            with act.Fori(0, FFN_STEPS) as i:
                split_w(S_UP + 2, i)
                for j in range(2):
                    act.wait_ge(up_scaled, 4 * i + (j + 1))
                    A(tmp[:, 2 + j], tmp[:, j], ACT.Copy, scale=tap_col(2, 2 * i + j)).then_inc(up_tap, 1)
                for j in range(2):
                    act.wait_ge(up_conv, 4 * i + (j + 1))
                    A(tmp[:, 2 + j], tmp[:, 2 + j], ACT.Silu).then_inc(up_silu, 1)
                split_w(S_UP + 3, i)
                for j in range(2):
                    act.wait_ge(up_scaled, 4 * i + (j + 3))
                    A(tmp[:, j], tmp[:, 4 + j], ACT.Copy, scale=tap_col(2, 2 * i + (FC + j))).then_inc(up_tap, 1)
                for j in range(2):
                    act.wait_ge(up_hidden, 2 * i + (j + 1))
                    A(hid_hi[:, bass.ds(2 * i + j, 1)].rearrange("p a n -> p (a n)"), tmp[:, j], ACT.Copy).then_inc(hid_hi_ready, 1)
            for s in range(S_DOWN2, N_SLABS):
                split_w(s + 2)
                half = (s - S_DOWN2) // DOWN_SLABS
                if (s - S_DOWN2) % DOWN_SLABS == DOWN_SLABS - 1:
                    for b in range(TB):
                        n = TB * half + b
                        act.wait_ge(xn_sum, n + 1)
                        if n:
                            act.wait_ge(xn_sq, n)
                        A(junk[:, :], xnat[:, b, half * WIDTH:(half + 1) * WIDTH], ACT.Square,
                          accum_out=small[:, 8 + n:9 + n]).then_inc(xn_sq, 1)
            act.wait_ge(xn_mean, 1)
            A(small[:, 48:52], small[:, 48:52], ACT.Sqrt, bias=eps[:, 0:1], scale=1.0 / D).then_inc(xn_root, 1)

        @block.vector
        def _(dve):
            V = nc.vector
            steps = {"n": 0, "evicted": 0}

            def mark(ins):
                steps["n"] += 1
                ins.then_inc(dve_step, 1)

            def settle():
                if steps["n"]:
                    dve.wait_ge(dve_step, steps["n"])
                if steps["evicted"]:
                    dve.wait_ge(evicted, steps["evicted"])

            def free(ins):
                steps["evicted"] += 1
                ins.then_inc(evicted, 1)

            def split_w(s, i=None):
                if s >= N_SLABS:
                    return
                step = 0 if i is None else i
                n = SLABS[s][3] * SLABS[s][5] if i is None else SLAB
                dve.wait_ge(w_hi_ready, s + 1 + 2 * step)
                V.tensor_tensor(w_lo[:, s % 2, 0:n], raw[:, s % 2, 0:n], w_hi[:, s % 2, 0:n].bitcast(F32),
                                ALU.subtract).then_inc(w_lo_ready, 1)

            def split_act(q, hi, lo, src, gain=None):
                dve.wait_ge(act_hi_ready, q + 1)
                if gain is None:
                    ins = V.tensor_tensor(lo, src, hi.bitcast(F32), ALU.subtract)
                else:
                    ins = V.scalar_tensor_tensor(lo, src, gain, hi.bitcast(F32), ALU.mult, ALU.subtract)
                ins.then_inc(act_lo_ready, 1)

            def finished(s, i=None):
                dve.wait_ge(slab_done, s + 1 + (0 if i is None else 2 * i))

            def bank(s, m):
                return psum[:, bank_of(GROUP[s]) + m]

            def inverse(r):
                dve.wait_ge(root_done, TURN[r] + 1)
                f = rstd[:, RSTD_AT[r]]
                V.reciprocal(f, f).then_inc(rstd_ready, 1)
                dve.wait_ge(rstd_ready, TURN[r] + 1)

            def R(r):
                return rstd[:, RSTD_AT[r]]

            split_w(0)
            for c in range(DC):
                dve.wait_ge(x_turned, c + 1)
                V.tensor_copy(xT[:, c], psum[:, c]).then_inc(src_ready, 1)
                if c == 0:
                    dve.wait_ge(par_ready, 1)
                else:
                    split_act(C_MIX + c - 1, act_hi[:, c - 1], act_lo[:, c - 1], xT[:, c - 1], col("norm_mix", c - 1))
                if c == 5:
                    split_w(1)
            split_act(C_MIX + DC - 1, act_hi[:, DC - 1], act_lo[:, DC - 1], xT[:, DC - 1], col("norm_mix", DC - 1))
            mark(V.tensor_tensor(gain_both[:, :], par[:, AT["norm_final"]:AT["norm_final"] + DC],
                                 par[:, AT["norm_mix_g_2"]:AT["norm_mix_g_2"] + DC], ALU.mult))
            lam = par[:, AT["lru_lambda"]:AT["lru_lambda"] + WC]
            dve.wait_ge(lam_exp, 1)
            mark(V.tensor_scalar(small[:, 8:12], small[:, 4:8], 2.0, None, ALU.add))
            settle()
            mark(V.reciprocal(small[:, 8:12], small[:, 8:12]))
            settle()
            mark(V.tensor_tensor(small[:, 12:16], small[:, 8:12], small[:, 4:8], ALU.mult))
            settle()
            mark(V.tensor_tensor(small[:, 16:20], small[:, 12:16], small[:, 12:16], ALU.mult))
            settle()
            mark(V.tensor_scalar(small[:, 20:24], small[:, 16:20], 1.0 / 19, None, ALU.mult))
            for k in range(17, 1, -2):
                settle()
                mark(V.scalar_tensor_tensor(small[:, 20:24], small[:, 20:24], 1.0 / k, small[:, 16:20], ALU.add, ALU.mult))
            settle()
            mark(V.scalar_tensor_tensor(small[:, 20:24], small[:, 20:24], 1.0, small[:, 12:16], ALU.add, ALU.mult))
            mark(V.tensor_scalar(small[:, 24:28], lam, 0.0, -4.0, ALU.min, ALU.mult))
            settle()
            V.scalar_tensor_tensor(decay[:, :], small[:, 20:24], 8.0, small[:, 24:28], ALU.mult, ALU.add).then_inc(decay_ready, 1)

            def conv(c):
                mark(V.tensor_scalar(xc[:, c], lx[:, c], col("conv_w", 3 * WC + c), col("conv_b", c), ALU.mult, ALU.add))
                for d in range(1, 4):
                    settle()
                    ins = V.scalar_tensor_tensor(xc[:, c, d:], lx[:, c, 0:TOKENS - d], col("conv_w", (3 - d) * WC + c),
                                                 xc[:, c, d:], ALU.mult, ALU.add)
                    if d < 3:
                        mark(ins)
                    else:
                        ins.then_inc(conv_done, 1)

            def lru(c):
                k = c % 2
                dve.wait_ge(tanh_done, c + 1)
                mark(V.tensor_scalar(lru_rc[:, :], gate_t[:, k], 1.0, None, ALU.add))
                mark(V.tensor_tensor(gate_i[:, k], gate_i[:, k], xc[:, c], ALU.mult))
                settle()
                mark(V.reciprocal(lru_rc[:, :], lru_rc[:, :]))
                settle()
                mark(V.tensor_scalar(lru_a[:, :], lru_rc[:, :], 2.0, -1.0, ALU.mult, ALU.add))
                dve.wait_ge(root_t_done, c + 1)
                mark(V.scalar_tensor_tensor(root_t[:, k], root_t[:, k], 2.0, lru_rc[:, :], ALU.mult, ALU.mult))
                settle()
                mark(V.tensor_tensor(root_t[:, k], root_t[:, k], gate_i[:, k], ALU.mult))
                settle()
                mark(V.tensor_tensor_scan(lru_rc[:, :], lru_a[:, :], root_t[:, k], 0.0, ALU.mult, ALU.add))
                settle()
                dve.wait_ge(gelu_done, c + 1)
                V.tensor_tensor(lx[:, c], lru_rc[:, :], lg[:, c], ALU.mult).then_inc(src_ready, 1)
                dve.wait_ge(src_ready, C_LRU + c + 1)


            inverse(N_MIX)
            for s in range(S_LX, S_V):
                finished(s)
                for j in range(2):
                    c = 2 * (s % 2) + j
                    if s < S_LG:
                        ins = V.tensor_tensor(lx[:, c], bank(s, j), R(N_MIX), ALU.mult)
                    elif s < S_Q:
                        ins = V.tensor_tensor(lg[:, c], bank(s, j), R(N_MIX), ALU.mult)
                        ins.then_inc(lg_ready, 1)
                    elif s < S_K:
                        ins = V.scalar_tensor_tensor(qT[:, c], bank(s, j), SCALE, R(N_MIX), ALU.mult, ALU.mult)
                    else:
                        ins = V.tensor_tensor(kT[:, c], bank(s, j), R(N_MIX), ALU.mult)
                if not S_LG <= s < S_Q:
                    free(ins)
                split_w(s + 2)
                if s < S_LG:
                    settle()
                    conv(2 * s)
                    conv(2 * s + 1)
                if 3 <= s < 3 + WC:
                    lru(s - 3)
            dve.wait_ge(row_turned, 1)
            V.tensor_copy(small[:, 32:32 + TB], psum[:, 7, 0:TB]).then_inc(row_read, 1)
            dve.wait_ge(row_read, 1)
            finished(S_V)
            split_w(S_V + 2)

            def head_columns(h):
                b = head_bank(h)
                return psum[:, b:b + 3].rearrange("p b n -> p (b n)")[:, 0:CAUSAL]

            def log_part(h):
                dve.wait_ge(z_log, h + 1)
                if h >= 2:
                    dve.wait_ge(suffix_done, h - 1)
                V.scalar_tensor_tensor(soft[:, h % 2], head_columns(h), 0.0, stick[:, h % 2],
                                       ALU.max, ALU.add).then_inc(soft_ready, 1)

            def att_out(c):
                dve.wait_ge(pv_done, 2 * c + 2)
                V.tensor_copy(yatt[:, c], psum[:, pair_bank(c)]).then_inc(src_ready, 1)

            log_part(0)
            finished(S_V + 1)
            for b in range(TB):
                ins = V.tensor_scalar(v[:, b], bank(S_V + 1, b), small[:, 32 + b:33 + b], None, ALU.mult)
            free(ins)
            split_w(S_V + 3)
            for h in range(HEADS):
                if h + 1 < HEADS:
                    log_part(h + 1)
                if h == 0:
                    inverse(N_LRU)
                if h >= 2 and h % 2 == 0:
                    att_out((h - 2) // 2)
                if h < WC:
                    split_act(C_LRU + h, act_hi[:, h], act_lo[:, h], lx[:, h], col("norm_lru_out", h))
                if h >= 3 and h % 2:
                    c = (h - 3) // 2
                    split_act(C_ATT + c, act_hi[:, WC + c], act_lo[:, WC + c], yatt[:, c], col("norm_att_out", c))
            att_out(WC - 1)
            split_act(C_ATT + WC - 1, act_hi[:, DC - 1], act_lo[:, DC - 1], yatt[:, WC - 1], col("norm_att_out", WC - 1))
            for s in range(S_OUT_LRU, S_FFN):
                finished(s)
                if s == S_OUT_ATT:
                    inverse(N_ATT)
                r = N_LRU if s < S_OUT_ATT else N_ATT
                order = (1, 2, 3, 0) if s == S_OUT_LRU + 1 else (0, 1, 2, 3)

                def operand(m):
                    c = 4 * (s % 2) + m
                    split_act(C_FFN + c, act_hi[:, c], act_lo[:, c], xT[:, c], col("norm_ffn", c))

                for m in order:
                    c = 4 * (s % 2) + m
                    ins = V.tensor_tensor(tmp[:, m % 2], bank(s, m), R(r), ALU.mult)
                    free(ins) if m == order[-1] else mark(ins)
                    settle()
                    ins = V.tensor_tensor(xT[:, c], xT[:, c], tmp[:, m % 2], ALU.add)
                    if s >= S_OUT_ATT:
                        ins.then_inc(src_ready, 1)
                        dve.wait_ge(src_ready, src_count(C_FFN + c))
                        if m:
                            operand(m - 1)
                    else:
                        mark(ins)
                settle()
                split_w(s + 2)
                if s >= S_OUT_ATT:
                    operand(3)
            inverse(N_FFN)
            with dve.Fori(0, FFN_STEPS) as i:
                finished(S_FFN, i)
                for j in range(2):
                    V.tensor_tensor(tmp[:, j], bank(S_FFN, j), R(N_FFN), ALU.mult).then_inc(ffn_gate, 1)
                split_w(S_FFN + 2, i)
                finished(S_FFN + 1, i)
                for j in range(2):
                    V.tensor_tensor(tmp[:, 4 + j], bank(S_FFN + 1, j), R(N_FFN), ALU.mult).then_inc(ffn_up, 1)
                for j in range(2):
                    dve.wait_ge(ffn_up, 2 * i + (j + 1))
                    dve.wait_ge(ffn_silu, 2 * i + (j + 1))
                    V.tensor_tensor(tmp[:, 4 + j], tmp[:, 4 + j], tmp[:, 2 + j], ALU.mult).then_inc(ffn_hidden, 1)
                split_w(S_FFN + 3, i)
                for j in range(2):
                    dve.wait_ge(ffn_hidden, 2 * i + (j + 1))
                    dve.wait_ge(hid_hi_ready, 2 * i + (j + 1))
                    at = bass.ds(2 * i + j, 1)
                    V.tensor_tensor(hid_lo[:, at].rearrange("p a n -> p (a n)"), tmp[:, 4 + j],
                                    hid_hi[:, at].rearrange("p a n -> p (a n)").bitcast(F32),
                                    ALU.subtract).then_inc(hid_lo_ready, 1)
                dve.wait_ge(hid_lo_ready, 2 * i + 2)
            for s in range(S_DOWN, S_F2):
                finished(s)
                half = (s - S_DOWN) // DOWN_SLABS
                last = (s - S_DOWN) % DOWN_SLABS == DOWN_SLABS - 1
                if not last:
                    split_w(s + 2)
                    continue
                for m in range(4):
                    c = 4 * half + m
                    V.tensor_tensor(xT[:, c], bank(s, m), xT[:, c], ALU.add).then_inc(src_ready, 1)
                    dve.wait_ge(src_ready, src_count(C_MIX2 + c))
                    if m:
                        split_act(C_MIX2 + c - 1, act_hi[:, c - 1], act_lo[:, c - 1], xT[:, c - 1], gain_both[:, c - 1:c])
                split_w(s + 2)
                split_act(C_MIX2 + c, act_hi[:, c], act_lo[:, c], xT[:, c], gain_both[:, c:c + 1])
            dve.wait_ge(ssq_done, N_MIX2 + 1)
            mark(V.tensor_scalar(R(N_MIX2), bank(S_F2, 2), EPS, None, ALU.mult))
            settle()
            V.tensor_tensor(R(N_MIX2), bank(S_F2, 3), R(N_MIX2), ALU.add).then_inc(ms2_ready, 1)
            inverse(N_MIX2)
            both = R(N_MIX2)
            n_gate = 0
            for s in range(S_F2, S_OA2 - 1):
                finished(s)
                c0 = (s - S_K2) % 2 * 2 if s < S_V2 else (s - S_CC) % 2 * 2
                if s == S_F2:
                    free(V.tensor_tensor(fsum[:, 0], psum[0:HEADS, bank_of(GROUP[s])], rstd[0:HEADS, RSTD_AT[N_MIX2]], ALU.mult))
                    settle()
                    V.tensor_scalar(fsum[:, 0], fsum[:, 0], f_bias[:, 0:1], None, ALU.add).then_inc(f_pre, 1)
                elif s < S_V2:
                    for j in range(2):
                        if s < S_Q2:
                            ins = V.tensor_tensor(k2[:, c0 + j], bank(s, j), both, ALU.mult)
                        else:
                            ins = V.scalar_tensor_tensor(q2[:, c0 + j], bank(s, j), SCALE, both, ALU.mult, ALU.mult)
                    free(ins)
                elif s < S_CC:
                    if s > S_V2:
                        dve.wait_ge(row_turned, 2)
                        mark(V.tensor_copy(small[:, 52:52 + TB], psum[:, bank_of(GROUP[S_K2 + 1]) + 3, 0:TB]))
                        settle()
                        for b in range(TB):
                            ins = V.tensor_scalar(v2[:, b], bank(s, b), small[:, 52 + b:53 + b], None, ALU.mult)
                        free(ins)
                elif s < S_CIN:
                    for j in range(2):
                        ins = V.tensor_tensor(conv_p[:, c0 + j], bank(s, j), both, ALU.mult)
                    free(ins)
                elif s < S_GC:
                    for j in range(2):
                        ins = V.tensor_tensor(tmp[:, 4 + j], bank(s, j), both, ALU.mult)
                    free(ins)
                elif s < S_OC2 or s >= S_GA:
                    for j in range(2):
                        if n_gate >= 4:
                            dve.wait_ge(gate_ready, n_gate - 3)
                        V.tensor_tensor(tmp[:, n_gate % 4], bank(s, j), both, ALU.mult).then_inc(gate_pre, 1)
                        n_gate += 1
                else:
                    dve.wait_ge(gate_ready, DC)
                    for m in range(4):
                        c = 4 * (s - S_OC2) + m
                        ins = V.tensor_tensor(gc[:, c], bank(s, m), gc[:, c], ALU.mult)
                    free(ins)
                split_w(s + 2)
                if s == S_F2:
                    dve.wait_ge(f_ln, 1)
                    mark(V.scalar_tensor_tensor(fsum[:, 1], fsum[:, 0], 0.0, fsum[:, 1], ALU.min, ALU.subtract))
                    mark(V.memset(tmp[0:HEADS, 5], 1.0))
                    settle()
                    V.tensor_tensor_scan(fsum[:, 0], tmp[0:HEADS, 5], fsum[:, 1], 0.0, ALU.mult, ALU.subtract).then_inc(f_sum, 1)
                if s == S_K2:
                    inverse(N_FINAL)
                if S_K2 <= s < S_K2 + 4:
                    for c in (2 * (s - S_K2), 2 * (s - S_K2) + 1):
                        dve.wait_ge(sq_ready, SQ_DONE[N_MIX2])
                        mark(V.scalar_tensor_tensor(xT[:, c], xT[:, c], col("norm_final", c), R(N_FINAL), ALU.mult, ALU.mult))
                if S_CIN <= s < S_CB:
                    settle()
                    for j in range(2):
                        c = c0 + j
                        mark(V.tensor_tensor(conv_p[:, c], conv_p[:, c], tmp[:, 4 + j], ALU.mult))
                    settle()
                    for j in range(2):
                        c = c0 + j
                        mark(V.tensor_scalar(conv_u[:, c], conv_p[:, c], col("conv_mix_w_2", 2 * WC + c), None, ALU.mult))
                    for d in range(1, 3):
                        settle()
                        for j in range(2):
                            c = c0 + j
                            mark(V.scalar_tensor_tensor(conv_u[:, c, d:], conv_p[:, c, 0:TOKENS - d],
                                                        col("conv_mix_w_2", (2 - d) * WC + c), conv_u[:, c, d:],
                                                        ALU.mult, ALU.add))
                if S_CB <= s < S_GC:
                    settle()
                    for j in range(2):
                        c = c0 + j
                        V.tensor_tensor(conv_u[:, c], conv_u[:, c], tmp[:, 4 + j], ALU.mult).then_inc(src_ready, 1)
                    dve.wait_ge(src_ready, src_count(C_Z2 + c0 + 1))
                if S_CB < s <= S_CB + 2:
                    for c in range(2 * (s - S_CB - 1), 2 * (s - S_CB)):
                        split_act(C_Z2 + c, z_hi[:, c], z_lo[:, c], conv_u[:, c])

            def largest(h):
                dve.wait_ge(s_done, h + 1)
                dve.wait_ge(negf_ready, h + 1)
                if h >= 2:
                    dve.wait_ge(pt_done, h - 1)
                at = 16 + 4 * (h % 2)
                for i in range(TB):
                    w = P * (i + 1)
                    mark(V.tensor_tensor_reduce(out=probs[:, h % 2, QUERY_AT[i]:QUERY_AT[i] + w],
                                                in0=head_columns(h)[:, QUERY_AT[i]:QUERY_AT[i] + w], in1=neg_f[:, h, 0:w],
                                                scale=1.0, scalar=-3.0e38, op0=ALU.add, op1=ALU.max,
                                                accum_out=small[:, at + i:at + i + 1]))
                settle()
                V.tensor_scalar(small[:, at + 8:at + 12], small[:, at:at + 4], -1.0, None, ALU.mult).then_inc(s_max, 1)

            def normalise(h):
                dve.wait_ge(p_exp, 4 * h + 4)
                at = 32 + 4 * (h % 2)
                mark(V.reciprocal(small[:, at + 8:at + 12], small[:, at:at + 4]))
                settle()
                for i in range(TB):
                    part = probs[:, h % 2, QUERY_AT[i]:QUERY_AT[i] + P * (i + 1)]
                    ins = V.tensor_scalar(part, part, small[:, at + 8 + i:at + 9 + i], None, ALU.mult)
                ins.then_inc(p_ready2, 1)

            largest(0)
            normalise(0)
            finished(S_OA2 - 1)
            for j in range(2):
                V.tensor_tensor(ga[:, DC - 2 + j], bank(S_OA2 - 1, j), both, ALU.mult).then_inc(gate_pre, 1)
            split_w(S_OA2 + 1)
            for h in range(HEADS):
                if h + 1 < HEADS:
                    largest(h + 1)
                    normalise(h + 1)
                if h >= 2 and h % 2 == 0:
                    c = (h - 2) // 2
                    split_act(C_O2 + c, act_hi[:, WC + c], act_lo[:, WC + c], psum[:, pair_bank(c)])
            split_act(C_O2 + WC - 1, act_hi[:, DC - 1], act_lo[:, DC - 1], psum[:, pair_bank(WC - 1)])
            for s in range(S_OA2, S_O2):
                finished(s)
                if s > S_OA2:
                    dve.wait_ge(gate_ready, 2 * DC)
                for m in range(4):
                    ins = V.tensor_tensor(tmp[:, m], bank(s, m), ga[:, 4 * (s - S_OA2) + m], ALU.mult)
                free(ins)
                settle()
                for m in range(4):
                    c = 4 * (s - S_OA2) + m
                    V.tensor_tensor(gc[:, c], gc[:, c], tmp[:, m], ALU.add).then_inc(src_ready, 1)
                split_w(s + 2)
                for m in range(4):
                    c = 4 * (s - S_OA2) + m
                    dve.wait_ge(src_ready, src_count(C_M2 + c))
                    split_act(C_M2 + c, m_hi[:, c], m_lo[:, c], gc[:, c])
            for s in range(S_O2, S_UP):
                finished(s)
                for j in range(2):
                    c = 2 * (s - S_O2) + j
                    V.tensor_tensor(xT[:, c], bank(s, j), xT[:, c], ALU.add).then_inc(src_ready, 1)
                split_w(s + 2)
                dve.wait_ge(src_ready, src_count(C_UP2 + c))
                for c in (c - 1, c):
                    split_act(C_UP2 + c, act_hi[:, c], act_lo[:, c], xT[:, c], col("norm_ffn_g_2", c))
            inverse(N_FFN2)
            with dve.Fori(0, FFN_STEPS) as i:
                for side in range(2):
                    own, to = (0, 2) if side == 0 else (4, 0)
                    finished(S_UP + side, i)
                    for j in range(2):
                        V.tensor_tensor(tmp[:, own + j], bank(S_UP + side, j), R(N_FFN2), ALU.mult).then_inc(up_scaled, 1)
                    if side == 0:
                        split_w(S_UP + 2, i)
                    for j in range(2):
                        dve.wait_ge(up_scaled, 4 * i + (2 * side + j + 1))
                        dve.wait_ge(up_tap, 4 * i + (2 * side + j + 1))
                        V.scalar_tensor_tensor(tmp[:, to + j, 1:], tmp[:, own + j, 0:TOKENS - 1],
                                               tap_col(1, 2 * i + (side * FC + j)), tmp[:, to + j, 1:],
                                               ALU.mult, ALU.add).then_inc(up_mid, 1)
                    for j in range(2):
                        dve.wait_ge(up_mid, 4 * i + (2 * side + j + 1))
                        V.scalar_tensor_tensor(tmp[:, to + j, 2:], tmp[:, own + j, 0:TOKENS - 2],
                                               tap_col(0, 2 * i + (side * FC + j)), tmp[:, to + j, 2:],
                                               ALU.mult, ALU.add).then_inc(up_conv, 1)
                for j in range(2):
                    dve.wait_ge(up_conv, 4 * i + (j + 3))
                    dve.wait_ge(up_silu, 2 * i + (j + 1))
                    V.tensor_tensor(tmp[:, j], tmp[:, j], tmp[:, 2 + j], ALU.mult).then_inc(up_hidden, 1)
                split_w(S_UP + 3, i)
                for j in range(2):
                    dve.wait_ge(up_hidden, 2 * i + (j + 1))
                    dve.wait_ge(hid_hi_ready, 2 * i + (FC + j + 1))
                    at = bass.ds(2 * i + j, 1)
                    V.tensor_tensor(hid_lo[:, at].rearrange("p a n -> p (a n)"), tmp[:, j],
                                    hid_hi[:, at].rearrange("p a n -> p (a n)").bitcast(F32),
                                    ALU.subtract).then_inc(hid_lo_ready, 1)
                dve.wait_ge(hid_lo_ready, 2 * i + (FC + 2))
            for s in range(S_DOWN2, N_SLABS):
                finished(s)
                half = (s - S_DOWN2) // DOWN_SLABS
                if (s - S_DOWN2) % DOWN_SLABS == DOWN_SLABS - 1:
                    for b in range(TB):
                        part = xnat[:, b, half * WIDTH:(half + 1) * WIDTH]
                        V.tensor_tensor(part, bank(s, b), part, ALU.add).then_inc(xn_sum, 1)
                split_w(s + 2)
                if s in (S_DOWN2 + 1, S_DOWN2 + 3):
                    k = (s - S_DOWN2 - 1) // 2
                    dve.wait_ge(xn_turned, k + 1)
                    V.tensor_copy(xnat[:, 2 * k:2 * k + 2].rearrange("p b d -> p (b d)"),
                                  psum[:, 0:4].rearrange("p b n -> p (b n)")).then_inc(xn_ready, 1)
                    dve.wait_ge(xn_ready, k + 1)
            dve.wait_ge(xn_sq, 2 * TB)
            V.tensor_tensor(small[:, 48:52], small[:, 8:8 + TB], small[:, 8 + TB:8 + 2 * TB], ALU.add).then_inc(xn_mean, 1)
            dve.wait_ge(xn_root, 1)
            mark(V.reciprocal(small[:, 52:56], small[:, 48:52]))
            settle()
            dve.wait_ge(gain_in, 16)
            dve.wait_ge(xn_sum, 2 * TB)
            for b in range(TB):
                V.scalar_tensor_tensor(xnat[:, b], xnat[:, b], small[:, 52 + b:53 + b], gain_out[:, :],
                                       ALU.mult, ALU.mult).then_inc(xn_out, 1)

        @block.tensor
        def _(pe):
            mm = nc.tensor.matmul
            sems = {"evicted": evicted, "lg_ready": lg_ready, "ffn_gate": ffn_gate, "ffn_up": ffn_up, 
                    "gate_pre": gate_pre, "src_ready": src_ready, "up_scaled": up_scaled, "xn_sum": xn_sum}

            def wait_freed(g, more=0):
                name, count = freed(g)
                pe.wait_ge(sems[name], count + more)

            def wait_banks(g):
                for k in (g - 1, g - 2):
                    if k >= 0 and bank_of(k) == bank_of(g):
                        wait_freed(k)
                        break

            def wait_w(s, i=None):
                pe.wait_ge(w_lo_ready, s + 1 + (0 if i is None else 2 * i))

            def product(dst, stationary, moving, first, last):
                mm(dst, stationary[0], moving[0], start=first, stop=False)
                mm(dst, stationary[0], moving[1], start=False, stop=False)
                return mm(dst, stationary[1], moving[0], start=False, stop=last)

            def w_part(s, k, c0, n):
                at = k * SLABS[s][5] + c0
                return w_hi[:, s % 2, at:at + n], w_lo[:, s % 2, at:at + n]

            def act_part(chunk, t0=0, n=TOKENS):
                return act_hi[:, chunk, t0:t0 + n], act_lo[:, chunk, t0:t0 + n]

            def slab_a(s, q=None, i=None, part=act_part):
                wait_w(s, i)
                b = bank_of(GROUP[s])
                for k in range(DC):
                    if q is not None:
                        pe.wait_ge(act_lo_ready, q + k + 1)
                    for j in range(SLABS[s][5] // P):
                        ins = product(psum[:, b + j], w_part(s, k, j * P, P), part(k), k == 0, k == DC - 1)
                ins.then_inc(slab_done, 1)

            def slab_b(s, part, q=None, order=(0, 1, 2, 3), before_last=None):
                wait_w(s)
                wait_banks(GROUP[s])
                b = bank_of(GROUP[s])
                if q is not None:
                    pe.wait_ge(act_lo_ready, q + WC)
                for m in order:
                    if m == order[-1] and before_last is not None:
                        before_last()
                    for k in range(WC):
                        ins = product(psum[:, b + m], w_part(s, k, m * P, P), part(k), k == 0, k == WC - 1)
                ins.then_inc(slab_done, 1)

            def slab_v(s, part):
                wait_w(s)
                if part == 0:
                    wait_banks(GROUP[s])
                b = bank_of(GROUP[s])
                for k in range(ROWS_B):
                    for tb in range(TB):
                        ins = product(psum[:, b + tb], act_part(ROWS_B * part + k, tb * P, P), w_part(s, k, 0, WIDTH),
                                      part == 0 and k == 0, part == 1 and k == ROWS_B - 1)
                ins.then_inc(slab_done, 1)

            def sum_squares(r, bank):
                pe.wait_ge(sq_summed, SQ_DONE[r])
                mm(psum[:, bank], ones[:], acc[:, r % 2], start=True, stop=True).then_inc(ssq_done, 1)

            def turn_row(row, bank):
                for tb in range(TB):
                    ins = mm(psum[:, bank, tb:tb + 1], row[:, tb * P:(tb + 1) * P], ident[:, 0:1],
                             start=tb == 0, stop=True, skip_group_check=True)
                ins.then_inc(row_turned, 1)

            def turn_x_in(tb, c):
                return nc.tensor.transpose(psum[:, c, tb * P:(tb + 1) * P], xin[:, tb, c * P:(c + 1) * P], ident[:])

            pe.wait_ge(ident_set, 1)
            for tb in range(TB - 1):
                pe.wait_ge(x_in[tb], 16)
                for c in range(DC - 1):
                    turn_x_in(tb, c)
            pe.wait_ge(row_in, 16 * (len(ROWS) + 3))
            nc.tensor.transpose(psum[:, 7, 0:NROWS], rows[:, :], ident[0:NROWS, 0:NROWS])
            for j in range(2):
                ins = nc.tensor.transpose(psum[:, 7, NROWS + j * TAP_ROWS:NROWS + (j + 1) * TAP_ROWS], tap_rows[:, j],
                                          ident[0:TAP_ROWS, 0:TAP_ROWS])
            ins.then_inc(par_done, 1)
            pe.wait_ge(x_in[TB - 1], 16)
            for c in range(DC - 1):
                turn_x_in(TB - 1, c).then_inc(x_turned, 1)
            pe.wait_ge(par_ready, 1)
            for tb in range(TB):
                ins = turn_x_in(tb, DC - 1)
            ins.then_inc(x_turned, 1)
            for s in range(S_V):
                if s == 0:
                    pe.wait_ge(src_ready, 2)
                    pe.wait_ge(const_bf, 3)
                if s == S_Q:
                    pe.wait_ge(evicted, 2)
                wait_banks(GROUP[s])
                slab_a(s, q=C_MIX if s == 0 else None)
                if s == 0:
                    sum_squares(N_MIX, bank_of(0) + 3)
                if 2 <= s < 2 + WC:
                    c = s - 2
                    if c == 0:
                        pe.wait_ge(bd_in, 64)
                    if c >= 2:
                        pe.wait_ge(gate_read, c - 1)
                    pe.wait_ge(conv_done, c + 1)
                    b = bank_of(GROUP[s])
                    mm(psum[:, b + 2], gate_bd[:, 0, c], xc[:, c], start=True, stop=True)
                    mm(psum[:, b + 3], gate_bd[:, 1, c], xc[:, c], start=True, stop=True).then_inc(gates_done, 1)

            def columns(h, at, n):
                return psum[:, head_bank(h) + at // TOKENS, at % TOKENS:at % TOKENS + n]

            def head_rows(x, h, t0, n):
                p = HD * (h % 2)
                return x[p:p + HD, h // 2, t0:t0 + n]

            def values(h, weights, v_rows):
                p = HD * (h % 2)
                for kb in range(TB):
                    n = TOKENS - kb * P
                    ins = mm(psum[p:p + HD, pair_bank(h // 2), kb * P:TOKENS], v_rows[:, kb, h * HD:(h + 1) * HD],
                             weights[:, h % 2, KEY_AT[kb]:KEY_AT[kb] + n], start=kb == 0, stop=kb == TB - 1,
                             skip_group_check=True)
                return ins

            def scores_kq(h):
                if h >= 2:
                    pe.wait_ge(att_ready, h - 1)
                for kb in (0, 1, 3, 2):
                    n = TOKENS - kb * P
                    dst = columns(h, KEY_AT[kb], n)
                    mm(dst, head_rows(kT, h, kb * P, P), head_rows(qT, h, kb * P, n), start=kb != 3, stop=False,
                       skip_group_check=True)
                    ins = mm(dst[:, 0:P], ident_bf[:], mask_kq[:], start=False, stop=True, skip_group_check=True)
                ins.then_inc(z_done, 1)

            def suffix(h):
                pe.wait_ge(soft_ready, h + 1)
                for kb in (0, 1, 3, 2):
                    for jb in range(kb, TB):
                        n = TOKENS - jb * P
                        ins = mm(columns(h, KEY_AT[kb] + (jb - kb) * P, n), neg_tri[:] if jb == kb else neg_ones[:],
                                 soft[:, h % 2, KEY_AT[jb]:KEY_AT[jb] + n], start=False, stop=True, skip_group_check=True)
                ins.then_inc(suffix_done, 1)

            def values_kq(h):
                pe.wait_ge(att_ready, h + 1)
                if h >= 4 and h % 2 == 0:
                    pe.wait_ge(src_ready, C_ATT + h // 2 - 1)
                values(h, att, v).then_inc(pv_done, 1)

            pe.wait_ge(gate_read, WC)
            turn_row(rstd[:, 0], 7)
            slab_v(S_V, 0)
            wait_freed(GROUP[S_V] - 1)
            sum_squares(N_LRU, 4)
            pe.wait_ge(row_read, 1)
            scores_kq(0)
            slab_v(S_V + 1, 1)
            wait_freed(GROUP[S_V])
            pe.wait_ge(root_done, N_LRU + 1)
            for h in range(HEADS):
                if h + 1 < HEADS:
                    scores_kq(h + 1)
                suffix(h)
                if h:
                    values_kq(h - 1)
            pe.wait_ge(att_ready, HEADS)
            values_kq(HEADS - 1)
            slab_b(S_OUT_LRU, act_part, q=C_LRU)
            pe.wait_ge(src_ready, C_ATT + WC)
            sum_squares(N_ATT, 0)
            slab_b(S_OUT_LRU + 1, act_part, order=(1, 2, 3, 0), before_last=lambda: pe.wait_ge(root_done, N_ATT + 1))
            slab_b(S_OUT_ATT, lambda k: act_part(WC + k), q=C_ATT)
            slab_b(S_OUT_ATT + 1, lambda k: act_part(WC + k))


            def up_and_down(s0, s_down, q, r, transposed, hid0, between):
                wait_banks(GROUP[s0])
                slab_a(s0, q=q)
                sum_squares(r, bank_of(GROUP[s0]) + 3)
                wait_banks(GROUP[s0 + 1])
                slab_a(s0 + 1)
                with pe.Fori(1, FFN_STEPS) as i:
                    for j in range(2):
                        name, _ = freed(GROUP[s0 + j])
                        per = freed(GROUP[s0 + 2 + j])[1] - freed(GROUP[s0 + j])[1]
                        pe.wait_ge(sems[name], i * per + (freed(GROUP[s0 + j])[1] - per))
                        slab_a(s0 + j, i=i)
                for s in range(s_down, s_down + 2 * DOWN_SLABS):
                    half, part = (s - s_down) // DOWN_SLABS, (s - s_down) % DOWN_SLABS
                    wait_w(s)
                    if part == 0:
                        wait_banks(GROUP[s])
                    b = bank_of(GROUP[s])
                    for k in range(SLABS[s][3]):
                        n = SLABS[s][2] + k
                        if half == 0:
                            pe.wait_ge(hid_lo_ready, hid0 + n + 1)
                        for m in range(4):
                            if transposed:
                                ins = product(psum[:, b + m], w_part(s, k, m * P, P), (hid_hi[:, n], hid_lo[:, n]),
                                              n == 0, n == FC - 1)
                            else:
                                ins = product(psum[:, b + m], (hid_hi[:, n, m * P:(m + 1) * P], hid_lo[:, n, m * P:(m + 1) * P]),
                                              w_part(s, k, 0, WIDTH), n == 0, n == FC - 1)
                    ins.then_inc(slab_done, 1)
                    between(s)

            up_and_down(S_FFN, S_DOWN, C_FFN, N_FFN, True, 0, lambda s: None)
            wait_banks(GROUP[S_F2])
            slab_a(S_F2, q=C_MIX2)
            sum_squares(N_FINAL, bank_of(GROUP[S_F2]) + 2)
            sum_squares(N_MIX2, bank_of(GROUP[S_F2]) + 3)
            for s in list(range(S_K2, S_V2)) + list(range(S_CC, S_OA2 - 1)):
                if s == S_OC2:
                    pe.wait_ge(negf_ready, HEADS)
                if S_OC2 <= s < S_GA:
                    slab_b(s, lambda k: (z_hi[:, k], z_lo[:, k]), q=C_Z2)
                    continue
                wait_banks(GROUP[s])
                slab_a(s)
                if s == S_K2 + 1:
                    pe.wait_ge(rstd_ready, TURN[N_MIX2] + 1)
                    turn_row(rstd[:, RSTD_AT[N_MIX2]], bank_of(GROUP[s]) + 3)
                if s == S_V2 - 1:
                    pe.wait_ge(row_turned, 2)
                    slab_v(S_V2, 0)
                    slab_v(S_V2 + 1, 1)
                if S_CC <= s < S_CC + HEADS:
                    h = s - S_CC
                    pe.wait_ge(f_sum, 1)
                    if h == 0:
                        wait_freed(GROUP[S_V2])
                    if h >= 2:
                        pe.wait_ge(negf_ready, h - 1)
                    mm(psum[:, bank_of(GROUP[s]) + 3], ident[0:HEADS, h:h + 1].broadcast_to([HEADS, P]), fsum[:, 0], start=True, stop=True).then_inc(negf_done, 1)

            def scores_qk(h):
                if h >= 2:
                    pe.wait_ge(pt_ready, h - 1)
                for i in (3, 2, 0, 1):
                    n = P * (i + 1)
                    dst = columns(h, QUERY_AT[i], n)
                    mm(dst, head_rows(q2, h, i * P, P), head_rows(k2, h, 0, n), start=i != 0, stop=False,
                       skip_group_check=True)
                    ins = mm(dst[:, i * P:n], ident_bf[:], mask_qk[:], start=False, stop=True, skip_group_check=True)
                ins.then_inc(s_done, 1)

            def turn_probs(h):
                pe.wait_ge(p_ready2, h + 1)
                for kb in range(TB):
                    for i in range(kb, TB):
                        ins = nc.tensor.transpose(columns(h, KEY_AT[kb] + (i - kb) * P, P),
                                                  probs[:, h % 2, QUERY_AT[i] + kb * P:QUERY_AT[i] + (kb + 1) * P], ident[:])
                ins.then_inc(pt_done, 1)

            def values_qk(h):
                pe.wait_ge(pt_ready, h + 1)
                if h >= 4 and h % 2 == 0:
                    pe.wait_ge(act_lo_ready, C_O2 + h // 2 - 1)
                values(h, probs_T, v2).then_inc(pv2_done, 1)

            s = S_OA2 - 1
            wait_w(s)
            wait_banks(GROUP[s])
            for j in range(2):
                for k in range(DC):
                    if j == 0 and k == WC:
                        wait_freed(GROUP[s - 1])
                        scores_qk(0)
                    ins = product(psum[:, bank_of(GROUP[s]) + j], w_part(s, k, j * P, P), act_part(k), k == 0, k == DC - 1)
            ins.then_inc(slab_done, 1)
            for h in range(HEADS):
                if h + 1 < HEADS:
                    scores_qk(h + 1)
                if h == HEADS - 1:
                    values_qk(h - 1)
                    wait_w(S_OA2)
                    pe.wait_ge(act_lo_ready, C_O2 + WC - 1)
                    for m in range(1, 4):
                        for k in range(WC - 1):
                            product(psum[:, bank_of(GROUP[S_OA2]) + m], w_part(S_OA2, k, m * P, P), act_part(WC + k), k == 0, False)
                turn_probs(h)
                if h == 0:
                    wait_freed(GROUP[S_OA2 - 1])
                if 0 < h < HEADS - 1:
                    values_qk(h - 1)
            values_qk(HEADS - 1)
            pe.wait_ge(act_lo_ready, C_O2 + WC)
            for m in range(4):
                for k in range(WC - 1 if m else 0, WC):
                    ins = product(psum[:, bank_of(GROUP[S_OA2]) + m], w_part(S_OA2, k, m * P, P), act_part(WC + k), k == 0, k == WC - 1)
            ins.then_inc(slab_done, 1)
            slab_b(S_OA2 + 1, lambda k: act_part(WC + k))
            for s in range(S_O2, S_UP):
                wait_banks(GROUP[s])
                slab_a(s, q=C_M2 if s == S_O2 else None, part=lambda k: (m_hi[:, k], m_lo[:, k]))

            def turn_x(s):
                if s not in (S_DOWN2 + 1, S_DOWN2 + 3):
                    return
                k = (s - S_DOWN2 - 1) // 2
                if k == 0:
                    wait_freed(GROUP[S_DOWN2 - 1])
                else:
                    pe.wait_ge(xn_ready, 1)
                for tb in range(2):
                    for c in range(DC):
                        ins = nc.tensor.transpose(psum[:, 2 * tb + c // 4, (c % 4) * P:(c % 4 + 1) * P],
                                                  xT[:, c, (2 * k + tb) * P:(2 * k + tb + 1) * P], ident[:])
                ins.then_inc(xn_turned, 1)

            assert bank_of(GROUP[S_DOWN2]) == 4
            up_and_down(S_UP, S_DOWN2, C_UP2, N_FFN2, False, FC, turn_x)


NAMES = ["x", "norm_mix", "w_in", "conv_w", "conv_b", "w_rg", "b_rg", "w_ig", "b_ig", "lru_lambda", "norm_lru_out",
         "norm_att_out", "w_out", "norm_ffn", "w_ffn_in", "w_ffn_out", "norm_final", "norm_mix_g_2", "w_in_2", "b_f_2",
         "b_gate_2", "conv_mix_w_2", "w_out_conv_2", "w_out_attn_2", "w_o_2", "norm_ffn_g_2", "w_up_2",
         "conv_ffn_w_2", "w_down_2", "norm_f_g_2"]


def kernel(**inputs):
    import numpy as np
    import concourse.bacc as bacc
    from concourse.bass_utils import run_bass_kernel_spmd

    nc = bacc.Bacc("TRN2", target_bir_lowering=False, num_devices=1)
    arrays, tensors = {}, {}
    for name in NAMES:
        a = np.ascontiguousarray(inputs[name])
        arrays[f"in_{name}"] = a
        tensors[name] = nc.dram_tensor(f"in_{name}", a.shape, mybir.dt.from_np(a.dtype), kind="ExternalInput").ap()
    out = nc.dram_tensor("out", (1, TOKENS, D), F32, kind="ExternalOutput").ap()
    two_blocks(nc, tensors, out)
    r = run_bass_kernel_spmd(nc, [arrays], core_ids=[0])
    return r.results[0]["out"]
```

```python
from contextlib import ExitStack

import concourse.bass as bass
from concourse import mybir

F32 = mybir.dt.float32
F32R = mybir.dt.float32r
BF16 = mybir.dt.bfloat16
ALU = mybir.AluOpType
ACT = mybir.ActivationFunctionType

P = 128
TOKENS = 512
D = 1024
DC = D // P
TB = TOKENS // P
WIDTH = 512
WC = WIDTH // P
HEADS = 8
HD = WIDTH // HEADS
FF = 2816
FC = FF // P
EPS = 1e-6
SCALE = HD ** -0.5
MASKED = -1e30
SLAB = 2048
COLS_A = SLAB // DC
ROWS_B = SLAB // WIDTH
FFN_STEPS = FF // COLS_A
CAUSAL = sum(TOKENS - P * b for b in range(TB))
KEY_AT = [512, 128, 1024, 0]
QUERY_AT = [896, 1024, 512, 0]
QUERY_ORDER = [3, 2, 0, 1]

ROWS = [("norm_mix", 8), ("norm_ffn", 8), ("norm_final", 8), ("conv_w", 16), ("conv_b", 4), ("b_rg", 4),
        ("b_ig", 4), ("lru_lambda", 4), ("norm_lru_out", 4), ("norm_att_out", 4), ("norm_mix_g_2", 8),
        ("b_gate_2", 16), ("conv_mix_w_2", 12), ("norm_ffn_g_2", 8)]
AT = {}
_n = 0
FIRST_ROWS = ROWS[0][1]
for _name, _rows in ROWS:
    AT[_name] = _n
    _n += _rows
NROWS = _n
LRU_HEAD = 0
EARLY, EARLY_HEAD = 2, 3
TAP_ROWS = 3 * 2 * FC // 2

SLABS = []


def _add(w, kind, k0, nk, c0, nc_):
    SLABS.append((w, kind, k0, nk, c0, nc_))
    return len(SLABS) - 1


def _cols_a(w, c0, n):
    first = len(SLABS)
    for j in range(n // COLS_A):
        _add(w, "A", 0, DC, c0 + j * COLS_A, COLS_A)
    return first


def _down(w):
    first = len(SLABS)
    for half in range(2):
        for k0 in range(0, FC, ROWS_B):
            _add(w, "B", k0, min(ROWS_B, FC - k0), half * WIDTH, WIDTH)
    return first


S_LX = _cols_a("w_in", 0, WIDTH)
S_LG = _cols_a("w_in", WIDTH, WIDTH)
S_Q = _cols_a("w_in", 2 * WIDTH, WIDTH)
S_K = _cols_a("w_in", 3 * WIDTH, WIDTH)
S_V = _add("w_in", "B", 0, ROWS_B, 4 * WIDTH, WIDTH)
_add("w_in", "B", ROWS_B, ROWS_B, 4 * WIDTH, WIDTH)
S_OUT_LRU = _add("w_out", "B", 0, WC, 0, WIDTH)
_add("w_out", "B", 0, WC, WIDTH, WIDTH)
S_OUT_ATT = _add("w_out", "B", WC, WC, 0, WIDTH)
_add("w_out", "B", WC, WC, WIDTH, WIDTH)
S_FFN = len(SLABS)
for _i in range(FFN_STEPS):
    _add("w_ffn_in", "A", 0, DC, _i * COLS_A, COLS_A)
    _add("w_ffn_in", "A", 0, DC, FF + _i * COLS_A, COLS_A)
S_DOWN = _down("w_ffn_out")
F_AT = 6 * WIDTH
S_K2 = _cols_a("w_in_2", 4 * WIDTH, WIDTH)
S_Q2 = _cols_a("w_in_2", 3 * WIDTH, WIDTH)
S_F2 = _add("w_in_2", "A", 0, DC, F_AT, P)
S_V2 = _add("w_in_2", "B", 0, ROWS_B, 5 * WIDTH, WIDTH)
_add("w_in_2", "B", ROWS_B, ROWS_B, 5 * WIDTH, WIDTH)
S_CC = _cols_a("w_in_2", WIDTH, WIDTH)
S_CIN = _cols_a("w_in_2", 2 * WIDTH, WIDTH)
S_CB = _cols_a("w_in_2", 0, WIDTH)
S_GC = _cols_a("w_in_2", F_AT + HEADS, D)
S_OC2 = _add("w_out_conv_2", "B", 0, WC, 0, WIDTH)
_add("w_out_conv_2", "B", 0, WC, WIDTH, WIDTH)
S_GA = _cols_a("w_in_2", F_AT + HEADS + D, D)
S_OA2 = _add("w_out_attn_2", "B", 0, WC, 0, WIDTH)
_add("w_out_attn_2", "B", 0, WC, WIDTH, WIDTH)
S_O2 = _cols_a("w_o_2", 0, D)
S_UP = len(SLABS)
for _i in range(FFN_STEPS):
    _add("w_up_2", "A", 0, DC, _i * COLS_A, COLS_A)
    _add("w_up_2", "A", 0, DC, FF + _i * COLS_A, COLS_A)
S_DOWN2 = _down("w_down_2")
N_SLABS = len(SLABS)
DOWN_SLABS = (N_SLABS - S_DOWN2) // 2

GROUP = []
_g = -1
for _s in range(N_SLABS):
    _inner = (_s in (S_V + 1, S_V2 + 1)
              or any(f <= _s < f + 2 * DOWN_SLABS and (_s - f) % DOWN_SLABS for f in (S_DOWN, S_DOWN2)))
    _g += not _inner
    GROUP.append(_g)


def src_count(q):
    return q + 1 - (WC if q >= C_M2 else 0)


def bank_of(g):
    return 4 * (g % 2)


def head_bank(h):
    return 5 - 3 * (h % 2)


def pair_bank(c):
    return c % 2


def early_part(h):
    return ((h - EARLY_HEAD) // 2, 2 * ((h - EARLY_HEAD) % 2)) if EARLY_HEAD <= h < EARLY_HEAD + 2 * EARLY else None


def _shares_count(g):
    s = GROUP.index(g)
    return s < S_LG or S_Q <= s < S_FFN or S_K2 <= s < S_GC or S_OC2 <= s < S_GA or S_OA2 <= s < S_O2


EVICTED_BEFORE = [sum(_shares_count(k) for k in range(g)) for g in range(GROUP[-1] + 1)]


def freed(g):
    s = GROUP.index(g)
    if S_LG <= s < S_Q:
        return "lg_ready", 2 * (s - S_LG + 1)
    if S_FFN <= s < S_DOWN:
        return ("ffn_up" if (s - S_FFN) % 2 else "ffn_gate"), 2 * ((s - S_FFN) // 2 + 1)
    if S_DOWN <= s < S_K2:
        return "src_ready", src_count(C_MIX2 + WC * ((s - S_DOWN) // DOWN_SLABS + 1) - 1)
    if S_GC <= s < S_OC2:
        return "gate_pre", 2 * (s - S_GC + 1)
    if S_GA <= s < S_OA2:
        return "gate_pre", DC + 2 * (s - S_GA + 1)
    if S_O2 <= s < S_UP:
        return "src_ready", src_count(C_UP2 + 2 * (s - S_O2) + 1)
    if S_UP <= s < S_DOWN2:
        return "up_scaled", 2 * (s - S_UP + 1)
    if S_DOWN2 <= s:
        return "xn_sum", TB * ((s - S_DOWN2) // DOWN_SLABS + 1)
    return "evicted", 1 + EVICTED_BEFORE[g]


C_MIX, C_LRU, C_ATT, C_FFN, C_MIX2, C_Z2, C_O2, C_M2, C_UP2 = 0, 8, 12, 16, 24, 32, 36, 40, 48
N_MIX, N_LRU, N_ATT, N_FFN, N_FINAL, N_MIX2, N_FFN2 = range(7)
SQ_FIRST = [0, 8, 12, 16, 24, 25, 40]
SQ_DONE = [8, 12, 16, 24, 39, 40, 48]
RSTD_AT = [0, 1, 2, 0, 1, 2, 0]
TURN = [0, 1, 2, 3, 5, 4, 6]


def two_blocks(nc, t, out):
    with ExitStack() as ctx:
        def sb(name, shape, dt=F32, where=None):
            return (where or ctx).enter_context(nc.sbuf_tensor(name, shape, dt))

        def sem(name):
            return ctx.enter_context(nc.semaphore(name))

        xT = sb("xT", [P, DC, TOKENS])
        raw = sb("raw", [P, 2, SLAB])
        w_hi = sb("w_hi", [P, 2, SLAB], F32R)
        w_lo = sb("w_lo", [P, 2, SLAB], F32R)
        tmp = sb("tmp", [P, 6, TOKENS])
        rstd = sb("rstd", [P, 3, TOKENS])
        acc = tmp[:, 2:4]
        sq = tmp[:, 4:6]
        par = sb("par", [P, NROWS + 2 * TAP_ROWS])
        ident = sb("ident", [P, P])
        ones = sb("ones", [P, P])
        neg_ones = sb("neg_ones", [P, P], F32R)
        neg_tri = sb("neg_tri", [P, P], F32R)
        ident_bf = sb("ident_bf", [P, P], BF16)
        mask_kq = sb("mask_kq", [P, P], BF16)
        mask_qk = sb("mask_qk", [P, P], BF16)
        small = sb("small", [P, 64])
        decay = sb("decay", [P, WC])
        f_bias = sb("f_bias", [HEADS, 1])
        eps = sb("eps", [P, 2])
        ident_r = sb("ident_r", [HEADS, HEADS], F32R)
        gain_both = sb("gain_both", [P, DC])
        act_scope = ExitStack()
        act_hi = sb("act_hi", [P, DC, TOKENS], F32R, act_scope)
        act_lo = sb("act_lo", [P, DC, TOKENS], F32R, act_scope)
        scope = ExitStack()
        hid_hi = sb("hid_hi", [P, FC, TOKENS], F32R, scope)
        hid_lo = sb("hid_lo", [P, FC, TOKENS], F32R, scope)
        scope.close()
        lx = sb("lx", [P, WC, TOKENS], F32, scope)
        inner = ExitStack()
        soft_hi = sb("soft_hi", [P, 2, CAUSAL], F32R, inner)
        inner.close()
        lg = sb("lg", [P, WC, TOKENS], F32, scope)
        xc = sb("xc", [P, WC, TOKENS], F32, scope)
        xin = sb("xin", [P, TB, D], F32, inner)
        first_rows = sb("first_rows", [FIRST_ROWS, P], F32, inner)
        rows = sb("rows", [NROWS - FIRST_ROWS, P], F32, inner)
        tap_rows = sb("tap_rows", [TAP_ROWS, 2, P], F32, inner)
        inner.close()
        qT = sb("qT", [P, WC, TOKENS], F32, scope)
        kT = sb("kT", [P, WC, TOKENS], F32, scope)
        v = sb("v", [P, TB, WIDTH], F32, scope)
        yatt = sb("yatt", [P, WC, TOKENS], F32, scope)
        gate_bd = sb("gate_bd", [P, 2, WC, P], F32, inner)
        gate_t = sb("gate_t", [P, 2, TOKENS], F32, inner)
        gate_i = sb("gate_i", [P, 2, TOKENS], F32, inner)
        root_t = sb("root_t", [P, 2, TOKENS], F32, inner)
        lru_rc = sb("lru_rc", [P, TOKENS], F32, inner)
        lru_a = sb("lru_a", [P, TOKENS], F32, inner)
        inner.close()
        stick = sb("stick", [P, 2, CAUSAL], F32, inner)
        soft = sb("soft", [P, 2, CAUSAL], F32, inner)
        att = sb("att", [P, 2, CAUSAL], F32, inner)
        inner.close()
        sb("stick_place", [P, 2, CAUSAL], F32, inner)
        soft_lo = sb("soft_lo", [P, 2, CAUSAL], F32R, inner)
        inner.close()
        scope.close()
        m_hi = sb("m_hi", [P, DC, TOKENS], F32R, inner)
        inner.close()
        q2 = sb("q2", [P, WC, TOKENS], F32, scope)
        k2 = sb("k2", [P, WC, TOKENS], F32, scope)
        v2 = sb("v2", [P, TB, WIDTH], F32, scope)
        gc = sb("gc", [P, DC, TOKENS], F32, scope)
        fsum = sb("fsum", [HEADS, 2, TOKENS], F32, inner)
        f_split = sb("f_split", [HEADS, 2, TOKENS], F32R, inner)
        inner.close()
        ga = sb("ga", [P, DC, TOKENS], F32, scope)
        m_lo = sb("m_lo", [P, DC, TOKENS], F32R, inner)
        inner.close()
        neg_f = sb("neg_f", [P, HEADS, TOKENS], F32, scope)
        conv_p = sb("conv_p", [P, WC, TOKENS], F32, inner)
        conv_u = sb("conv_u", [P, WC, TOKENS], F32, inner)
        inner.close()
        z_hi = sb("z_hi", [P, WC, TOKENS], F32R, inner)
        z_lo = sb("z_lo", [P, WC, TOKENS], F32R, inner)
        inner.close()
        probs = sb("probs", [P, 2, CAUSAL], F32, inner)
        probs_T = tmp[:, 0:5].rearrange("p a n -> p (a n)").rearrange("p (a n) -> p a n", a=2)
        inner.close()
        scope.close()
        act_scope.close()
        xnat = sb("xnat", [P, TB, D], F32, act_scope)
        gain_out = sb("gain_out", [P, D], F32, act_scope)
        junk = sb("junk", [P, WIDTH], F32, act_scope)
        act_scope.close()

        psum = ctx.enter_context(nc.psum_tensor("psum", [P, 8, TOKENS], F32))

        x_in = [sem(f"x_in{b}") for b in range(TB)]
        first_in, row_in = sem("first_in"), sem("row_in")
        bd_in, gain_in = sem("bd_in"), sem("gain_in")
        raw_in = [sem("raw_in0"), sem("raw_in1")]
        ident_zeroed, ident_set, const_set = sem("ident_zeroed"), sem("ident_set"), sem("const_set")
        bd_zeroed = sem("bd_zeroed")
        const_bf = sem("const_bf")
        row_read = sem("row_read")
        par_done, par_ready = sem("par_done"), sem("par_ready")
        decay_ready = sem("decay_ready")
        lam_abs, lam_exp = sem("lam_abs"), sem("lam_exp")
        x_turned = sem("x_turned")
        w_hi_ready, w_lo_ready = sem("w_hi_ready"), sem("w_lo_ready")
        slab_done = sem("slab_done")
        evicted = sem("evicted")
        src_ready = sem("src_ready")
        act_hi_ready, act_lo_ready = sem("act_hi_ready"), sem("act_lo_ready")
        sq_ready, sq_summed = sem("sq_ready"), sem("sq_summed")
        ssq_done, root_done, rstd_ready = sem("ssq_done"), sem("root_done"), sem("rstd_ready")
        dve_step = sem("dve_step")
        act_step = sem("act_step")
        conv_done, gates_done, gate_read, tanh_done = sem("conv_done"), sem("gates_done"), sem("gate_read"), sem("tanh_done")
        root_t_done, gelu_done = sem("root_t_done"), sem("gelu_done")
        row_turned = sem("row_turned")
        lg_ready = sem("lg_ready")
        lru_scaled = sem("lru_scaled")
        v_half, v_read = sem("v_half"), sem("v_read")
        early_done, early_read = sem("early_done"), sem("early_read")
        z_done, z_abs, z_log, soft_ready = sem("z_done"), sem("z_abs"), sem("z_log"), sem("soft_ready")
        soft_hi_ready, soft_lo_ready = sem("soft_hi_ready"), sem("soft_lo_ready")
        suffix_done, att_ready, pv_done = sem("suffix_done"), sem("att_ready"), sem("pv_done")
        ffn_gate, ffn_silu = sem("ffn_gate"), sem("ffn_silu")
        ffn_up, ffn_hidden = sem("ffn_up"), sem("ffn_hidden")
        hid_hi_ready, hid_lo_ready = sem("hid_hi_ready"), sem("hid_lo_ready")
        xn_sq, xn_mean = sem("xn_sq"), sem("xn_mean")
        f_abs = sem("f_abs")
        ms2_ready, f_pre, f_exp, f_ln, f_sum = sem("ms2_ready"), sem("f_pre"), sem("f_exp"), sem("f_ln"), sem("f_sum")
        f_parts = sem("f_parts")
        negf_done, negf_ready = sem("negf_done"), sem("negf_ready")
        gate_pre, gate_ready = sem("gate_pre"), sem("gate_ready")
        s_done, s_max, p_exp, p_ready2, pt_done, pt_ready = sem("s_done"), sem("s_max"), sem("p_exp"), sem("p_ready2"), sem("pt_done"), sem("pt_ready")
        pv2_done = sem("pv2_done")
        up_scaled, up_tap, up_conv, up_silu = sem("up_scaled"), sem("up_tap"), sem("up_conv"), sem("up_silu")
        up_mid = sem("up_mid")
        up_hidden, up_hi, up_lo = sem("up_hidden"), sem("up_hi"), sem("up_lo")
        rows_done, xn_gained, xn_scaled = sem("rows_done"), sem("xn_gained"), sem("xn_scaled")
        xn_inverse = sem("xn_inverse")
        xn_turned, xn_ready, xn_sum, xn_root, xn_out, stored = sem("xn_turned"), sem("xn_ready"), sem("xn_sum"), sem("xn_root"), sem("xn_out"), sem("stored")

        def col(name, j, n=P):
            return par[0:n, AT[name] + j:AT[name] + j + 1]

        def tap_col(tap, chunk):
            return par[:, bass.ds(chunk + (NROWS + tap * 2 * FC), 1)]

        block = ctx.enter_context(nc.Block())

        @block.sync
        def _(sp):
            def load_slab(s, i=None):
                w, kind, k0, nk, c0, nc_ = SLABS[s]
                step = 0 if i is None else i
                if s >= 2 or i is not None:
                    sp.wait_ge(w_lo_ready, s - 1 + 2 * step)
                src = t[w][0].rearrange("(k p) n -> p k n", p=P)[:, k0:k0 + nk]
                src = src[:, :, c0:c0 + nc_] if i is None else src[:, :, bass.ds(i * COLS_A + c0, COLS_A)]
                dst = raw[:, s % 2, 0:nk * nc_].rearrange("p (k n) -> p k n", k=nk)
                sp.dma_start(dst, src).then_inc(raw_in[s % 2], 16)

            load_slab(0)
            x_rows = t["x"][0].rearrange("(b p) d -> p b d", p=P)
            for b in range(TB):
                sp.dma_start(xin[:, b, :], x_rows[:, b, :]).then_inc(x_in[b], 16)
            load_slab(1)
            r = 0
            for name, n in ROWS[1:]:
                src = t[name]
                flat = src[0] if len(src.shape) > 1 else src
                if len(flat.shape) == 2:
                    flat = flat.rearrange("a b -> (a b)")
                sp.dma_start(rows[r:r + n, :], flat.rearrange("(r c) -> r c", c=P)).then_inc(row_in, 16)
                r += n
            taps = t["conv_ffn_w_2"][0].rearrange("k (c p) -> (k c) p", p=P)
            for j in range(2):
                sp.dma_start(tap_rows[:, j, :], taps[j * TAP_ROWS:(j + 1) * TAP_ROWS, :]).then_inc(row_in, 16)
            sp.dma_start(f_bias[:, :], t["b_f_2"].rearrange("a h -> h a")).then_inc(row_in, 16)
            load_slab(2)
            sp.wait_ge(bd_zeroed, 1)
            for g, name in enumerate(("w_rg", "w_ig")):
                for e in range(2):
                    src = t[name][0].rearrange("(c e) i o -> e i c o", e=2)
                    sp.dma_start(gate_bd[64 * e:64 * e + 64, g, :, 64 * e:64 * e + 64], src[e]).then_inc(bd_in, 16)
            for s in range(3, S_FFN):
                load_slab(s)
            with sp.Fori(0, FFN_STEPS) as i:
                load_slab(S_FFN, i)
                load_slab(S_FFN + 1, i)
            for s in range(S_DOWN, S_UP):
                load_slab(s)
            with sp.Fori(0, FFN_STEPS) as i:
                load_slab(S_UP, i)
                load_slab(S_UP + 1, i)
            for s in range(S_DOWN2, N_SLABS):
                load_slab(s)
                if s == S_DOWN2 + 2:
                    sp.wait_ge(slab_done, S_DOWN2)
                    sp.dma_start(gain_out[:, :], t["norm_f_g_2"].rearrange("(a d) -> a d", a=1).broadcast_to([P, D])).then_inc(gain_in, 16)
            out_rows = out[0].rearrange("(b p) d -> p b d", p=P)
            for b in range(TB):
                sp.wait_ge(xn_scaled, b + 1)
                sp.wait_ge(xn_out, b + 1)
                sp.dma_start(out_rows[:, b, :], xnat[:, b, :]).then_inc(stored, 16)
            sp.wait_ge(stored, 16 * TB)

        @block.gpsimd
        def _(pool):
            g = nc.gpsimd
            g.memset(ident[:], 0.0).then_inc(ident_zeroed, 1)
            pool.wait_ge(ident_zeroed, 1)
            g.affine_select(out=ident[:], in_=ident[:], compare_op=ALU.not_equal, fill=1.0, base=0,
                            pattern=[[-1, P]], channel_multiplier=1).then_inc(ident_set, 1)
            g.memset(ones[:], 1.0).then_inc(const_set, 1)
            g.memset(eps[:, 0:1], EPS).then_inc(const_set, 1)
            g.memset(eps[:, 1:2], EPS * EPS).then_inc(const_set, 1)
            g.memset(tmp[:, 1, 0:2 * P], -1.0).then_inc(const_set, 1)
            g.memset(tmp[:, 0, 0:2 * P], MASKED).then_inc(const_set, 1)
            pool.wait_ge(const_set, 5)
            g.affine_select(out=tmp[:, 1, 0:P], in_=tmp[:, 1, 0:P], compare_op=ALU.is_ge, fill=0.0, base=0,
                            pattern=[[-1, P]], channel_multiplier=1).then_inc(const_set, 1)
            g.affine_select(out=tmp[:, 0, 0:P], in_=tmp[:, 0, 0:P], compare_op=ALU.is_ge, fill=0.0, base=0,
                            pattern=[[-1, P]], channel_multiplier=1).then_inc(const_set, 1)
            g.affine_select(out=tmp[:, 0, P:2 * P], in_=tmp[:, 0, P:2 * P], compare_op=ALU.is_gt, fill=0.0, base=0,
                            pattern=[[1, P]], channel_multiplier=-1).then_inc(const_set, 1)
            pool.wait_ge(const_set, 8)
            pool.wait_ge(ident_set, 1)
            g.tensor_copy(mask_kq[:], tmp[:, 0, 0:P]).then_inc(const_bf, 1)
            g.tensor_copy(mask_qk[:], tmp[:, 0, P:2 * P]).then_inc(const_bf, 1)
            g.tensor_copy(ident_bf[:], ident[:]).then_inc(const_bf, 1)
            g.tensor_copy(ident_r[:], ident[0:HEADS, 0:HEADS]).then_inc(const_bf, 1)
            g.tensor_copy(neg_tri[:], tmp[:, 1, 0:P]).then_inc(const_bf, 1)
            g.tensor_copy(neg_ones[:], tmp[:, 1, P:2 * P]).then_inc(const_bf, 1)
            n = 0
            for rs in ((N_MIX,), (N_LRU,), (N_ATT,), (N_FFN,), (N_FINAL, N_MIX2), (N_FFN2,)):
                for c in range(4 if rs[0] in (N_LRU, N_ATT) else DC):
                    for r in rs:
                        pool.wait_ge(sq_ready, n + 1)
                        if c == 0:
                            if r >= 2:
                                pool.wait_ge(ssq_done, r - 1)
                            ins = g.tensor_copy(acc[:, r % 2], sq[:, n % 2])
                        else:
                            pool.wait_ge(sq_summed, n)
                            ins = g.tensor_tensor(acc[:, r % 2], acc[:, r % 2], sq[:, n % 2], ALU.add)
                        ins.then_inc(sq_summed, 1)
                        n += 1
                if rs[0] == N_MIX:
                    pool.wait_ge(x_turned, DC)
                    pool.wait_ge(par_done, 2)
                    g.memset(gate_bd[:], 0.0).then_inc(bd_zeroed, 1)

        @block.scalar
        def _(act):
            A = nc.scalar.activation
            state = {"sq": 0}

            def split_w(s, i=None, last=False):
                if s >= N_SLABS:
                    return
                step = 0 if i is None else i
                n = SLABS[s][3] * SLABS[s][5] if i is None else SLAB
                act.wait_ge(raw_in[s % 2], 16 * (s // 2 + 1 + step))
                if s >= 2:
                    act.wait_ge(slab_done, s - 1 + step * 2)
                A(w_hi[:, s % 2, 0:n], raw[:, s % 2, 0:n], ACT.Copy).then_inc(w_hi_ready, 1)

            def square(src, scale=1.0):
                n = state["sq"]
                if n >= 2:
                    act.wait_ge(sq_summed, n - 1)
                A(sq[:, n % 2], src, ACT.Square, scale=scale).then_inc(sq_ready, 1)
                state["sq"] += 1

            def split_act(q, hi, src, gain, free=None):
                act.wait_ge(src_ready, src_count(q))
                if free is not None:
                    act.wait_ge(slab_done, free)
                A(hi, src, ACT.Copy, scale=gain).then_inc(act_hi_ready, 1)

            def root(r, src):
                act.wait_ge(ssq_done, r + 1)
                A(rstd[:, RSTD_AT[r]], src, ACT.Sqrt, bias=eps[:, 0:1],
                  scale=1.0 / (WIDTH if r in (N_LRU, N_ATT) else D)).then_inc(root_done, 1)

            act.dma_start(first_rows[:, :], t[ROWS[0][0]][0].rearrange("(r c) -> r c", c=P)).then_inc(first_in, 16)
            act.wait_ge(par_done, 1)
            A(par[:, 0:FIRST_ROWS], psum[:, 7, 0:FIRST_ROWS], ACT.Copy).then_inc(par_ready, 1)
            split_w(0)
            act.wait_ge(par_ready, 1)
            for c in range(DC):
                split_act(C_MIX + c, act_hi[:, c], xT[:, c], col("norm_mix", c))
                square(xT[:, c])
            split_w(1)
            root(N_MIX, psum[:, bank_of(0) + 3])
            act.wait_ge(par_done, 2)
            A(par[:, FIRST_ROWS:], psum[:, 7, FIRST_ROWS:NROWS + 2 * TAP_ROWS], ACT.Copy).then_inc(par_ready, 1)
            act.wait_ge(par_ready, 2)
            A(small[:, 0:4], par[:, AT["lru_lambda"]:AT["lru_lambda"] + WC], ACT.Abs).then_inc(lam_abs, 1)
            act.wait_ge(lam_abs, 1)
            A(small[:, 4:8], small[:, 0:4], ACT.Exp, scale=-1.0).then_inc(lam_exp, 1)
            for s in range(0, S_V + 1):
                if s == S_V:
                    root(N_LRU, psum[:, 6])
                split_w(s + 2)
                if s in (S_LG, S_LG + 1):
                    for c in range(2 * (s - S_LG), 2 * (s - S_LG) + 2):
                        act.wait_ge(lg_ready, c + 1)
                        A(lg[:, c], lg[:, c], ACT.Gelu_apprx_tanh).then_inc(gelu_done, 1)
                if 2 <= s < 2 + WC:
                    c = s - 2
                    b = bank_of(GROUP[s])
                    act.wait_ge(gates_done, c + 1)
                    if c >= 2:
                        act.wait_ge(src_ready, C_LRU + c - 1)
                    A(gate_t[:, c % 2], psum[:, b + 2], ACT.Sigmoid, bias=col("b_rg", c)).then_inc(act_step, 1)
                    A(gate_i[:, c % 2], psum[:, b + 3], ACT.Sigmoid, bias=col("b_ig", c)).then_inc(gate_read, 1)
                    act.wait_ge(act_step, c + 1)
                    if c == 0:
                        act.wait_ge(decay_ready, 1)
                    A(gate_t[:, c % 2], gate_t[:, c % 2], ACT.Tanh, scale=decay[:, c:c + 1]).then_inc(tanh_done, 1)
                    act.wait_ge(tanh_done, c + 1)
                    A(root_t[:, c % 2], gate_t[:, c % 2], ACT.Sqrt).then_inc(root_t_done, 1)
                if 4 <= s < 4 + WC:
                    act.wait_ge(src_ready, C_LRU + s - 3)
                    square(lx[:, s - 4])
            nc.scalar.preload_act_table_set("natural_log_exp_and_others")

            def log_part(h):
                z = stick[:, h % 2]
                act.wait_ge(z_done, h + 1)
                b = head_bank(h)
                A(z, psum[:, b:b + 3].rearrange("p b n -> p (b n)")[:, 0:CAUSAL], ACT.Abs).then_inc(z_abs, 1)
                act.wait_ge(z_abs, h + 1)
                A(z, z, ACT.Exp, scale=-1.0).then_inc(act_step, 1)
                act.wait_ge(act_step, WC + h + 1)
                A(z, z, ACT.Ln, bias=1.0).then_inc(z_log, 1)

            def att_operand(c):
                act.wait_ge(src_ready, C_ATT + c + 1)
                square(yatt[:, c])
                split_act(C_ATT + c, act_hi[:, WC + c], yatt[:, c], col("norm_att_out", c), S_V + 2)

            def weights(h):
                act.wait_ge(suffix_done, h + 1)
                if h >= 2:
                    act.wait_ge(pv_done, h - 1)
                b = head_bank(h)
                for n0, n1 in ((0, TOKENS), (TOKENS, CAUSAL)):
                    A(att[:, h % 2, n0:n1], psum[:, b:b + 3].rearrange("p b n -> p (b n)")[:, n0:n1], ACT.Exp).then_inc(att_ready, 1)

            log_part(0)
            log_part(1)
            weights(0)
            split_w(S_V + 3)
            for h in range(HEADS):
                if 1 < h + 1 < HEADS:
                    log_part(h + 1)
                if h:
                    weights(h)
                if LRU_HEAD <= h < LRU_HEAD + WC:
                    c = h - LRU_HEAD
                    act.wait_ge(lru_scaled, c + 1)
                    split_act(C_LRU + c, act_hi[:, c], lx[:, c], col("norm_lru_out", c), S_V + 2)
                if h >= 3 and h % 2:
                    att_operand((h - 3) // 2)
            att_operand(WC - 1)

            for s in range(S_OUT_LRU, S_FFN):
                split_w(s + 2)
                if s == S_OUT_LRU:
                    root(N_ATT, psum[:, 0])
                if s >= S_OUT_ATT:
                    for c in range(4 * (s - S_OUT_ATT), 4 * (s - S_OUT_ATT) + 4):
                        split_act(C_FFN + c, act_hi[:, c], xT[:, c], col("norm_ffn", c), S_OUT_ATT if c < WC else S_FFN)
                        square(xT[:, c])
            root(N_FFN, psum[:, bank_of(GROUP[S_FFN]) + 3])
            nc.scalar.preload_act_table(ACT.Silu)
            with act.Fori(0, FFN_STEPS) as i:
                split_w(S_FFN + 2, i)
                for j in range(2):
                    act.wait_ge(ffn_gate, 2 * i + (j + 1))
                    A(tmp[:, 2 + j], tmp[:, j], ACT.Silu).then_inc(ffn_silu, 1)
                split_w(S_FFN + 3, i)
                for j in range(2):
                    act.wait_ge(ffn_hidden, 2 * i + (j + 1))
                    A(hid_hi[:, bass.ds(2 * i + j, 1)].rearrange("p a n -> p (a n)"), tmp[:, 4 + j], ACT.Copy).then_inc(hid_hi_ready, 1)
            for s in range(S_DOWN, S_K2):
                split_w(s + 2)
                half = (s - S_DOWN) // DOWN_SLABS
                if (s - S_DOWN) % DOWN_SLABS == DOWN_SLABS - 1:
                    chunks = range(4 * half, 4 * half + 4)
                    if half == 0:
                        for c in chunks:
                            split_act(C_MIX2 + c, act_hi[:, c], xT[:, c], gain_both[:, c:c + 1], S_DOWN)
                    for c in chunks:
                        if half:
                            split_act(C_MIX2 + c, act_hi[:, c], xT[:, c], gain_both[:, c:c + 1], S_DOWN)
                        square(xT[:, c])
                        square(xT[:, c], col("norm_final", c))
            b = bank_of(GROUP[S_K2])
            act.wait_ge(ms2_ready, 1)
            A(rstd[:, RSTD_AT[N_MIX2]], rstd[:, RSTD_AT[N_MIX2]], ACT.Sqrt, bias=eps[:, 1:2], scale=1.0 / D).then_inc(root_done, 1)
            root(N_FINAL, psum[:, b + 2])
            n_gate = 0
            for s in range(S_K2, S_OA2 - 1):
                split_w(s + 2)
                if s == S_F2:
                    act.wait_ge(f_pre, 1)
                    nc.scalar.preload_act_table_set("natural_log_exp_and_others")
                    A(fsum[:, 1], fsum[:, 0], ACT.Abs).then_inc(f_abs, 1)
                    act.wait_ge(f_abs, 1)
                    A(fsum[:, 1], fsum[:, 1], ACT.Exp, scale=-1.0).then_inc(f_exp, 1)
                    act.wait_ge(f_exp, 1)
                    A(fsum[:, 1], fsum[:, 1], ACT.Ln, bias=1.0).then_inc(f_ln, 1)
                if S_CC <= s < S_CC + HEADS:
                    h = s - S_CC
                    act.wait_ge(negf_done, h + 1)
                    A(neg_f[:, h], psum[:, bank_of(GROUP[s]) + 3], ACT.Copy).then_inc(negf_ready, 1)
                if S_GC <= s < S_OC2 or S_GA <= s < S_OA2 - 1:
                    for j in range(2):
                        m = n_gate % DC
                        dst = gc[:, m] if n_gate < DC else ga[:, m]
                        act.wait_ge(gate_pre, n_gate + 1)
                        A(dst, tmp[:, n_gate % 4], ACT.Sigmoid, bias=col("b_gate_2", n_gate)).then_inc(gate_ready, 1)
                        n_gate += 1
                if s in (S_CB, S_CB + 1):
                    for c in range(2 * (s - S_CB), 2 * (s - S_CB) + 2):
                        split_act(C_Z2 + c, z_hi[:, c], conv_u[:, c], 1.0)

            def exps(h):
                for n, i in enumerate(QUERY_ORDER):
                    act.wait_ge(s_max, TB * h + n + 1)
                    part = probs[:, h % 2, QUERY_AT[i]:QUERY_AT[i] + P * (i + 1)]
                    k = 4 * (h % 2) + i
                    A(part, part, ACT.Exp, bias=small[:, 16 + k:17 + k], scale=-1.0, accum_out=small[:, 32 + k:33 + k]).then_inc(p_exp, 1)

            exps(0)
            split_w(S_OA2 + 1)
            for h in range(HEADS):
                act.wait_ge(pt_done, h + 1)
                if h >= 2:
                    act.wait_ge(pv2_done, h - 1)
                b = head_bank(h)
                for n0, n1 in ((0, TOKENS), (TOKENS, CAUSAL)):
                    A(probs_T[:, h % 2, n0:n1], psum[:, b:b + 3].rearrange("p b n -> p (b n)")[:, n0:n1], ACT.Copy).then_inc(pt_ready, 1)
                if h >= 2 and h % 2 == 0:
                    c = (h - 2) // 2
                    act.wait_ge(pv2_done, 2 * c + 2)
                    A(act_hi[:, WC + c], psum[:, pair_bank(c)], ACT.Copy).then_inc(act_hi_ready, 1)
                if h + 1 < HEADS:
                    exps(h + 1)
            act.wait_ge(pv2_done, HEADS)
            A(act_hi[:, DC - 1], psum[:, pair_bank(WC - 1)], ACT.Copy).then_inc(act_hi_ready, 1)
            act.wait_ge(gate_pre, 2 * DC)
            for m in (DC - 2, DC - 1):
                A(ga[:, m], ga[:, m], ACT.Sigmoid, bias=col("b_gate_2", DC + m)).then_inc(gate_ready, 1)
            for s in range(S_OA2, S_UP):
                split_w(s + 2)
                if s < S_O2:
                    for m in range(4 * (s - S_OA2), 4 * (s - S_OA2) + 4):
                        split_act(C_M2 + m, m_hi[:, m], gc[:, m], 1.0)
                else:
                    for c in range(2 * (s - S_O2), 2 * (s - S_O2) + 2):
                        split_act(C_UP2 + c, act_hi[:, c], xT[:, c], col("norm_ffn_g_2", c))
                        square(xT[:, c])
            root(N_FFN2, psum[:, bank_of(GROUP[S_UP]) + 3])
            nc.scalar.preload_act_table(ACT.Silu)
            with act.Fori(0, FFN_STEPS) as i:
                split_w(S_UP + 2, i)
                for j in range(2):
                    act.wait_ge(up_scaled, 4 * i + (j + 1))
                    A(tmp[:, 2 + j], tmp[:, j], ACT.Copy, scale=tap_col(2, 2 * i + j)).then_inc(up_tap, 1)
                for j in range(2):
                    act.wait_ge(up_conv, 4 * i + (j + 1))
                    A(tmp[:, 2 + j], tmp[:, 2 + j], ACT.Silu).then_inc(up_silu, 1)
                split_w(S_UP + 3, i)
                for j in range(2):
                    act.wait_ge(up_scaled, 4 * i + (j + 3))
                    A(tmp[:, j], tmp[:, 4 + j], ACT.Copy, scale=tap_col(2, 2 * i + (FC + j))).then_inc(up_tap, 1)
                for j in range(2):
                    act.wait_ge(up_hidden, 2 * i + (j + 1))
                    A(hid_hi[:, bass.ds(2 * i + j, 1)].rearrange("p a n -> p (a n)"), tmp[:, j], ACT.Copy).then_inc(hid_hi_ready, 1)
            def square_rows(n):
                b, half = n % TB, n // TB
                act.wait_ge(xn_sum, n + 1)
                if n:
                    act.wait_ge(xn_sq, n)
                A(junk[:, :], xnat[:, b, half * WIDTH:(half + 1) * WIDTH], ACT.Square,
                  accum_out=small[:, 8 + n:9 + n]).then_inc(xn_sq, 1)

            for s in range(S_DOWN2, N_SLABS - 2):
                split_w(s + 2)
                if s == S_DOWN2 + DOWN_SLABS:
                    for b in range(TB):
                        square_rows(b)
            nc.scalar.preload_act_table(ACT.Sqrt)
            for n in range(TB + 2):
                if n < TB:
                    square_rows(TB + n)
                if 0 <= n - 1 < TB:
                    b = n - 1
                    act.wait_ge(xn_mean, b + 1)
                    A(small[:, 48 + b:49 + b], small[:, 48 + b:49 + b], ACT.Sqrt, bias=eps[:, 0:1], scale=1.0 / D).then_inc(xn_root, 1)
                if n >= 2:
                    b = n - 2
                    act.wait_ge(xn_gained, b + 1)
                    act.wait_ge(xn_inverse, b + 1)
                    A(xnat[:, b, 0:WIDTH], xnat[:, b, 0:WIDTH], ACT.Copy, scale=small[:, 52 + b:53 + b]).then_inc(xn_scaled, 1)

        @block.vector
        def _(dve):
            V = nc.vector
            steps = {"n": 0, "evicted": 0}

            def mark(ins):
                steps["n"] += 1
                ins.then_inc(dve_step, 1)

            def settle():
                if steps["n"]:
                    dve.wait_ge(dve_step, steps["n"])
                if steps["evicted"]:
                    dve.wait_ge(evicted, steps["evicted"])

            def free(ins):
                steps["evicted"] += 1
                ins.then_inc(evicted, 1)

            def split_w(s, i=None):
                if s >= N_SLABS:
                    return
                step = 0 if i is None else i
                n = SLABS[s][3] * SLABS[s][5] if i is None else SLAB
                dve.wait_ge(w_hi_ready, s + 1 + 2 * step)
                V.tensor_tensor(w_lo[:, s % 2, 0:n], raw[:, s % 2, 0:n], w_hi[:, s % 2, 0:n].bitcast(F32),
                                ALU.subtract).then_inc(w_lo_ready, 1)

            def split_act(q, hi, lo, src, gain=None):
                dve.wait_ge(act_hi_ready, q + 1)
                if gain is None:
                    ins = V.tensor_tensor(lo, src, hi.bitcast(F32), ALU.subtract)
                else:
                    ins = V.scalar_tensor_tensor(lo, src, gain, hi.bitcast(F32), ALU.mult, ALU.subtract)
                ins.then_inc(act_lo_ready, 1)

            def finished(s, i=None):
                dve.wait_ge(slab_done, s + 1 + (0 if i is None else 2 * i))

            def bank(s, m):
                return psum[:, bank_of(GROUP[s]) + m]

            def inverse(r):
                dve.wait_ge(root_done, TURN[r] + 1)
                f = rstd[:, RSTD_AT[r]]
                V.reciprocal(f, f).then_inc(rstd_ready, 1)
                dve.wait_ge(rstd_ready, TURN[r] + 1)

            def R(r):
                return rstd[:, RSTD_AT[r]]

            split_w(0)
            for c in range(DC):
                dve.wait_ge(x_turned, c + 1)
                V.tensor_copy(xT[:, c], psum[:, c]).then_inc(src_ready, 1)
                if c == 0:
                    dve.wait_ge(par_ready, 1)
                else:
                    split_act(C_MIX + c - 1, act_hi[:, c - 1], act_lo[:, c - 1], xT[:, c - 1], col("norm_mix", c - 1))
            split_act(C_MIX + DC - 1, act_hi[:, DC - 1], act_lo[:, DC - 1], xT[:, DC - 1], col("norm_mix", DC - 1))
            split_w(1)
            def decay_rate():
                dve.wait_ge(par_ready, 2)
                mark(V.tensor_tensor(gain_both[:, :], par[:, AT["norm_final"]:AT["norm_final"] + DC],
                                     par[:, AT["norm_mix_g_2"]:AT["norm_mix_g_2"] + DC], ALU.mult))
                lam = par[:, AT["lru_lambda"]:AT["lru_lambda"] + WC]
                dve.wait_ge(lam_exp, 1)
                mark(V.tensor_scalar(small[:, 8:12], small[:, 4:8], 2.0, None, ALU.add))
                settle()
                mark(V.reciprocal(small[:, 8:12], small[:, 8:12]))
                settle()
                mark(V.tensor_tensor(small[:, 12:16], small[:, 8:12], small[:, 4:8], ALU.mult))
                settle()
                mark(V.tensor_tensor(small[:, 16:20], small[:, 12:16], small[:, 12:16], ALU.mult))
                settle()
                mark(V.tensor_scalar(small[:, 20:24], small[:, 16:20], 1.0 / 19, None, ALU.mult))
                for k in range(17, 1, -2):
                    settle()
                    mark(V.scalar_tensor_tensor(small[:, 20:24], small[:, 20:24], 1.0 / k, small[:, 16:20], ALU.add, ALU.mult))
                settle()
                mark(V.scalar_tensor_tensor(small[:, 20:24], small[:, 20:24], 1.0, small[:, 12:16], ALU.add, ALU.mult))
                mark(V.tensor_scalar(small[:, 24:28], lam, 0.0, -4.0, ALU.min, ALU.mult))
                settle()
                V.scalar_tensor_tensor(decay[:, :], small[:, 20:24], 8.0, small[:, 24:28], ALU.mult, ALU.add).then_inc(decay_ready, 1)

            def conv(c):
                mark(V.tensor_scalar(xc[:, c], lx[:, c], col("conv_w", 3 * WC + c), col("conv_b", c), ALU.mult, ALU.add))
                for d in range(1, 4):
                    settle()
                    ins = V.scalar_tensor_tensor(xc[:, c, d:], lx[:, c, 0:TOKENS - d], col("conv_w", (3 - d) * WC + c),
                                                 xc[:, c, d:], ALU.mult, ALU.add)
                    if d < 3:
                        mark(ins)
                    else:
                        ins.then_inc(conv_done, 1)

            def lru(c):
                k = c % 2
                dve.wait_ge(tanh_done, c + 1)
                mark(V.tensor_scalar(lru_rc[:, :], gate_t[:, k], 1.0, None, ALU.add))
                mark(V.tensor_tensor(gate_i[:, k], gate_i[:, k], xc[:, c], ALU.mult))
                settle()
                mark(V.reciprocal(lru_rc[:, :], lru_rc[:, :]))
                settle()
                mark(V.tensor_scalar(lru_a[:, :], lru_rc[:, :], 2.0, -1.0, ALU.mult, ALU.add))
                dve.wait_ge(root_t_done, c + 1)
                mark(V.scalar_tensor_tensor(root_t[:, k], root_t[:, k], 2.0, lru_rc[:, :], ALU.mult, ALU.mult))
                settle()
                mark(V.tensor_tensor(root_t[:, k], root_t[:, k], gate_i[:, k], ALU.mult))
                settle()
                mark(V.tensor_tensor_scan(lru_rc[:, :], lru_a[:, :], root_t[:, k], 0.0, ALU.mult, ALU.add))
                settle()
                dve.wait_ge(gelu_done, c + 1)
                V.tensor_tensor(lx[:, c], lru_rc[:, :], lg[:, c], ALU.mult).then_inc(src_ready, 1)
                dve.wait_ge(src_ready, C_LRU + c + 1)


            inverse(N_MIX)
            for s in range(S_LX, S_V):
                finished(s)
                for j in range(2):
                    c = 2 * (s % 2) + j
                    if s < S_LG:
                        ins = V.tensor_tensor(lx[:, c], bank(s, j), R(N_MIX), ALU.mult)
                    elif s < S_Q:
                        ins = V.tensor_tensor(lg[:, c], bank(s, j), R(N_MIX), ALU.mult)
                        ins.then_inc(lg_ready, 1)
                    elif s < S_K:
                        ins = V.scalar_tensor_tensor(qT[:, c], bank(s, j), SCALE, R(N_MIX), ALU.mult, ALU.mult)
                    else:
                        ins = V.tensor_tensor(kT[:, c], bank(s, j), R(N_MIX), ALU.mult)
                if not S_LG <= s < S_Q:
                    free(ins)
                split_w(s + 2)
                if s == 0:
                    decay_rate()
                if s < S_LG:
                    settle()
                    conv(2 * s)
                    conv(2 * s + 1)
                if 3 <= s < 3 + WC:
                    lru(s - 3)
            dve.wait_ge(row_turned, 1)
            V.tensor_copy(small[:, 32:32 + TB], psum[:, 7, 0:TB]).then_inc(row_read, 1)
            dve.wait_ge(row_read, 1)
            inverse(N_LRU)
            finished(S_V)
            split_w(S_V + 2)

            def head_columns(h):
                b = head_bank(h)
                return psum[:, b:b + 3].rearrange("p b n -> p (b n)")[:, 0:CAUSAL]

            def log_part(h):
                dve.wait_ge(z_log, h + 1)
                if h >= 2:
                    dve.wait_ge(suffix_done, h - 1)
                V.scalar_tensor_tensor(soft[:, h % 2], head_columns(h), 0.0, stick[:, h % 2],
                                       ALU.max, ALU.add).then_inc(soft_ready, 1)
                dve.wait_ge(soft_ready, h + 1)
                V.tensor_copy(soft_hi[:, h % 2, P:], soft[:, h % 2, P:]).then_inc(soft_hi_ready, 1)
                dve.wait_ge(soft_hi_ready, h + 1)
                V.tensor_tensor(soft_lo[:, h % 2, P:], soft[:, h % 2, P:], soft_hi[:, h % 2, P:].bitcast(F32),
                                ALU.subtract).then_inc(soft_lo_ready, 1)

            def att_out(c):
                dve.wait_ge(pv_done, 2 * c + 2)
                V.tensor_copy(yatt[:, c], psum[:, 0]).then_inc(src_ready, 1)

            dve.wait_ge(v_half, 1)
            for b in (2, 3):
                V.tensor_scalar(v[:, b], bank(S_V + 1, b), small[:, 32 + b:33 + b], None, ALU.mult).then_inc(v_read, 1)
            log_part(0)
            for c in range(WC):
                V.tensor_tensor(lx[:, c], lx[:, c], R(N_LRU), ALU.mult).then_inc(lru_scaled, 1)
            dve.wait_ge(lru_scaled, WC)
            finished(S_V + 1)
            for b in (0, 1):
                ins = V.tensor_scalar(v[:, b], bank(S_V + 1, b), small[:, 32 + b:33 + b], None, ALU.mult)
            free(ins)
            log_part(1)
            split_w(S_V + 3)
            for h in range(HEADS):
                if LRU_HEAD < h <= LRU_HEAD + WC:
                    c = h - LRU_HEAD - 1
                    split_act(C_LRU + c, act_hi[:, c], act_lo[:, c], lx[:, c], col("norm_lru_out", c))
                if h > EARLY_HEAD and early_part(h - 1) and early_part(h - 1)[1]:
                    m = early_part(h - 1)[0]
                    dve.wait_ge(early_done, m + 1)
                    V.tensor_tensor(xT[:, m], psum[:, 1], xT[:, m], ALU.add).then_inc(early_read, 1)
                if 1 < h + 1 < HEADS:
                    log_part(h + 1)
                if h >= 2 and h % 2 == 0:
                    att_out((h - 2) // 2)
                if h >= 4 and h % 2 == 0:
                    c = (h - 4) // 2
                    split_act(C_ATT + c, act_hi[:, WC + c], act_lo[:, WC + c], yatt[:, c], col("norm_att_out", c))
            att_out(WC - 1)
            c = WC - 2
            split_act(C_ATT + c, act_hi[:, WC + c], act_lo[:, WC + c], yatt[:, c], col("norm_att_out", c))
            split_act(C_ATT + WC - 1, act_hi[:, DC - 1], act_lo[:, DC - 1], yatt[:, WC - 1], col("norm_att_out", WC - 1))
            for s in (S_OUT_LRU, S_OUT_LRU + 1):
                finished(s)
                for m in range(EARLY if s == S_OUT_LRU else 0, 4):
                    c = 4 * (s % 2) + m
                    ins = V.tensor_tensor(xT[:, c], bank(s, m), xT[:, c], ALU.add)
                    mark(ins) if m < 3 else free(ins)
                split_w(s + 2)
            inverse(N_ATT)
            settle()
            dve.wait_ge(early_read, EARLY)
            for s in (S_OUT_ATT, S_OUT_ATT + 1):
                finished(s)
                for m in range(4):
                    c = 4 * (s % 2) + m
                    ins = V.tensor_tensor(tmp[:, m % 2], bank(s, m), R(N_ATT), ALU.mult)
                    mark(ins) if m < 3 else free(ins)
                    settle()
                    V.tensor_tensor(xT[:, c], xT[:, c], tmp[:, m % 2], ALU.add).then_inc(src_ready, 1)
                    dve.wait_ge(src_ready, src_count(C_FFN + c))
                    if m:
                        split_act(C_FFN + c - 1, act_hi[:, c - 1], act_lo[:, c - 1], xT[:, c - 1], col("norm_ffn", c - 1))
                split_act(C_FFN + c, act_hi[:, c], act_lo[:, c], xT[:, c], col("norm_ffn", c))
                split_w(s + 2)
            inverse(N_FFN)
            with dve.Fori(0, FFN_STEPS) as i:
                finished(S_FFN, i)
                for j in range(2):
                    V.tensor_tensor(tmp[:, j], bank(S_FFN, j), R(N_FFN), ALU.mult).then_inc(ffn_gate, 1)
                split_w(S_FFN + 2, i)
                finished(S_FFN + 1, i)
                for j in range(2):
                    V.tensor_tensor(tmp[:, 4 + j], bank(S_FFN + 1, j), R(N_FFN), ALU.mult).then_inc(ffn_up, 1)
                for j in range(2):
                    dve.wait_ge(ffn_up, 2 * i + (j + 1))
                    dve.wait_ge(ffn_silu, 2 * i + (j + 1))
                    V.tensor_tensor(tmp[:, 4 + j], tmp[:, 4 + j], tmp[:, 2 + j], ALU.mult).then_inc(ffn_hidden, 1)
                split_w(S_FFN + 3, i)
                for j in range(2):
                    dve.wait_ge(ffn_hidden, 2 * i + (j + 1))
                    dve.wait_ge(hid_hi_ready, 2 * i + (j + 1))
                    at = bass.ds(2 * i + j, 1)
                    V.tensor_tensor(hid_lo[:, at].rearrange("p a n -> p (a n)"), tmp[:, 4 + j],
                                    hid_hi[:, at].rearrange("p a n -> p (a n)").bitcast(F32),
                                    ALU.subtract).then_inc(hid_lo_ready, 1)
                dve.wait_ge(hid_lo_ready, 2 * i + 2)
            for s in range(S_DOWN, S_K2):
                finished(s)
                half = (s - S_DOWN) // DOWN_SLABS
                last = (s - S_DOWN) % DOWN_SLABS == DOWN_SLABS - 1
                if not last:
                    split_w(s + 2)
                    continue
                for m in range(4):
                    c = 4 * half + m
                    V.tensor_tensor(xT[:, c], bank(s, m), xT[:, c], ALU.add).then_inc(src_ready, 1)
                    dve.wait_ge(src_ready, src_count(C_MIX2 + c))
                    if m:
                        split_act(C_MIX2 + c - 1, act_hi[:, c - 1], act_lo[:, c - 1], xT[:, c - 1], gain_both[:, c - 1:c])
                split_act(C_MIX2 + c, act_hi[:, c], act_lo[:, c], xT[:, c], gain_both[:, c:c + 1])
                split_w(s + 2)
            dve.wait_ge(ssq_done, N_MIX2 + 1)
            mark(V.tensor_scalar(R(N_MIX2), bank(S_K2, 2), EPS, None, ALU.mult))
            settle()
            V.tensor_tensor(R(N_MIX2), bank(S_K2, 3), R(N_MIX2), ALU.add).then_inc(ms2_ready, 1)
            inverse(N_MIX2)
            both = R(N_MIX2)
            n_gate = 0
            for s in range(S_K2, S_OA2 - 1):
                finished(s)
                c0 = (s - S_K2) % 2 * 2 if s < S_V2 else (s - S_CC) % 2 * 2
                if s == S_F2:
                    free(V.tensor_tensor(fsum[:, 0], psum[0:HEADS, bank_of(GROUP[s])], rstd[0:HEADS, RSTD_AT[N_MIX2]], ALU.mult))
                    settle()
                    V.tensor_scalar(fsum[:, 0], fsum[:, 0], f_bias[:, 0:1], None, ALU.add).then_inc(f_pre, 1)
                elif s < S_V2:
                    for j in range(2):
                        if s < S_Q2:
                            ins = V.tensor_tensor(k2[:, c0 + j], bank(s, j), both, ALU.mult)
                        else:
                            ins = V.scalar_tensor_tensor(q2[:, c0 + j], bank(s, j), SCALE, both, ALU.mult, ALU.mult)
                    free(ins)
                elif s < S_CC:
                    if s > S_V2:
                        dve.wait_ge(row_turned, 2)
                        mark(V.tensor_copy(small[:, 52:52 + TB], psum[:, bank_of(GROUP[S_Q2]) + 3, 0:TB]))
                        settle()
                        for b in range(TB):
                            ins = V.tensor_scalar(v2[:, b], bank(s, b), small[:, 52 + b:53 + b], None, ALU.mult)
                        free(ins)
                elif s < S_CIN:
                    for j in range(2):
                        ins = V.tensor_tensor(conv_p[:, c0 + j], bank(s, j), both, ALU.mult)
                    free(ins)
                elif s < S_GC:
                    for j in range(2):
                        ins = V.tensor_tensor(tmp[:, 4 + j], bank(s, j), both, ALU.mult)
                    free(ins)
                elif s < S_OC2 or s >= S_GA:
                    for j in range(2):
                        if n_gate >= 4:
                            dve.wait_ge(gate_ready, n_gate - 3)
                        V.tensor_tensor(tmp[:, n_gate % 4], bank(s, j), both, ALU.mult).then_inc(gate_pre, 1)
                        n_gate += 1
                else:
                    dve.wait_ge(gate_ready, DC)
                    for m in range(4):
                        c = 4 * (s - S_OC2) + m
                        ins = V.tensor_tensor(gc[:, c], bank(s, m), gc[:, c], ALU.mult)
                    free(ins)
                split_w(s + 2)
                if s == S_F2:
                    dve.wait_ge(f_ln, 1)
                    mark(V.scalar_tensor_tensor(fsum[:, 1], fsum[:, 0], 0.0, fsum[:, 1], ALU.min, ALU.subtract))
                    mark(V.memset(tmp[0:HEADS, 5], 1.0))
                    settle()
                    V.tensor_tensor_scan(fsum[:, 0], tmp[0:HEADS, 5], fsum[:, 1], 0.0, ALU.mult, ALU.subtract).then_inc(f_sum, 1)
                    dve.wait_ge(f_sum, 1)
                    V.tensor_copy(f_split[:, 0], fsum[:, 0]).then_inc(f_parts, 1)
                    dve.wait_ge(f_parts, 1)
                    V.tensor_tensor(f_split[:, 1], fsum[:, 0], f_split[:, 0].bitcast(F32), ALU.subtract).then_inc(f_parts, 1)
                if s == S_K2:
                    inverse(N_FINAL)
                if S_K2 <= s < S_K2 + 4:
                    for c in (2 * (s - S_K2), 2 * (s - S_K2) + 1):
                        dve.wait_ge(sq_ready, SQ_DONE[N_MIX2])
                        mark(V.scalar_tensor_tensor(xT[:, c], xT[:, c], col("norm_final", c), R(N_FINAL), ALU.mult, ALU.mult))
                if S_CIN <= s < S_CB:
                    settle()
                    for j in range(2):
                        c = c0 + j
                        mark(V.tensor_tensor(conv_p[:, c], conv_p[:, c], tmp[:, 4 + j], ALU.mult))
                    settle()
                    for j in range(2):
                        c = c0 + j
                        mark(V.tensor_scalar(conv_u[:, c], conv_p[:, c], col("conv_mix_w_2", 2 * WC + c), None, ALU.mult))
                    for d in range(1, 3):
                        settle()
                        for j in range(2):
                            c = c0 + j
                            mark(V.scalar_tensor_tensor(conv_u[:, c, d:], conv_p[:, c, 0:TOKENS - d],
                                                        col("conv_mix_w_2", (2 - d) * WC + c), conv_u[:, c, d:],
                                                        ALU.mult, ALU.add))
                if S_CB <= s < S_GC:
                    settle()
                    for j in range(2):
                        c = c0 + j
                        V.tensor_tensor(conv_u[:, c], conv_u[:, c], tmp[:, 4 + j], ALU.mult).then_inc(src_ready, 1)
                    dve.wait_ge(src_ready, src_count(C_Z2 + c0 + 1))
                if S_CB < s <= S_CB + 2:
                    for c in range(2 * (s - S_CB - 1), 2 * (s - S_CB)):
                        split_act(C_Z2 + c, z_hi[:, c], z_lo[:, c], conv_u[:, c])

            def largest(h):
                dve.wait_ge(negf_ready, h + 1)
                if h >= 2:
                    dve.wait_ge(pt_done, h - 1)
                at = 16 + 4 * (h % 2)
                for n, i in enumerate(QUERY_ORDER):
                    dve.wait_ge(s_done, 3 * h + (1, 2, 2, 3)[n])
                    w = P * (i + 1)
                    V.tensor_tensor_reduce(out=probs[:, h % 2, QUERY_AT[i]:QUERY_AT[i] + w],
                                           in0=head_columns(h)[:, QUERY_AT[i]:QUERY_AT[i] + w], in1=neg_f[:, h, 0:w],
                                           scale=-1.0, scalar=3.0e38, op0=ALU.add, op1=ALU.min,
                                           accum_out=small[:, at + i:at + i + 1]).then_inc(s_max, 1)

            def normalise(h):
                at = 32 + 4 * (h % 2)
                for n, i in enumerate(QUERY_ORDER):
                    dve.wait_ge(p_exp, TB * h + n + 1)
                    mark(V.reciprocal(small[:, at + 8 + i:at + 9 + i], small[:, at + i:at + i + 1]))
                    settle()
                    part = probs[:, h % 2, QUERY_AT[i]:QUERY_AT[i] + P * (i + 1)]
                    V.tensor_scalar(part, part, small[:, at + 8 + i:at + 9 + i], None, ALU.mult).then_inc(p_ready2, 1)

            largest(0)
            normalise(0)
            finished(S_OA2 - 1)
            for j in range(2):
                V.tensor_tensor(ga[:, DC - 2 + j], bank(S_OA2 - 1, j), both, ALU.mult).then_inc(gate_pre, 1)
            split_w(S_OA2 + 1)
            for h in range(HEADS):
                if h + 1 < HEADS:
                    largest(h + 1)
                if h >= 2 and h % 2 == 0:
                    c = (h - 2) // 2
                    split_act(C_O2 + c, act_hi[:, WC + c], act_lo[:, WC + c], psum[:, pair_bank(c)])
                if h + 1 < HEADS:
                    normalise(h + 1)
            split_act(C_O2 + WC - 1, act_hi[:, DC - 1], act_lo[:, DC - 1], psum[:, pair_bank(WC - 1)])
            for s in range(S_OA2, S_O2):
                finished(s)
                if s > S_OA2:
                    dve.wait_ge(gate_ready, 2 * DC)
                for m in range(4):
                    c = 4 * (s - S_OA2) + m
                    ins = V.tensor_tensor(tmp[:, m], bank(s, m), ga[:, c], ALU.mult)
                    mark(ins) if m < 3 else free(ins)
                    settle()
                    V.tensor_tensor(gc[:, c], gc[:, c], tmp[:, m], ALU.add).then_inc(src_ready, 1)
                    dve.wait_ge(src_ready, src_count(C_M2 + c))
                    if m:
                        split_act(C_M2 + c - 1, m_hi[:, c - 1], m_lo[:, c - 1], gc[:, c - 1])
                split_act(C_M2 + c, m_hi[:, c], m_lo[:, c], gc[:, c])
                split_w(s + 2)
            for s in range(S_O2, S_UP):
                finished(s)
                for j in range(2):
                    c = 2 * (s - S_O2) + j
                    V.tensor_tensor(xT[:, c], bank(s, j), xT[:, c], ALU.add).then_inc(src_ready, 1)
                split_w(s + 2)
                dve.wait_ge(src_ready, src_count(C_UP2 + c))
                for c in (c - 1, c):
                    split_act(C_UP2 + c, act_hi[:, c], act_lo[:, c], xT[:, c], col("norm_ffn_g_2", c))
            inverse(N_FFN2)
            with dve.Fori(0, FFN_STEPS) as i:
                for side in range(2):
                    own, to = (0, 2) if side == 0 else (4, 0)
                    finished(S_UP + side, i)
                    for j in range(2):
                        V.tensor_tensor(tmp[:, own + j], bank(S_UP + side, j), R(N_FFN2), ALU.mult).then_inc(up_scaled, 1)
                    if side == 0:
                        split_w(S_UP + 2, i)
                    for j in range(2):
                        dve.wait_ge(up_scaled, 4 * i + (2 * side + j + 1))
                        dve.wait_ge(up_tap, 4 * i + (2 * side + j + 1))
                        V.scalar_tensor_tensor(tmp[:, to + j, 1:], tmp[:, own + j, 0:TOKENS - 1],
                                               tap_col(1, 2 * i + (side * FC + j)), tmp[:, to + j, 1:],
                                               ALU.mult, ALU.add).then_inc(up_mid, 1)
                    for j in range(2):
                        dve.wait_ge(up_mid, 4 * i + (2 * side + j + 1))
                        V.scalar_tensor_tensor(tmp[:, to + j, 2:], tmp[:, own + j, 0:TOKENS - 2],
                                               tap_col(0, 2 * i + (side * FC + j)), tmp[:, to + j, 2:],
                                               ALU.mult, ALU.add).then_inc(up_conv, 1)
                for j in range(2):
                    dve.wait_ge(up_conv, 4 * i + (j + 3))
                    dve.wait_ge(up_silu, 2 * i + (j + 1))
                    V.tensor_tensor(tmp[:, j], tmp[:, j], tmp[:, 2 + j], ALU.mult).then_inc(up_hidden, 1)
                split_w(S_UP + 3, i)
                for j in range(2):
                    dve.wait_ge(up_hidden, 2 * i + (j + 1))
                    dve.wait_ge(hid_hi_ready, 2 * i + (FC + j + 1))
                    at = bass.ds(2 * i + j, 1)
                    V.tensor_tensor(hid_lo[:, at].rearrange("p a n -> p (a n)"), tmp[:, j],
                                    hid_hi[:, at].rearrange("p a n -> p (a n)").bitcast(F32),
                                    ALU.subtract).then_inc(hid_lo_ready, 1)
                dve.wait_ge(hid_lo_ready, 2 * i + (FC + 2))
            def add_rows(s, n):
                b, half = n % TB, n // TB
                part = xnat[:, b, half * WIDTH:(half + 1) * WIDTH]
                V.tensor_tensor(part, bank(s, b), part, ALU.add).then_inc(xn_sum, 1)

            for s in range(S_DOWN2, N_SLABS - 2):
                finished(s)
                if s == S_DOWN2 + DOWN_SLABS - 1:
                    for b in range(TB):
                        add_rows(s, b)
                split_w(s + 2)
                if s in (S_DOWN2 + 1, S_DOWN2 + 3):
                    k = (s - S_DOWN2 - 1) // 2
                    dve.wait_ge(xn_turned, k + 1)
                    V.tensor_copy(xnat[:, 2 * k:2 * k + 2].rearrange("p b d -> p (b d)"),
                                  psum[:, 0:4].rearrange("p b n -> p (b n)")).then_inc(xn_ready, 1)
                    dve.wait_ge(xn_ready, k + 1)
                if s == S_DOWN2 + DOWN_SLABS:
                    dve.wait_ge(gain_in, 16)
                    for b in range(TB):
                        dve.wait_ge(xn_sum, b + 1)
                        dve.wait_ge(xn_sq, b + 1)
                        V.tensor_tensor(xnat[:, b, 0:WIDTH], xnat[:, b, 0:WIDTH], gain_out[:, 0:WIDTH], ALU.mult).then_inc(xn_gained, 1)
            for n in range(TB + 2):
                if n < TB:
                    dve.wait_ge(rows_done, n + 1)
                    add_rows(N_SLABS - 1, TB + n)
                if 0 <= n - 1 < TB:
                    b = n - 1
                    dve.wait_ge(xn_sq, TB + b + 1)
                    V.tensor_tensor(small[:, 48 + b:49 + b], small[:, 8 + b:9 + b], small[:, 8 + TB + b:9 + TB + b], ALU.add).then_inc(xn_mean, 1)
                if n >= 2:
                    b = n - 2
                    dve.wait_ge(xn_root, b + 1)
                    V.reciprocal(small[:, 52 + b:53 + b], small[:, 48 + b:49 + b]).then_inc(xn_inverse, 1)
                    dve.wait_ge(xn_inverse, b + 1)
                    dve.wait_ge(xn_sum, TB + b + 1)
                    part = xnat[:, b, WIDTH:D]
                    V.scalar_tensor_tensor(part, part, small[:, 52 + b:53 + b], gain_out[:, WIDTH:D],
                                           ALU.mult, ALU.mult).then_inc(xn_out, 1)

        @block.tensor
        def _(pe):
            mm = nc.tensor.matmul
            sems = {"evicted": evicted, "lg_ready": lg_ready, "ffn_gate": ffn_gate, "ffn_up": ffn_up, 
                    "gate_pre": gate_pre, "src_ready": src_ready, "up_scaled": up_scaled, "xn_sum": xn_sum}

            def wait_freed(g, more=0):
                name, count = freed(g)
                pe.wait_ge(sems[name], count + more)

            def wait_banks(g):
                for k in (g - 1, g - 2):
                    if k >= 0 and bank_of(k) == bank_of(g):
                        wait_freed(k)
                        break

            def wait_w(s, i=None):
                pe.wait_ge(w_lo_ready, s + 1 + (0 if i is None else 2 * i))

            def product(dst, stationary, moving, first, last):
                mm(dst, stationary[0], moving[0], start=first, stop=False)
                mm(dst, stationary[0], moving[1], start=False, stop=False)
                return mm(dst, stationary[1], moving[0], start=False, stop=last)

            def w_part(s, k, c0, n):
                at = k * SLABS[s][5] + c0
                return w_hi[:, s % 2, at:at + n], w_lo[:, s % 2, at:at + n]

            def act_part(chunk, t0=0, n=TOKENS):
                return act_hi[:, chunk, t0:t0 + n], act_lo[:, chunk, t0:t0 + n]

            def slab_a(s, q=None, i=None, part=act_part):
                wait_w(s, i)
                b = bank_of(GROUP[s])
                for k in range(DC):
                    if q is not None:
                        pe.wait_ge(act_lo_ready, q + k + 1)
                    for j in range(SLABS[s][5] // P):
                        ins = product(psum[:, b + j], w_part(s, k, j * P, P), part(k), k == 0, k == DC - 1)
                ins.then_inc(slab_done, 1)

            def slab_b(s, part, q=None, order=(0, 1, 2, 3), before_last=None):
                wait_w(s)
                wait_banks(GROUP[s])
                b = bank_of(GROUP[s])
                if q is not None:
                    pe.wait_ge(act_lo_ready, q + WC)
                for m in order:
                    if m == order[-1] and before_last is not None:
                        before_last()
                    for k in range(WC):
                        ins = product(psum[:, b + m], w_part(s, k, m * P, P), part(k), k == 0, k == WC - 1)
                ins.then_inc(slab_done, 1)

            def slab_v(s, part, before=lambda k: None):
                wait_w(s)
                if part == 0:
                    wait_banks(GROUP[s])
                b = bank_of(GROUP[s])
                for k in range(ROWS_B):
                    before(k)
                    for tb in range(TB):
                        ins = product(psum[:, b + tb], act_part(ROWS_B * part + k, tb * P, P), w_part(s, k, 0, WIDTH),
                                      part == 0 and k == 0, part == 1 and k == ROWS_B - 1)
                ins.then_inc(slab_done, 1)

            def sum_squares(r, bank):
                pe.wait_ge(sq_summed, SQ_DONE[r])
                mm(psum[:, bank], ones[:], acc[:, r % 2], start=True, stop=True).then_inc(ssq_done, 1)

            def turn_row(row, bank):
                for tb in range(TB):
                    ins = mm(psum[:, bank, tb:tb + 1], row[:, tb * P:(tb + 1) * P], ident[:, 0:1],
                             start=tb == 0, stop=True, skip_group_check=True)
                ins.then_inc(row_turned, 1)

            def turn_x_in(tb, c):
                return nc.tensor.transpose(psum[:, c, tb * P:(tb + 1) * P], xin[:, tb, c * P:(c + 1) * P], ident[:])

            pe.wait_ge(ident_set, 1)
            pe.wait_ge(first_in, 16)
            nc.tensor.transpose(psum[:, 7, 0:FIRST_ROWS], first_rows[:, :], ident[0:FIRST_ROWS, 0:FIRST_ROWS]).then_inc(par_done, 1)
            for tb in range(TB):
                pe.wait_ge(x_in[tb], 16)
                for c in range(DC):
                    if tb == 0 and c == DC - 1:
                        pe.wait_ge(par_ready, 1)
                    ins = turn_x_in(tb, c)
                    if tb == TB - 1:
                        ins.then_inc(x_turned, 1)
            for s in range(S_V):
                if s == 0:
                    pe.wait_ge(src_ready, 2)
                    pe.wait_ge(const_bf, 6)
                if s == S_Q:
                    pe.wait_ge(evicted, 2)
                wait_banks(GROUP[s])
                slab_a(s, q=C_MIX if s == 0 else None)
                if s == 0:
                    sum_squares(N_MIX, bank_of(0) + 3)
                    pe.wait_ge(row_in, 16 * (len(ROWS) + 2))
                    n = NROWS - FIRST_ROWS
                    nc.tensor.transpose(psum[:, 7, FIRST_ROWS:NROWS], rows[:, :], ident[0:n, 0:n])
                    for j in range(2):
                        ins = nc.tensor.transpose(psum[:, 7, NROWS + j * TAP_ROWS:NROWS + (j + 1) * TAP_ROWS], tap_rows[:, j],
                                                  ident[0:TAP_ROWS, 0:TAP_ROWS])
                    ins.then_inc(par_done, 1)
                if 2 <= s < 2 + WC:
                    c = s - 2
                    if c == 0:
                        pe.wait_ge(bd_in, 64)
                    if c >= 2:
                        pe.wait_ge(gate_read, c - 1)
                    pe.wait_ge(conv_done, c + 1)
                    b = bank_of(GROUP[s])
                    mm(psum[:, b + 2], gate_bd[:, 0, c], xc[:, c], start=True, stop=True)
                    mm(psum[:, b + 3], gate_bd[:, 1, c], xc[:, c], start=True, stop=True).then_inc(gates_done, 1)

            def columns(h, at, n):
                return psum[:, head_bank(h) + at // TOKENS, at % TOKENS:at % TOKENS + n]

            def head_rows(x, h, t0, n):
                p = HD * (h % 2)
                return x[p:p + HD, h // 2, t0:t0 + n]

            def values(h, weights, v_rows, bank):
                p = HD * (h % 2)
                for kb in range(TB):
                    n = TOKENS - kb * P
                    ins = mm(psum[p:p + HD, bank, kb * P:TOKENS], v_rows[:, kb, h * HD:(h + 1) * HD],
                             weights[:, h % 2, KEY_AT[kb]:KEY_AT[kb] + n], start=kb == 0, stop=kb == TB - 1,
                             skip_group_check=True)
                return ins

            def scores_kq(h):
                for kb in (1, 3, 0, 2):
                    if h >= 2 and kb in (1, 0):
                        pe.wait_ge(att_ready, 2 * (h - 2) + (1 if kb else 2))
                    n = TOKENS - kb * P
                    dst = columns(h, KEY_AT[kb], n)
                    mm(dst, head_rows(kT, h, kb * P, P), head_rows(qT, h, kb * P, n), start=kb != 3, stop=False,
                       skip_group_check=True)
                    ins = mm(dst[:, 0:P], ident_bf[:], mask_kq[:], start=False, stop=True, skip_group_check=True)
                ins.then_inc(z_done, 1)

            def suffix(h):
                pairs = [(kb, jb) for kb in (0, 1, 3, 2) for jb in range(kb, TB)]

                def part(kb, jb, source, kind):
                    n = TOKENS - jb * P
                    weights = neg_tri if jb == kb else neg_ones
                    return mm(columns(h, KEY_AT[kb] + (jb - kb) * P, n), weights[:].bitcast(F32) if kind == F32 else weights[:],
                              source[:, h % 2, KEY_AT[jb]:KEY_AT[jb] + n], start=False, stop=True, skip_group_check=True)

                pe.wait_ge(soft_ready, h + 1)
                for kb, jb in pairs:
                    if jb == TB - 1:
                        part(kb, jb, soft, F32)
                for source, ready in ((soft_hi, soft_hi_ready), (soft_lo, soft_lo_ready)):
                    pe.wait_ge(ready, h + 1)
                    for kb, jb in pairs:
                        if jb < TB - 1:
                            ins = part(kb, jb, source, F32R)
                ins.then_inc(suffix_done, 1)

            def values_kq(h):
                pe.wait_ge(att_ready, 2 * h + 2)
                if h >= 2 and h % 2 == 0:
                    pe.wait_ge(src_ready, C_ATT + h // 2)
                values(h, att, v, 0).then_inc(pv_done, 1)

            pe.wait_ge(gate_read, WC)
            turn_row(rstd[:, 0], 7)
            slab_v(S_V, 0, lambda k: sum_squares(N_LRU, 6) if k == ROWS_B - 1 else None)
            wait_freed(GROUP[S_V] - 1)
            pe.wait_ge(root_done, N_LRU + 1)
            pe.wait_ge(row_read, 1)
            scores_kq(0)
            wait_w(S_V + 1)
            for tb in (2, 3, 0, 1):
                if tb == 1:
                    pe.wait_ge(v_read, 2)
                    scores_kq(1)
                for k in range(ROWS_B):
                    ins = product(psum[:, bank_of(GROUP[S_V]) + tb], act_part(ROWS_B + k, tb * P, P), w_part(S_V + 1, k, 0, WIDTH),
                                  False, k == ROWS_B - 1)
                if tb == 3:
                    ins.then_inc(v_half, 1)
            ins.then_inc(slab_done, 1)
            suffix(0)
            wait_freed(GROUP[S_V])
            for h in range(1, HEADS):
                if h + 1 < HEADS:
                    scores_kq(h + 1)
                if h == 1:
                    values_kq(h - 1)
                suffix(h)
                if h > 1:
                    values_kq(h - 1)
                if early_part(h):
                    m, k0 = early_part(h)
                    if h == EARLY_HEAD:
                        wait_w(S_OUT_LRU)
                    if k0 == 0 and m:
                        pe.wait_ge(early_read, m)
                    pe.wait_ge(act_lo_ready, C_LRU + (WC if m else k0 + 2))
                    for k in (k0, k0 + 1):
                        ins = product(psum[:, 1], w_part(S_OUT_LRU, k, m * P, P), act_part(k), k == 0, k == WC - 1)
                    if k0:
                        ins.then_inc(early_done, 1)
            pe.wait_ge(att_ready, 2 * HEADS)
            values_kq(HEADS - 1)
            slab_b(S_OUT_LRU, act_part, q=C_LRU, order=range(EARLY, 4))
            pe.wait_ge(src_ready, C_ATT + WC)
            sum_squares(N_ATT, 0)
            pe.wait_ge(early_read, EARLY)
            slab_b(S_OUT_LRU + 1, act_part, order=(1, 2, 3, 0), before_last=lambda: pe.wait_ge(root_done, N_ATT + 1))
            slab_b(S_OUT_ATT, lambda k: act_part(WC + k), q=C_ATT)
            slab_b(S_OUT_ATT + 1, lambda k: act_part(WC + k))


            def up_and_down(s0, s_down, q, r, transposed, hid0, between):
                wait_banks(GROUP[s0])
                slab_a(s0, q=q)
                sum_squares(r, bank_of(GROUP[s0]) + 3)
                wait_banks(GROUP[s0 + 1])
                slab_a(s0 + 1)
                with pe.Fori(1, FFN_STEPS) as i:
                    for j in range(2):
                        name, _ = freed(GROUP[s0 + j])
                        per = freed(GROUP[s0 + 2 + j])[1] - freed(GROUP[s0 + j])[1]
                        pe.wait_ge(sems[name], i * per + (freed(GROUP[s0 + j])[1] - per))
                        slab_a(s0 + j, i=i)
                for s in range(s_down, s_down + 2 * DOWN_SLABS):
                    half, part = (s - s_down) // DOWN_SLABS, (s - s_down) % DOWN_SLABS
                    wait_w(s)
                    if part == 0:
                        wait_banks(GROUP[s])
                    b = bank_of(GROUP[s])
                    for k in range(SLABS[s][3]):
                        n = SLABS[s][2] + k
                        if half == 0:
                            pe.wait_ge(hid_lo_ready, hid0 + n + 1)
                        for m in range(4):
                            if transposed:
                                ins = product(psum[:, b + m], w_part(s, k, m * P, P), (hid_hi[:, n], hid_lo[:, n]),
                                              n == 0, n == FC - 1)
                            elif s < N_SLABS - 1:
                                ins = product(psum[:, b + m], (hid_hi[:, n, m * P:(m + 1) * P], hid_lo[:, n, m * P:(m + 1) * P]),
                                              w_part(s, k, 0, WIDTH), n == 0, n == FC - 1)
                    if s == N_SLABS - 1:
                        for m in range(TB):
                            for k in range(SLABS[s][3]):
                                n = SLABS[s][2] + k
                                ins = product(psum[:, b + m], (hid_hi[:, n, m * P:(m + 1) * P], hid_lo[:, n, m * P:(m + 1) * P]),
                                              w_part(s, k, 0, WIDTH), False, n == FC - 1)
                            ins.then_inc(rows_done, 1)
                    else:
                        ins.then_inc(slab_done, 1)
                        between(s)

            up_and_down(S_FFN, S_DOWN, C_FFN, N_FFN, True, 0, lambda s: None)
            for s in list(range(S_K2, S_V2)) + list(range(S_CC, S_OA2 - 1)):
                if s == S_OC2:
                    pe.wait_ge(negf_ready, HEADS)
                if S_OC2 <= s < S_GA:
                    slab_b(s, lambda k: (z_hi[:, k], z_lo[:, k]), q=C_Z2)
                    continue
                wait_banks(GROUP[s])
                slab_a(s, q=C_MIX2 if s == S_K2 else None)
                if s == S_K2:
                    sum_squares(N_FINAL, bank_of(GROUP[s]) + 2)
                    sum_squares(N_MIX2, bank_of(GROUP[s]) + 3)
                if s == S_Q2:
                    pe.wait_ge(rstd_ready, TURN[N_MIX2] + 1)
                    turn_row(rstd[:, RSTD_AT[N_MIX2]], bank_of(GROUP[s]) + 3)
                if s == S_V2 - 1:
                    pe.wait_ge(row_turned, 2)
                    slab_v(S_V2, 0)
                    slab_v(S_V2 + 1, 1)
                if S_CC <= s < S_CC + HEADS:
                    h = s - S_CC
                    pe.wait_ge(f_parts, 2)
                    if h == 0:
                        wait_freed(GROUP[S_V2])
                    if h >= 2:
                        pe.wait_ge(negf_ready, h - 1)
                    row = ident_r[:, h:h + 1].broadcast_to([HEADS, P])
                    mm(psum[:, bank_of(GROUP[s]) + 3], row, f_split[:, 0], start=True, stop=False)
                    mm(psum[:, bank_of(GROUP[s]) + 3], row, f_split[:, 1], start=False, stop=True).then_inc(negf_done, 1)

            def scores_qk(h):
                for i in QUERY_ORDER:
                    if h >= 2 and i >= 2:
                        pe.wait_ge(pt_ready, 2 * (h - 2) + (1 if i == 3 else 2))
                    n = P * (i + 1)
                    dst = columns(h, QUERY_AT[i], n)
                    mm(dst, head_rows(q2, h, i * P, P), head_rows(k2, h, 0, n), start=i != 0, stop=False,
                       skip_group_check=True)
                    ins = mm(dst[:, i * P:n], ident_bf[:], mask_qk[:], start=False, stop=True, skip_group_check=True)
                    if i != 2:
                        ins.then_inc(s_done, 1)

            def turn_probs(h):
                pe.wait_ge(s_max, TB * (h + 1))
                for n, i in enumerate(QUERY_ORDER):
                    pe.wait_ge(p_ready2, TB * h + n + 1)
                    for kb in range(i + 1):
                        ins = nc.tensor.transpose(columns(h, KEY_AT[kb] + (i - kb) * P, P),
                                                  probs[:, h % 2, QUERY_AT[i] + kb * P:QUERY_AT[i] + (kb + 1) * P], ident[:])
                ins.then_inc(pt_done, 1)

            def values_qk(h):
                pe.wait_ge(pt_ready, 2 * h + 2)
                if h >= 4 and h % 2 == 0:
                    pe.wait_ge(act_lo_ready, C_O2 + h // 2 - 1)
                values(h, probs_T, v2, pair_bank(h // 2)).then_inc(pv2_done, 1)

            s = S_OA2 - 1
            wait_w(s)
            wait_banks(GROUP[s])
            for j in range(2):
                for k in range(DC):
                    if j == 0 and k == WC:
                        wait_freed(GROUP[s - 1])
                        scores_qk(0)
                    ins = product(psum[:, bank_of(GROUP[s]) + j], w_part(s, k, j * P, P), act_part(k), k == 0, k == DC - 1)
            ins.then_inc(slab_done, 1)
            turn_probs(0)
            scores_qk(1)

            def branch_part(m):
                if m == 1:
                    wait_w(S_OA2)
                    pe.wait_ge(act_lo_ready, C_O2 + WC - 1)
                for k in range(WC - 1):
                    product(psum[:, bank_of(GROUP[S_OA2]) + m], w_part(S_OA2, k, m * P, P), act_part(WC + k), k == 0, False)

            for h in range(1, HEADS):
                if h + 1 < HEADS:
                    scores_qk(h + 1)
                if h == HEADS - 1:
                    values_qk(h - 1)
                    branch_part(1)
                turn_probs(h)
                if h == 1:
                    wait_freed(GROUP[S_OA2 - 1])
                if h < HEADS - 1:
                    values_qk(h - 1)
            branch_part(2)
            values_qk(HEADS - 1)
            branch_part(3)
            pe.wait_ge(act_lo_ready, C_O2 + WC)
            for m in (1, 2, 3, 0):
                for k in range(WC - 1 if m else 0, WC):
                    ins = product(psum[:, bank_of(GROUP[S_OA2]) + m], w_part(S_OA2, k, m * P, P), act_part(WC + k), k == 0, k == WC - 1)
            ins.then_inc(slab_done, 1)
            slab_b(S_OA2 + 1, lambda k: act_part(WC + k))
            for s in range(S_O2, S_UP):
                wait_banks(GROUP[s])
                slab_a(s, q=C_M2 if s == S_O2 else None, part=lambda k: (m_hi[:, k], m_lo[:, k]))

            def turn_x(s):
                if s not in (S_DOWN2 + 1, S_DOWN2 + 3):
                    return
                k = (s - S_DOWN2 - 1) // 2
                if k == 0:
                    wait_freed(GROUP[S_DOWN2 - 1])
                else:
                    pe.wait_ge(xn_ready, 1)
                for tb in range(2):
                    for c in range(DC):
                        ins = nc.tensor.transpose(psum[:, 2 * tb + c // 4, (c % 4) * P:(c % 4 + 1) * P],
                                                  xT[:, c, (2 * k + tb) * P:(2 * k + tb + 1) * P], ident[:])
                ins.then_inc(xn_turned, 1)

            assert bank_of(GROUP[S_DOWN2]) == 4
            up_and_down(S_UP, S_DOWN2, C_UP2, N_FFN2, False, FC, turn_x)


NAMES = ["x", "norm_mix", "w_in", "conv_w", "conv_b", "w_rg", "b_rg", "w_ig", "b_ig", "lru_lambda", "norm_lru_out",
         "norm_att_out", "w_out", "norm_ffn", "w_ffn_in", "w_ffn_out", "norm_final", "norm_mix_g_2", "w_in_2", "b_f_2",
         "b_gate_2", "conv_mix_w_2", "w_out_conv_2", "w_out_attn_2", "w_o_2", "norm_ffn_g_2", "w_up_2",
         "conv_ffn_w_2", "w_down_2", "norm_f_g_2"]


def kernel(**inputs):
    import numpy as np
    import concourse.bacc as bacc
    from concourse.bass_utils import run_bass_kernel_spmd

    nc = bacc.Bacc("TRN2", target_bir_lowering=False, num_devices=1)
    arrays, tensors = {}, {}
    for name in NAMES:
        a = np.ascontiguousarray(inputs[name])
        arrays[f"in_{name}"] = a
        tensors[name] = nc.dram_tensor(f"in_{name}", a.shape, mybir.dt.from_np(a.dtype), kind="ExternalInput").ap()
    out = nc.dram_tensor("out", (1, TOKENS, D), F32, kind="ExternalOutput").ap()
    two_blocks(nc, tensors, out)
    r = run_bass_kernel_spmd(nc, [arrays], core_ids=[0])
    return r.results[0]["out"]
```
